# Optimizing a Trainium2 kernel written in Bass

```python
import math
import jax, jax.numpy as jnp
from jax import lax
import numpy as np

D_MODEL = 1024
BATCH = 1
SEQ = 512
DEPTH = 2
DEC_BATCH = 8
DEC_SEQ = 4
PAST_LEN = 1024
PAGE_SIZE = 128

N_A = DEPTH // 2
N_B = DEPTH - N_A
D_INNER = 2 * D_MODEL
SSM_HEAD_DIM = 64
SSM_HEADS = D_INNER // SSM_HEAD_DIM
SSM_GROUPS = 8
HEADS_PER_GROUP = SSM_HEADS // SSM_GROUPS
D_STATE = 128
CONV_W = 4
GN = SSM_GROUPS * D_STATE
CONV_DIM = D_INNER + 2 * GN
IN_DIM = D_INNER + CONV_DIM + SSM_HEADS
CHUNK = 128
ATT_HEAD_DIM = 64
ATT_HEADS = D_MODEL // (2 * ATT_HEAD_DIM)
Q_DIM = ATT_HEADS * 2 * ATT_HEAD_DIM
K_DIM = Q_DIM
V_HEAD_DIM = 2 * ATT_HEAD_DIM
V_DIM = ATT_HEADS * V_HEAD_DIM
Q_BLOCK = 128
D_FF = 4 * D_MODEL
EPS = 1e-6
F32 = jnp.float32

kernel_name = "yoco_mamba2_diffattn_decoder_step"

def rms_norm(x, g):
    xf = x.astype(F32)
    y = xf * lax.rsqrt(jnp.mean(xf * xf, axis=-1, keepdims=True) + EPS)
    return (y * g.astype(F32)).astype(x.dtype)

def sq_relu_mlp(h, w_up, w_down):
    return jnp.square(jax.nn.relu(h @ w_up)) @ w_down

def causal_depthwise_conv(xbc, buf, w, b):
    L = xbc.shape[1]
    xpad = jnp.concatenate([buf.astype(xbc.dtype), xbc], axis=1)
    out = b
    for k in range(CONV_W):
        out = out + w[k] * xpad[:, k:k + L]
    return out, xpad[:, L:]

def gated_group_rmsnorm(y, z, g):
    shp = y.shape
    yz = (y.astype(F32) * jax.nn.silu(z.astype(F32))).reshape(shp[:-1] + (SSM_GROUPS, D_INNER // SSM_GROUPS))
    yz = yz * lax.rsqrt(jnp.mean(yz * yz, axis=-1, keepdims=True) + EPS)
    return yz.reshape(shp) * g.astype(F32)

def ssd_chunked(x, a, bm, cm, h0):
    b, L = x.shape[:2]
    q = min(CHUNK, L)
    c = L // q
    x = x.reshape(b, c, q, SSM_GROUPS, HEADS_PER_GROUP, SSM_HEAD_DIM)
    a = a.reshape(b, c, q, SSM_GROUPS, HEADS_PER_GROUP)
    bm = bm.reshape(b, c, q, SSM_GROUPS, D_STATE)
    cm = cm.reshape(b, c, q, SSM_GROUPS, D_STATE)
    a_cs = jnp.cumsum(a, axis=2)
    causal = jnp.tril(jnp.ones((q, q), dtype=bool))[None, None, :, :, None, None]
    seg = a_cs[:, :, :, None] - a_cs[:, :, None, :]
    decay = jnp.exp(jnp.where(causal, seg, -jnp.inf))
    cb = jnp.einsum('bclgn,bcsgn->bclsg', cm, bm)
    y_diag = jnp.einsum('bclsg,bclsgr,bcsgrp->bclgrp', cb, decay, x)
    decay_to_end = jnp.exp(a_cs[:, :, -1:] - a_cs)
    states = jnp.einsum('bclgn,bclgr,bclgrp->bcgrpn', bm, decay_to_end, x)
    chunk_decay = jnp.exp(a_cs[:, :, -1])
    h_init = h0.reshape(b, SSM_GROUPS, HEADS_PER_GROUP, SSM_HEAD_DIM, D_STATE)

    def step(h, inp):
        st, dec = inp
        return h * dec[..., None, None] + st, h

    h_last, h_in = lax.scan(step, h_init, (jnp.swapaxes(states, 0, 1), jnp.swapaxes(chunk_decay, 0, 1)))
    h_in = jnp.swapaxes(h_in, 0, 1)
    y_off = jnp.einsum('bclgn,bcgrpn,bclgr->bclgrp', cm, h_in, jnp.exp(a_cs))
    y = (y_diag + y_off).reshape(b, L, SSM_HEADS, SSM_HEAD_DIM)
    return y, h_last.reshape(b, SSM_HEADS, SSM_HEAD_DIM, D_STATE)

def mamba2_mixer(u, conv_buf, h0, w_in, conv_w, conv_b, dt_bias, a_log, d_skip, gnorm_w, w_out):
    b, L, _ = u.shape
    zxbcdt = u @ w_in
    z = zxbcdt[..., :D_INNER]
    xbc = zxbcdt[..., D_INNER:D_INNER + CONV_DIM]
    dt = zxbcdt[..., D_INNER + CONV_DIM:]
    xbc, new_buf = causal_depthwise_conv(xbc, conv_buf, conv_w, conv_b)
    xbc = jax.nn.silu(xbc)
    xs = xbc[..., :D_INNER].reshape(b, L, SSM_HEADS, SSM_HEAD_DIM).astype(F32)
    bm = xbc[..., D_INNER:D_INNER + GN].reshape(b, L, SSM_GROUPS, D_STATE).astype(F32)
    cm = xbc[..., D_INNER + GN:].reshape(b, L, SSM_GROUPS, D_STATE).astype(F32)
    dt = jax.nn.softplus(dt.astype(F32) + dt_bias.astype(F32))
    a = -jnp.exp(a_log.astype(F32))
    y, h_last = ssd_chunked(xs * dt[..., None], dt * a, bm, cm, h0.astype(F32))
    y = y + d_skip.astype(F32)[:, None] * xs
    y = gated_group_rmsnorm(y.reshape(b, L, D_INNER), z, gnorm_w)
    return y.astype(u.dtype) @ w_out, new_buf, h_last.astype(h0.dtype)

def shared_kv(x, kv_norm, w_kv, k_norm):
    b, t, _ = x.shape
    kv = rms_norm(x, kv_norm) @ w_kv
    k = rms_norm(kv[..., :K_DIM].reshape(b, t, ATT_HEADS, 2, ATT_HEAD_DIM), k_norm)
    v = kv[..., K_DIM:].reshape(b, t, ATT_HEADS, V_HEAD_DIM)
    return k, v

def diff_attention(q, k, v, q_pos, k_pos, lam):
    s = jnp.einsum('bqhcd,bkhcd->bhcqk', q, k).astype(F32) * (ATT_HEAD_DIM ** -0.5)
    mask = k_pos[None, :] <= q_pos[:, None]
    p = jax.nn.softmax(jnp.where(mask, s, -jnp.inf), axis=-1)
    a = p[:, :, 0] - lam * p[:, :, 1]
    return jnp.einsum('bhqk,bkhe->bqhe', a.astype(v.dtype), v)

def causal_block_attention(q, k, v, lam):
    b, s = q.shape[:2]
    nb = s // Q_BLOCK
    qb = jnp.swapaxes(q.reshape(b, nb, Q_BLOCK, ATT_HEADS, 2, ATT_HEAD_DIM), 0, 1)
    k_pos = jnp.arange(s)

    def one(args):
        q_blk, i = args
        q_pos = i * Q_BLOCK + jnp.arange(Q_BLOCK)
        return diff_attention(q_blk, k, v, q_pos, k_pos, lam)

    o = lax.map(one, (qb, jnp.arange(nb)))
    return jnp.swapaxes(o, 0, 1).reshape(b, s, ATT_HEADS, V_HEAD_DIM)

def diff_attn_layer(x, attend, layer_idx, norm_g, w_q, q_norm, lq1, lk1, lq2, lk2, subln, w_o):
    b, t, _ = x.shape
    q = (rms_norm(x, norm_g) @ w_q).reshape(b, t, ATT_HEADS, 2, ATT_HEAD_DIM)
    q = rms_norm(q, q_norm)
    lam_init = 0.8 - 0.6 * math.exp(-0.3 * layer_idx)
    lam = (jnp.exp(jnp.sum(lq1.astype(F32) * lk1.astype(F32)))
           - jnp.exp(jnp.sum(lq2.astype(F32) * lk2.astype(F32))) + lam_init)
    o = attend(q, lam)
    o = rms_norm(o, subln) * (1.0 - lam_init)
    return o.reshape(b, t, V_DIM) @ w_o

def setup_inputs(seed: int = 0) -> dict:
    key = jax.random.key(seed)
    ks = jax.random.split(key, 40)

    def nrm(i, shape, scale):
        return jax.random.normal(ks[i], shape, F32) * scale

    n_pages = PAST_LEN // PAGE_SIZE
    n_pool = (5 * DEC_BATCH * n_pages + 3) // 4
    page_table = jax.random.permutation(ks[7], n_pool)[:DEC_BATCH * n_pages].reshape(DEC_BATCH, n_pages).astype(jnp.int32)
    dt0 = jnp.exp(jax.random.uniform(ks[12], (N_A, SSM_HEADS), F32, math.log(1e-3), math.log(1e-1)))
    dt0 = jnp.maximum(dt0, 1e-4)
    dt_bias = dt0 + jnp.log(-jnp.expm1(-dt0))
    a_log = jnp.log(jax.random.uniform(ks[13], (N_A, SSM_HEADS), F32, 1.0, 16.0))
    return {
        "x_prompt": nrm(0, (BATCH, SEQ, D_MODEL), 1.0),
        "x_sample": nrm(1, (DEC_BATCH, DEC_SEQ, D_MODEL), 1.0),
        "state_ssm": nrm(2, (N_A, DEC_BATCH, SSM_HEADS, SSM_HEAD_DIM, D_STATE), 0.1),
        "state_conv": nrm(3, (N_A, DEC_BATCH, CONV_W - 1, CONV_DIM), 1.0),
        "cache_k": nrm(4, (n_pool, PAGE_SIZE, ATT_HEADS, 2, ATT_HEAD_DIM), 1.0),
        "cache_v": nrm(5, (n_pool, PAGE_SIZE, ATT_HEADS, V_HEAD_DIM), 1.0),
        "page_table": page_table,
        "norm_a": 1.0 + nrm(8, (N_A, D_MODEL), 0.02),
        "w_in_a": nrm(9, (N_A, D_MODEL, IN_DIM), D_MODEL ** -0.5),
        "conv_w": nrm(10, (N_A, CONV_W, CONV_DIM), CONV_W ** -0.5),
        "conv_b": nrm(11, (N_A, CONV_DIM), 0.02),
        "dt_bias": dt_bias,
        "a_log": a_log,
        "d_skip": 1.0 + nrm(14, (N_A, SSM_HEADS), 0.02),
        "gnorm_w": 1.0 + nrm(15, (N_A, D_INNER), 0.02),
        "w_out_a": nrm(16, (N_A, D_INNER, D_MODEL), D_INNER ** -0.5),
        "kv_norm": 1.0 + nrm(17, (D_MODEL,), 0.02),
        "w_kv": nrm(18, (D_MODEL, K_DIM + V_DIM), D_MODEL ** -0.5),
        "k_norm": 1.0 + nrm(19, (ATT_HEAD_DIM,), 0.02),
        "norm_b": 1.0 + nrm(20, (N_B, D_MODEL), 0.02),
        "w_q": nrm(21, (N_B, D_MODEL, Q_DIM), D_MODEL ** -0.5),
        "q_norm": 1.0 + nrm(22, (N_B, ATT_HEAD_DIM), 0.02),
        "lam_q1": nrm(23, (N_B, ATT_HEAD_DIM), 0.1),
        "lam_k1": nrm(24, (N_B, ATT_HEAD_DIM), 0.1),
        "lam_q2": nrm(25, (N_B, ATT_HEAD_DIM), 0.1),
        "lam_k2": nrm(26, (N_B, ATT_HEAD_DIM), 0.1),
        "subln": 1.0 + nrm(27, (N_B, V_HEAD_DIM), 0.02),
        "w_o": nrm(28, (N_B, V_DIM, D_MODEL), V_DIM ** -0.5),
        "norm_m": 1.0 + nrm(29, (DEPTH, D_MODEL), 0.02),
        "w_up": nrm(30, (DEPTH, D_MODEL, D_FF), D_MODEL ** -0.5),
        "w_down": nrm(31, (DEPTH, D_FF, D_MODEL), D_FF ** -0.5),
    }

def reference(x_prompt, x_sample, state_ssm, state_conv, cache_k, cache_v, page_table,
              norm_a, w_in_a, conv_w, conv_b, dt_bias, a_log, d_skip, gnorm_w, w_out_a,
              kv_norm, w_kv, k_norm, norm_b, w_q, q_norm, lam_q1, lam_k1, lam_q2, lam_k2,
              subln, w_o, norm_m, w_up, w_down):

    def trunk(x, conv0, ssm0, make_attend):
        convs, ssms = [], []
        attend, k_new, v_new = None, None, None
        for l in range(DEPTH):
            if l < N_A:
                y, cbuf, hs = mamba2_mixer(rms_norm(x, norm_a[l]), conv0[l], ssm0[l], w_in_a[l], conv_w[l],
                                           conv_b[l], dt_bias[l], a_log[l], d_skip[l], gnorm_w[l], w_out_a[l])
                convs.append(cbuf)
                ssms.append(hs)
                x = x + y
            else:
                if l == N_A:
                    k_new, v_new = shared_kv(x, kv_norm, w_kv, k_norm)
                    attend = make_attend(k_new, v_new)
                j = l - N_A
                x = x + diff_attn_layer(x, attend, l, norm_b[j], w_q[j], q_norm[j], lam_q1[j], lam_k1[j],
                                        lam_q2[j], lam_k2[j], subln[j], w_o[j])
            x = x + sq_relu_mlp(rms_norm(x, norm_m[l]), w_up[l], w_down[l])
        return x, jnp.stack(ssms), jnp.stack(convs), k_new, v_new

    bp = x_prompt.shape[0]
    conv0_p = jnp.zeros((N_A, bp, CONV_W - 1, CONV_DIM), x_prompt.dtype)
    ssm0_p = jnp.zeros((N_A, bp, SSM_HEADS, SSM_HEAD_DIM, D_STATE), state_ssm.dtype)

    def prompt_attend_factory(k, v):
        return lambda q, lam: causal_block_attention(q, k, v, lam)

    y_p, ssm_p, conv_p, k_p, v_p = trunk(x_prompt, conv0_p, ssm0_p, prompt_attend_factory)

    bd = x_sample.shape[0]
    n_past = page_table.shape[1] * PAGE_SIZE
    k_past = cache_k[page_table].reshape(bd, n_past, ATT_HEADS, 2, ATT_HEAD_DIM)
    v_past = cache_v[page_table].reshape(bd, n_past, ATT_HEADS, V_HEAD_DIM)

    def sample_attend_factory(k, v):
        t = k.shape[1]
        k_all = jnp.concatenate([k_past.astype(k.dtype), k], axis=1)
        v_all = jnp.concatenate([v_past.astype(v.dtype), v], axis=1)
        q_pos = n_past + jnp.arange(t)
        k_pos = jnp.arange(n_past + t)
        return lambda q, lam: diff_attention(q, k_all, v_all, q_pos, k_pos, lam)

    y_s, ssm_s, conv_s, k_s, v_s = trunk(x_sample, state_conv, state_ssm, sample_attend_factory)

    return (y_p, y_s, ssm_p, conv_p, k_p, v_p, ssm_s, conv_s, k_s, v_s)


_drawn_inputs = setup_inputs


def setup_inputs(seed=0):
    import zlib

    import numpy as np

    out = dict(_drawn_inputs(seed))
    spreads = {}
    factors = {'d_skip': 6.552,
     'gnorm_w': 3.447,
     'kv_norm': 2.846,
     'k_norm': 2.816,
     'norm_b': 7.339,
     'q_norm': 8.0,
     'lam_k2': 6.911,
     'subln': 8.0,
     'norm_m': 2.88}
    for name, (base, spread) in spreads.items():
        noise = np.random.default_rng([zlib.crc32(name.encode()), seed]).standard_normal(out[name].shape)
        drawn = base * np.exp(spread * noise) if base else spread * noise
        out[name] = __import__('jax').numpy.asarray(drawn.astype(out[name].dtype))
    for name, factor in factors.items():
        out[name] = (out[name] * factor).astype(out[name].dtype)
    return out
```

```python
from contextlib import ExitStack

import numpy as np

import concourse.bass as bass
from concourse import mybir

F32 = mybir.dt.float32
I32 = mybir.dt.int32
ACT = mybir.ActivationFunctionType
ALU = mybir.AluOpType
AX = mybir.AxisListType

P = 128
D = 1024
KT = D // P
SEQ = 512
DB, DS = 8, 4
NS = DB * DS
T = SEQ + NS
HT = T // 2
GROUPS = 8
R = 4
HP = 64
CH = SEQ // P
GT = 6
CT = 4
NH = 8
DF = 4096
FT = DF // P // 2
PAGES = 8
PAST = P * PAGES
SLOTS = 4
NEG = -1.0e30
SCALE = 64 ** -0.5
LAM_INIT = 0.8 - 0.6 * float(np.exp(-0.3))
EPS = 1e-6
CB = 3 + SEQ + DB * 7
FIRST = 1
CO = CB - 3

C_ID, C_ONE, C_B64, C_CAU, C_NEG, C_ELAST = (P * n for n in range(6))
C_SAMP = 6 * P
C_SELE = C_SAMP + NS
C_LAST = C_SELE + NS
C_BLK = C_LAST + DB
C_RST = C_BLK + DB
C_NEWM = C_RST + T
C_EPS = C_NEWM + DB * 64
C_W = C_EPS + 1

G_A, G_MA, G_KV, G_B, G_MB = (KT * n for n in range(5))
G_GN = 5 * KT
G_DSK = G_GN + 16
G_CW = G_DSK + 16
G_CBI = G_CW + 32 * 4
G_KN = G_CBI + 32
G_QN = G_KN + 1
G_SUB = G_QN + 1
G_DTB = G_SUB + 1
G_ALOG = G_DTB + 1
G_LAM = G_ALOG + 1
G_W = G_LAM + 4


def constants():
    c = np.zeros((P, C_W), np.float32)
    i = np.arange(P)
    c[:, C_ID:C_ID + P] = np.eye(P)
    c[:, C_ONE:C_ONE + P] = 1
    c[:, C_B64:C_B64 + P] = (i[:, None] // 64 == i[None] // 64)
    c[:, C_CAU:C_CAU + P] = (i[None] >= i[:, None])
    c[:, C_NEG:C_NEG + P] = np.where(i[None] > i[:, None], NEG, 0)
    c[P - 1, C_ELAST:C_ELAST + P] = 1
    s = np.arange(NS)
    same = s[:, None] // DS == s[None] // DS
    c[:NS, C_SAMP:C_SAMP + NS] = same & (s[None] >= s[:, None])
    c[:NS, C_SELE:C_SELE + NS] = s[:, None] == DS * (s[None] // DS) + DS - 1
    b = np.arange(DB)
    c[:NS, C_LAST:C_LAST + DB] = s[:, None] == DS * b[None] + DS - 1
    c[:NS, C_BLK:C_BLK + DB] = s[:, None] // DS == b[None]
    t = np.arange(T)
    c[:NS, C_RST:C_RST + T] = np.where(t < SEQ, t % P != 0, (t - SEQ) % DS != 0)
    q = np.arange(64) % DS
    ok = (s[:, None, None] // DS == b[None, :, None]) & (s[:, None, None] % DS <= q[None, None])
    c[:NS, C_NEWM:C_NEWM + DB * 64] = np.where(ok, 0, NEG).reshape(NS, -1)
    c[:, C_EPS] = EPS
    return c


class Sems:

    def __init__(self, nc, ctx):
        self.nc, self.ctx, self.made = nc, ctx, {}

    def __getattr__(self, name):
        return self[name]

    def __getitem__(self, name):
        if name not in self.made:
            self.made[name] = self.ctx.enter_context(self.nc.semaphore(name))
        return self.made[name]


class Chip:
    pass


def col(t, k):
    return t[:, bass.ds(k, 1), :].rearrange("p a x -> p (a x)")


def one(t, c):
    return t[:, bass.ds(c, 1)]


def halves(ap):
    return ap.rearrange("p (h t) -> p h t", h=2)


def plan():
    stage, tiles, blocks = {}, 0, 0
    for name, n, nb in [("in", GT * GROUPS, 1), ("out", KT, 2), ("up00", FT, 1), ("dn00", KT, 2), ("up01", FT, 1),
                        ("dn01", KT, 2), ("qkv", 3 * KT, 1), ("o", KT, 1), ("up10", FT, 1), ("dn10", KT, 2),
                        ("up11", FT, 1), ("dn11", KT, 2)]:
        stage[name] = (tiles, blocks, n, nb)
        tiles += n
        blocks += n * nb
    return stage, blocks


def sp_stream(c, sp, b0, n):
    with sp.Fori(b0 // SLOTS, (b0 + n) // SLOTS) as i:
        for u in range(SLOTS):
            sp.wait_ge(c.S.block_done, i * SLOTS + (u + 1 - SLOTS))
            sp.dma_start(c.ring[:, u, :], c.wblocks[bass.ds(i * SLOTS + u, 1)].rearrange("a p n -> (a p) n")
                         ).then_inc(c.S[f"slot_loaded{u}"], 16)


def pe_tile(c, pe, pair, turn, slots, src, free, src_k=0):
    pe.wait_ge(c.S[f"pair_free{pair}"], free)
    for n, u in enumerate(slots):
        pe.wait_ge(c.S[f"slot_loaded{u}"], turn * 16 + 16)
        for k in range(KT):
            for h in range(2):
                mm = pe.matmul(c.LN[pair][:, h, 0:HT], c.ring[:, u, k * P:(k + 1) * P],
                               src[:, src_k + n * KT + k, h * HT:(h + 1) * HT],
                               start=(n == 0 and k == 0), stop=(n == len(slots) - 1 and k == KT - 1))
        mm.then_inc(c.S.block_done, 1)


def pe_layer(c, pe, name, src):
    t0, b0, n, nb = c.stage[name]
    per = SLOTS // nb
    with pe.Fori(0, n // per) as i:
        for u in range(per):
            pe_tile(c, pe, u % 2, i + b0 // SLOTS, range(u * nb, u * nb + nb), src, i * (per // 2) + (t0 + u) // 2)


def add_layer(c, dve, name):
    t0, b0, n, nb = c.stage[name]
    with dve.Fori(0, n // 2) as i:
        for u in range(2):
            dve.wait_ge(c.S.block_done, i * (2 * nb) + b0 + (u + 1) * nb)
            x = halves(col(c.xT, i * 2 + u))
            dve.tensor_tensor(x, x, c.LN[u][:, :, 0:HT], ALU.add).then_inc(c.S[f"pair_free{u}"], 1)


def act_wait_added(c, act, name):
    t0, _, n, _ = c.stage[name]
    for u in range(2):
        act.wait_ge(c.S[f"pair_free{u}"], (t0 + n) // 2)


def act_norm(c, act, n):
    for k in range(KT):
        if k >= 2 or n:
            act.wait_ge(c.S.square_summed, n * KT + k - 1)
        act.activation(c.tmp[:, k % 2, :], c.xT[:, k, :], ACT.Square).then_inc(c.S.squared, 1)
    act.wait_ge(c.S.square_summed, (n + 1) * KT)
    act.activation(halves(c.rn[:]), c.A[:, :, 0:HT], ACT.Sqrt, bias=c.eps, scale=1.0 / D).then_inc(c.S.rooted, 1)


def pe_norm(c, pe, n):
    for k in range(KT):
        pe.wait_ge(c.S.squared, n * KT + k + 1)
        for h in range(2):
            mm = pe.matmul(c.A[:, h, 0:HT], c.ones, c.tmp[:, k % 2, h * HT:(h + 1) * HT],
                           start=(k == 0), stop=(k == KT - 1))
        mm.then_inc(c.S.square_summed, 1)


def dve_norm(c, dve, n, gains):
    dve.wait_ge(c.S.rooted, n + 1)
    dve.reciprocal(c.rn[:], c.rn[:]).then_inc(c.S.inverted, 1)
    dve.wait_ge(c.S.inverted, n + 1)
    dve_scale(c, dve, gains)


def dve_scale(c, dve, gains):
    for k in range(KT):
        ins = dve.scalar_tensor_tensor(out=c.hT[:, k, :], in0=c.xT[:, k, :], scalar=c.par[:, gains + k:gains + k + 1],
                                       in1=c.rn[:], op0=ALU.mult, op1=ALU.mult)
    ins.then_inc(c.S.h_ready, 1)


def mixer_phase(c):
    nc, S = c.nc, c.S
    with ExitStack() as ctx:
        arena = ctx.enter_context(nc.sbuf_tensor("mixer_arena", [P, 22560], F32))
        top = [0]

        def carve(*shape, at=None):
            n = int(np.prod(shape))
            lo = top[0] if at is None else at
            if at is None:
                top[0] += n
                assert top[0] <= 22560, top[0]
            v = arena[:, lo:lo + n]
            if len(shape) > 1:
                names = "abcd"[:len(shape)]
                v = v.rearrange(f"p ({' '.join(names)}) -> p {' '.join(names)}", **dict(zip(names, shape)))
            return v

        cb = carve(2, CB)
        acc = carve(CO)
        xc = carve(2, CT, T)
        sz = carve(2, T)
        abc = carve(R, T)
        dt_at = top[0]
        M = carve(R, SEQ)
        Ms = carve(R, NS)
        ea = carve(R, T)
        xdt = carve(CH + 1, R * HP)
        xw = carve(CH + 1, R * HP)
        Btok = carve(CH, P)
        Bm = carve(DB, P)
        CBm = carve(CH, P)
        CBs = carve(NS)
        hst = carve(CH, R * HP)
        h0 = carve(DB, R * HP)
        yt = carve(2, T)
        yoff = carve(2, NS)
        dtf = carve(4, T, at=dt_at)[0:32]
        dtw = ctx.enter_context(nc.sbuf_tensor("dtw", [P, KT * 32], F32))
        dtt = ctx.enter_context(nc.sbuf_tensor("dtt", [P, CH + 1, 32], F32))
        acst = ctx.enter_context(nc.sbuf_tensor("acst", [P, CH + 1, 32], F32))
        xws = ctx.enter_context(nc.sbuf_tensor("xws", [P, CH + 1, 32], F32))
        cdec = ctx.enter_context(nc.sbuf_tensor("cdec", [P, CH, 32], F32))
        sdec = ctx.enter_context(nc.sbuf_tensor("sdec", [P, DB, 32], F32))
        zl = ctx.enter_context(nc.sbuf_tensor("zl", [NS, DB, 32], F32))
        hist = ctx.enter_context(nc.sbuf_tensor("hist", [P, 32, 24], F32))
        ncv = ctx.enter_context(nc.sbuf_tensor("ncv", [P, 32, 27], F32))
        nega = ctx.enter_context(nc.sbuf_tensor("nega", [32, 1], F32))
        A, Bp, LN, cst, par = c.A, c.Bp, c.LN, c.cst, c.par
        ident, ones = c.ident, c.ones

        def heads(t, n0, n1, i, s, rows=P):
            return t[0:rows, n0:n1, bass.ds(i * (2 * R) + s * R, R)]

        def head(t, n, i, s, r):
            return t[:, n, bass.ds(i * (2 * R) + (s * R + r), 1)]

        def over(ap, n):
            return ap.unsqueeze(len(ap.shape)).to_broadcast(list(ap.shape) + [n])

        block = ctx.enter_context(nc.Block())

        def steps(eng, step):
            with eng.Fori(0, GROUPS // 2 - 1) as i:
                step(i, 0)
                step(i, 1)
            step(0, GROUPS - 2)
            step(0, GROUPS - 1)

        @block.sync
        def _(sp):
            sp.dma_start(c.cst[:], c.cst_d).then_inc(S.const_loaded, 16)
            sp.dma_start(c.xT[:], c.xin).then_inc(S.x_loaded, 16)
            sp.dma_start(c.par[:], c.par_d).then_inc(S.par_loaded, 16)
            sp.dma_start(dtw[:], c.wdt).then_inc(S.dtw_loaded, 16)
            sp.dma_start(c.pt[:], c.pt_d).then_inc(S.table_loaded, 16)
            for u in range(SLOTS):
                sp.dma_start(c.ring[:, u, :], c.wblocks[u]).then_inc(S[f"slot_loaded{u}"], 16)
            sp.dma_start(hist[:], c.hist_d).then_inc(S.hist_loaded, 16)
            sp_stream(c, sp, SLOTS, GT * GROUPS)
            sp.wait_ge(S.history_out, 4 * GROUPS)
            sp.dma_start(c.nconv_o, ncv[:]).then_inc(S.stored, 16)

        @block.tensor
        def _(pe):
            def tile(i, s, u):
                pe_tile(c, pe, u % 2, i * 3 + (GT * s + u) // SLOTS, [(GT * s + u) % SLOTS], c.hT,
                        i * GT + (GT * s + u) // 2)

            pe.wait_ge(S.const_loaded, 16)
            pe_norm(c, pe, 0)
            pe.wait_ge(S.h_ready, 1)
            pe.wait_ge(S.dtw_loaded, 16)
            for k in range(KT):
                for h in range(2):
                    mm = pe.matmul(Bp[0:32, h, 0:HT], dtw[:, k * 32:(k + 1) * 32], c.hT[:, k, h * HT:(h + 1) * HT],
                                   start=(k == 0), stop=(k == KT - 1))
            mm.then_inc(S.dt_projected, 1)
            for u in range(3):
                tile(0, 0, u)
            pe.wait_ge(S.decay_summed, 1)
            for n in range(CH + 1):
                m = P if n < CH else NS
                pe.transpose(A[0:m, 0, n * 32:(n + 1) * 32], dtf[:, 1, n * P:n * P + m], ident[0:32, 0:32])
                mm = pe.transpose(A[0:m, 1, n * 32:(n + 1) * 32], dtf[:, 2, n * P:n * P + m], ident[0:32, 0:32])
            mm.then_inc(S.dt_turned, 1)
            pe.wait_ge(S.dt_kept, 2)
            pe.matmul(Bp[:, 0, 0:CH * 32], cst[:, C_ELAST:C_ELAST + P], acst[:, 0:CH, :].rearrange("p c h -> p (c h)"),
                      start=True, stop=True)
            pe.matmul(Bp[0:NS, 0, 128:160], cst[0:NS, C_SELE:C_SELE + NS], acst[0:NS, CH, :], start=True, stop=True)
            pe.wait_ge(S.last_kept, 1)
            pe.matmul(Bp[:, 1, 0:DB * 32], ones[0:NS, :], zl[:].rearrange("p b h -> p (b h)"),
                      start=True, stop=True).then_inc(S.ends_ready, 1)
            for u in range(3, GT):
                tile(0, 0, u)

            def step(i, s):
                par_ = s % 2
                g1 = i * 2 + (s + 1)
                X = xc[:, par_]
                pe.wait_ge(S.conv_done, i * 8 + 4 * s + 4)
                pe.wait_ge(S.group_done, i * 2 + s + FIRST)
                if s == 0:
                    pe.wait_ge(S.dt_scaled, 1)
                for n in range(CH):
                    for j in range(2):
                        mm = pe.transpose(A[:, n // 2, (n % 2) * 256 + j * P:(n % 2) * 256 + (j + 1) * P],
                                          X[:, j, n * P:(n + 1) * P], ident)
                mm.then_inc(S.x_turned, 1)
                for n in range(CH):
                    mm = pe.transpose(Bp[:, 0, n * P:(n + 1) * P], X[:, 2, n * P:(n + 1) * P], ident)
                mm.then_inc(S.b_turned, 1)
                for n in range(CH):
                    mm = pe.matmul(Bp[:, 1, n * P:(n + 1) * P], X[:, 2, n * P:(n + 1) * P], X[:, 3, n * P:(n + 1) * P],
                                   start=True, stop=True)
                mm.then_inc(S.cb_ready, 1)
                pe.wait_ge(S.x_scaled, g1)
                for j in range(2):
                    pe.transpose(A[0:NS, 0, j * P:(j + 1) * P], X[:, j, SEQ:T], ident)
                pe.transpose(A[0:NS, 1, 0:P], X[:, 2, SEQ:T], ident)
                pe.matmul(A[0:NS, 1, P:P + NS], X[:, 2, SEQ:T], X[:, 3, SEQ:T], start=True, stop=True)
                pe.wait_ge(S.h0_loaded, i * 32 + 16 * (s + 1))
                for b in range(DB):
                    for j in range(2):
                        lo = 192 + j * NS + DS * b
                        mm = pe.matmul(A[:, 1, lo:lo + DS], h0[:, b, j * P:(j + 1) * P],
                                       X[:, 3, SEQ + DS * b:SEQ + DS * (b + 1)], start=True, stop=True)
                mm.then_inc(S.sample_ready, 1)
                last = s == GROUPS - 1
                if not last:
                    for u in range(3):
                        tile(i, s + 1, u)
                pe.wait_ge(S.b_kept, g1)
                pe.wait_ge(S.sample_kept, g1)
                for n in range(CH):
                    mm = pe.matmul(A[:, n // 2, (n % 2) * 256:(n % 2) * 256 + 256], Btok[:, n, :], xw[:, n, :],
                                   start=True, stop=True)
                mm.then_inc(S.states_ready, 1)
                for q in range(2):
                    if q:
                        pe.wait_ge(S.state_added, i * 4 + 2 * s + 1)
                    for b in range(4 * q, 4 * q + 4):
                        mm = pe.matmul(Bp[:, (b // 2) % 2, (b % 2) * 256:(b % 2) * 256 + 256], Bm[0:NS, b, :],
                                       xw[0:NS, CH, :], start=True, stop=True)
                    mm.then_inc(S.update_ready, 1)
                    if q == 0:
                        pe.wait_ge(S.states_kept, g1)
                        for j in range(2):
                            for n in range(CH):
                                for r in (2 * j, 2 * j + 1):
                                    out = A[64 * (r % 2):64 * (r % 2) + 64, j, n * P:(n + 1) * P]
                                    mm = pe.matmul(out, xdt[:, n, r * HP:(r + 1) * HP], M[:, r, n * P:(n + 1) * P],
                                                   start=True, stop=(n == 0))
                                    if n:
                                        mm = pe.matmul(out, hst[:, n - 1, r * HP:(r + 1) * HP],
                                                       ea[:, r, n * P:(n + 1) * P], start=False, stop=True)
                        mm.then_inc(S.y_ready, 1)
                pe.wait_ge(S.state_added, i * 4 + 2 * s + 2)
                for r in range(R):
                    mm = pe.matmul(Bp[64 * (r % 2):64 * (r % 2) + 64, 0, (r // 2) * NS:(r // 2 + 1) * NS],
                                   xdt[0:NS, CH, r * HP:(r + 1) * HP], Ms[0:NS, r, :], start=True, stop=True)
                mm.then_inc(S.ys_ready, 1)
                if not last:
                    tile(i, s + 1, 3)
                    tile(i, s + 1, 4)
                pe.wait_ge(S.y_squared, g1)
                for j in range(2):
                    for h in range(2):
                        mm = pe.matmul(A[:, h, 0:HT], ones, c.tmp[:, j, h * HT:(h + 1) * HT],
                                       start=(j == 0), stop=(j == 1))
                mm.then_inc(S.y_summed, 1)
                if not last:
                    tile(i, s + 1, 5)

            steps(pe, step)

        @block.scalar
        def _(act):
            def tile(i, s, u):
                act.wait_ge(S.block_done, i * (2 * GT) + GT * s + u + 1)
                ps = LN[u % 2]
                if u >= CT:
                    if s or not isinstance(i, int):
                        act.wait_ge(S.gated, i * 2 + s)
                    act.activation(halves(sz[:, u - CT, :]), ps[:, :, 0:HT], ACT.Silu
                                   ).then_inc(S[f"pair_free{u % 2}"], 1)
                    return
                n = CT * s + u
                act.wait_ge(S.history_in, i * 8 + n + 1)
                b = cb[:, u % 2, :]
                act.activation(b[:, 3:3 + HT], ps[:, 0, 0:HT], ACT.Copy)
                act.activation(b[:, 3 + HT:3 + SEQ], ps[:, 1, 0:SEQ - HT], ACT.Copy)
                act.activation(b[:, 3 + SEQ:].rearrange("p (b t) -> p b t", t=7)[:, :, 3:7],
                               ps[:, 1, SEQ - HT:HT].rearrange("p (b t) -> p b t", t=DS), ACT.Copy
                               ).then_inc(S[f"pair_free{u % 2}"], 1)

            def silu(i, s, u):
                n = CT * s + u
                act.wait_ge(S.conv_summed, i * 8 + n + 1)
                act.activation(xc[:, s % 2, u, 0:SEQ], acc[:, 0:SEQ], ACT.Silu)
                act.activation(xc[:, s % 2, u, SEQ:T].rearrange("p (b t) -> p b t", t=DS), sample_sums(), ACT.Silu
                               ).then_inc(S.conv_done, 1)

            def sample_sums():
                v = arena[:, 2 * CB + SEQ + 3:2 * CB + SEQ + 3 + 56]
                return v.rearrange("p (b t) -> p b t", t=7)[:, :, 0:DS]

            act.wait_ge(S.x_loaded, 16)
            act.wait_ge(S.const_loaded, 16)
            act_norm(c, act, 0)
            act.wait_ge(S.par_loaded, 16)
            act.activation(nega[:], par[0:32, G_ALOG:G_ALOG + 1], ACT.Exp).then_inc(S.a_ready, 1)
            act.wait_ge(S.dt_folded, 2)
            act.activation(dtf[:, 3, :], dtf[:, 3, :], ACT.Exp).then_inc(S.dt_logged, 1)
            act.wait_ge(S.dt_logged, 1)
            act.activation(dtf[:, 3, :], dtf[:, 3, :], ACT.Ln, bias=ones[0:32, 0:1]).then_inc(S.dt_logged, 1)
            for u in range(3):
                tile(0, 0, u)
                silu(0, 0, u)
            act.wait_ge(S.to_end, 1)
            act.activation(cdec[:].rearrange("p c h -> p (c h)"), Bp[:, 0, 0:CH * 32], ACT.Exp)
            act.activation(sdec[:].rearrange("p b h -> p (b h)"), Bp[:, 1, 0:DB * 32], ACT.Exp)
            act.activation(xws[:, 0:CH, :], xws[:, 0:CH, :], ACT.Exp)
            act.activation(xws[0:NS, CH, :], xws[0:NS, CH, :], ACT.Exp).then_inc(S.end_decay, 1)
            for u in range(3, GT):
                tile(0, 0, u)
                if u < CT:
                    silu(0, 0, u)

            def step(i, s):
                g1 = i * 2 + (s + 1)
                last = s == GROUPS - 1
                act.wait_ge(S.b_turned, g1)
                act.activation(Btok.rearrange("p c n -> p (c n)"), Bp[:, 0, :], ACT.Copy).then_inc(S.b_kept, 1)
                act.wait_ge(S.decay_loaded, i * 32 + 16 * (s + 1))
                act.activation(ea.rearrange("p r t -> p (r t)"), abc.rearrange("p r t -> p (r t)"), ACT.Exp
                               ).then_inc(S.ea_ready, 1)
                act.wait_ge(S.seg_ready, g1)
                act.activation(M.rearrange("p r t -> p (r t)"), M.rearrange("p r t -> p (r t)"), ACT.Exp)
                act.activation(Ms[0:NS], Ms[0:NS], ACT.Exp).then_inc(S.decay_ready, 1)
                if not last:
                    for u in range(3):
                        tile(i, s + 1, u)
                        silu(i, s + 1, u)
                    tile(i, s + 1, 3)
                    silu(i, s + 1, 3)
                    tile(i, s + 1, 4)
                act.wait_ge(S.gated, g1)
                act.activation(c.tmp[:].rearrange("p j t -> p (j t)"), yt.rearrange("p j t -> p (j t)"), ACT.Square
                               ).then_inc(S.y_squared, 1)
                act.wait_ge(S.y_summed, g1)
                act.activation(halves(c.rn[:]), A[:, :, 0:HT], ACT.Sqrt, bias=c.eps, scale=1.0 / 256
                               ).then_inc(S.y_rooted, 1)
                if not last:
                    tile(i, s + 1, 5)

            steps(act, step)

        @block.vector
        def _(dve):
            def conv(i, s, u):
                n = CT * s + u
                dve.wait_ge(S[f"pair_free{u % 2}"], i * GT + (GT * s + u) // 2 + 1)
                if n:
                    dve.wait_ge(S.conv_done, i * 8 + n)
                w = (i * 8 + n)
                b = cb[:, u % 2, :]
                dve.tensor_scalar(acc, b[:, 0:CO], one(par, w * 4 + G_CW), one(par, w + G_CBI), ALU.mult, ALU.add
                                  ).then_inc(S.tap_added, 1)
                for k in range(1, 4):
                    dve.wait_ge(S.tap_added, w * 3 + k)
                    ins = dve.scalar_tensor_tensor(out=acc, in0=b[:, k:k + CO], scalar=one(par, w * 4 + (G_CW + k)),
                                                   in1=acc, op0=ALU.mult, op1=ALU.add)
                    ins.then_inc(S.tap_added if k < 3 else S.conv_summed, 1)

            dve.sem_inc(S.group_done, FIRST)
            dve.memset(cb[:, 0, 0:3], 0.0)
            dve.memset(cb[:, 1, 0:3], 0.0).then_inc(S.zero_history, 1)
            dve.wait_ge(S.par_loaded, 16)
            dve_norm(c, dve, 0, G_A)
            dve.wait_ge(S.dt_projected, 1)
            u_, dt_, cs_, w_ = (dtf[:, n, :] for n in range(4))
            dve.tensor_scalar(halves(u_), Bp[0:32, :, 0:HT], par[0:32, G_DTB:G_DTB + 1], None, ALU.add
                              ).then_inc(S.dt_folded, 1)
            dve.wait_ge(S.dt_folded, 1)
            dve.scalar_tensor_tensor(out=w_, in0=u_, scalar=-1.0, in1=u_, op0=ALU.mult, op1=ALU.min
                                     ).then_inc(S.dt_folded, 1)
            dve.wait_ge(S.dt_logged, 2)
            dve.wait_ge(S.a_ready, 1)
            dve.scalar_tensor_tensor(out=dt_, in0=u_, scalar=0.0, in1=w_, op0=ALU.max, op1=ALU.add
                                     ).then_inc(S.dt_step, 1)
            dve.wait_ge(S.dt_step, 1)
            dve.tensor_scalar(u_, dt_, nega[:, 0:1], -1.0, ALU.mult, ALU.mult).then_inc(S.dt_step, 1)
            dve.wait_ge(S.dt_step, 2)
            dve.tensor_tensor_scan(cs_, cst[0:32, C_RST:C_RST + T], u_, 0.0, ALU.mult, ALU.add
                                   ).then_inc(S.decay_summed, 1)
            dve.wait_ge(S.dt_turned, 1)
            for k, t in enumerate((dtt, acst)):
                dve.tensor_copy(t[:, 0:CH, :].rearrange("p c h -> p (c h)"), A[:, k, 0:CH * 32])
                dve.tensor_copy(t[0:NS, CH, :], A[0:NS, k, CH * 32:(CH + 1) * 32]).then_inc(S.dt_kept, 1)
            dve.wait_ge(S.dt_kept, 2)
            dve.tensor_tensor(zl[:], acst[0:NS, CH:CH + 1, :].to_broadcast([NS, DB, 32]),
                              cst[0:NS, C_LAST:C_LAST + DB].unsqueeze(2).to_broadcast([NS, DB, 32]), ALU.mult
                              ).then_inc(S.last_kept, 1)
            for u in range(3):
                conv(0, 0, u)
            dve.wait_ge(S.ends_ready, 1)
            dve.tensor_tensor(xws[:, 0:CH, :].rearrange("p c h -> p (c h)"), Bp[:, 0, 0:CH * 32],
                              acst[:, 0:CH, :].rearrange("p c h -> p (c h)"), ALU.subtract)
            dve.tensor_tensor(xws[0:NS, CH, :], Bp[0:NS, 0, 128:160], acst[0:NS, CH, :], ALU.subtract
                              ).then_inc(S.to_end, 1)
            dve.wait_ge(S.end_decay, 1)
            dve.tensor_tensor(xws[:, 0:CH, :], xws[:, 0:CH, :], dtt[:, 0:CH, :], ALU.mult)
            dve.tensor_tensor(xws[0:NS, CH, :], xws[0:NS, CH, :], dtt[0:NS, CH, :], ALU.mult).then_inc(S.dt_scaled, 1)
            conv(0, 0, 3)
            dve.wait_ge(S.dt_scaled, 1)

            def step(i, s):
                par_ = s % 2
                g1 = i * 2 + (s + 1)
                X = xc[:, par_]
                last = s == GROUPS - 1
                dve.wait_ge(S.decay_loaded, i * 32 + 16 * (s + 1))
                for r in range(R):
                    for n in range(CH):
                        dve.tensor_scalar(M[:, r, n * P:(n + 1) * P], abc[:, r, n * P:(n + 1) * P],
                                          head(acst, n, i, s, r), 0.0, ALU.subtract, ALU.min)
                    ins = dve.tensor_scalar(Ms[0:NS, r, :], abc[0:NS, r, SEQ:T], head(acst, CH, i, s, r)[0:NS], 0.0,
                                            ALU.subtract, ALU.min)
                ins.then_inc(S.seg_ready, 1)
                dve.wait_ge(S.x_turned, g1)
                for k, (dst, sc) in enumerate(((xdt, dtt), (xw, xws))):
                    for n in range(CH):
                        ins = dve.tensor_tensor(
                            dst[:, n, :].rearrange("p (r d) -> p r d", r=R),
                            A[:, n // 2, (n % 2) * 256:(n % 2) * 256 + 256].rearrange("p (r d) -> p r d", r=R),
                            over(heads(sc, n, n + 1, i, s).rearrange("p c r -> p (c r)"), HP), ALU.mult)
                ins.then_inc(S.x_scaled, 1)
                dve.wait_ge(S.cb_ready, g1)
                dve.tensor_tensor(CBm, Bp[:, 1, :].rearrange("p (c n) -> p c n", c=CH),
                                  cst[:, C_CAU:C_CAU + P].unsqueeze(1).to_broadcast([P, CH, P]), ALU.mult
                                  ).then_inc(S.cb_masked, 1)
                dve.wait_ge(S.cb_masked, g1)
                dve.wait_ge(S.decay_ready, g1)
                dve.tensor_tensor(M, M, CBm.rearrange("p c n -> p (c n)").unsqueeze(1).to_broadcast([P, R, SEQ]), ALU.mult)
                dve.tensor_tensor(ea[:, :, P:SEQ], ea[:, :, P:SEQ], X[:, 3:4, P:SEQ].to_broadcast([P, R, SEQ - P]),
                                  ALU.mult)
                dve.wait_ge(S.sample_ready, g1)
                for dst, sc in ((xdt, dtt), (xw, xws)):
                    dve.tensor_tensor(dst[0:NS, CH, :].rearrange("p (r d) -> p r d", r=R),
                                      A[0:NS, 0, 0:256].rearrange("p (r d) -> p r d", r=R),
                                      over(heads(sc, CH, CH + 1, i, s, NS).rearrange("p c r -> p (c r)"), HP),
                                      ALU.mult)
                dve.tensor_tensor(Bm[0:NS], A[0:NS, 1:2, 0:P].to_broadcast([NS, DB, P]),
                                  cst[0:NS, C_BLK:C_BLK + DB].unsqueeze(2).to_broadcast([NS, DB, P]), ALU.mult)
                dve.tensor_tensor(CBs[0:NS, :], A[0:NS, 1, P:P + NS], cst[0:NS, C_SAMP:C_SAMP + NS], ALU.mult
                                  ).then_inc(S.cbs_masked, 1)
                for r in range(R):
                    lo = 64 * (r % 2)
                    dve.tensor_tensor(yoff[lo:lo + 64, r // 2, :], A[lo:lo + 64, 1, 192 + (r // 2) * NS:192 + (r // 2 + 1) * NS],
                                      ea[lo:lo + 64, r, SEQ:T], ALU.mult)
                dve.wait_ge(S.cbs_masked, g1)
                dve.tensor_tensor(Ms[0:NS], Ms[0:NS], CBs[0:NS, :].unsqueeze(1).to_broadcast([NS, R, NS]), ALU.mult
                                  ).then_inc(S.sample_kept, 1)
                if not last:
                    for u in range(3):
                        conv(i, s + 1, u)
                dve.wait_ge(S.states_ready, g1)
                dve.tensor_copy(hst[:, 0, :], A[:, 0, 0:256]).then_inc(S.state_step, 1)
                for n in range(1, CH):
                    v = hst[:, n, :]
                    dve.wait_ge(S.state_step, i * 12 + (6 * s + 2 * n - 1))
                    dve.tensor_tensor(v.rearrange("p (r d) -> p r d", r=R),
                                      hst[:, n - 1, :].rearrange("p (r d) -> p r d", r=R),
                                      over(heads(cdec, n, n + 1, i, s).rearrange("p c r -> p (c r)"), HP),
                                      ALU.mult).then_inc(S.state_step, 1)
                    dve.wait_ge(S.state_step, i * 12 + (6 * s + 2 * n))
                    dve.tensor_tensor(v, v, A[:, n // 2, (n % 2) * 256:(n % 2) * 256 + 256], ALU.add
                                      ).then_inc(S.state_step if n < CH - 1 else S.states_kept, 1)
                dve.wait_ge(S.h0_decayed, g1)
                for q in range(2):
                    dve.wait_ge(S.update_ready, i * 4 + 2 * s + q + 1)
                    v = h0[:, 4 * q:4 * q + 4, :].rearrange("p (a b) x -> p a (b x)", a=2)
                    dve.tensor_tensor(v, v, Bp[:, :, :], ALU.add).then_inc(S.state_added, 1)
                dve.wait_ge(S.y_ready, g1)
                for j in range(2):
                    dve.scalar_tensor_tensor(out=yt[:, j, 0:SEQ], in0=X[:, j, 0:SEQ], scalar=one(par, g1 * 2 + (G_DSK + j - 2)),
                                             in1=A[:, j, :], op0=ALU.mult, op1=ALU.add)
                dve.wait_ge(S.ys_ready, g1)
                for j in range(2):
                    ins = dve.scalar_tensor_tensor(out=yt[:, j, SEQ:T], in0=X[:, j, SEQ:T],
                                                   scalar=one(par, g1 * 2 + (G_DSK + j - 2)),
                                                   in1=Bp[:, 0, j * NS:(j + 1) * NS], op0=ALU.mult, op1=ALU.add)
                ins.then_inc(S.y_skip, 1)
                dve.wait_ge(S.y_skip, g1)
                dve.tensor_tensor(yt[:, :, SEQ:T], yt[:, :, SEQ:T], yoff, ALU.add).then_inc(S.y_summed_up, 1)
                if not last:
                    conv(i, s + 1, 3)
                dve.wait_ge(S.y_rooted, g1)
                dve.reciprocal(c.rn[:], c.rn[:]).then_inc(S.y_inverted, 1)
                dve.wait_ge(S.y_inverted, g1)
                for j in range(2):
                    ins = dve.scalar_tensor_tensor(out=col(c.yT, g1 * 2 + (j - 2)), in0=yt[:, j, :],
                                                   scalar=one(par, g1 * 2 + (G_GN + j - 2)), in1=c.rn[:],
                                                   op0=ALU.mult, op1=ALU.mult)
                ins.then_inc(S.group_done, 1)

            steps(dve, step)

        @block.gpsimd
        def _(pool):
            def history(i, s, u):
                n = CT * s + u
                if n >= 2:
                    pool.wait_ge(S.conv_summed, i * 8 + n - 1)
                    pool.wait_ge(S.history_out, i * 8 + n - 1)
                pool.tensor_copy(cb[:, u % 2, 3 + SEQ:].rearrange("p (b t) -> p b t", t=7)[:, :, 0:3],
                                 col(hist, i * 8 + n).rearrange("p (b t) -> p b t", t=3)).then_inc(S.history_in, 1)

            def keep(i, s, u):
                n = CT * s + u
                pool.wait_ge(S[f"pair_free{u % 2}"], i * GT + (GT * s + u) // 2 + 1)
                v = col(ncv, i * 8 + n)
                pool.tensor_copy(v[:, 0:3], cb[:, u % 2, SEQ:SEQ + 3])
                pool.tensor_copy(v[:, 3:27].rearrange("p (b t) -> p b t", t=3),
                                 cb[:, u % 2, 3 + SEQ:].rearrange("p (b t) -> p b t", t=7)[:, :, 4:7]
                                 ).then_inc(S.history_out, 1)

            def load_state(i, s):
                pool.dma_start(h0.rearrange("p b x -> p (b x)"),
                               c.h0_d[bass.ds(i * 2 + s, 1)].rearrange("a p x -> (a p) x")).then_inc(S.h0_loaded, 16)

            def load_decay(i, s):
                pool.dma_start(abc, c.scr[bass.ds(i * (2 * R) + s * R, R)].unsqueeze(0).to_broadcast([P, R, T])
                               ).then_inc(S.decay_loaded, 16)

            load_state(0, 0)
            pool.wait_ge(S.decay_summed, 1)
            pool.dma_start(c.scr, dtf[:, 2, :]).then_inc(S.decay_written, 16)
            pool.wait_ge(S.hist_loaded, 16)
            history(0, 0, 0)
            history(0, 0, 1)
            pool.wait_ge(S.decay_written, 16)
            load_decay(0, 0)
            for u in range(CT):
                keep(0, 0, u)
                if u + 2 < CT:
                    history(0, 0, u + 2)

            def step(i, s):
                g1 = i * 2 + (s + 1)
                last = s == GROUPS - 1
                if not last:
                    history(i, s + 1, 0)
                    history(i, s + 1, 1)
                pool.wait_ge(S.sample_ready, g1)
                for b in range(DB):
                    v = h0[:, b, :].rearrange("p (r d) -> p r d", r=R)
                    ins = pool.tensor_tensor(v, v, over(heads(sdec, b, b + 1, i, s).rearrange("p c r -> p (c r)"), HP),
                                             ALU.mult)
                ins.then_inc(S.h0_decayed, 1)
                if not last:
                    pool.wait_ge(S.seg_ready, g1)
                    pool.wait_ge(S.ea_ready, g1)
                    load_decay(i, s + 1)
                    for u in range(3):
                        keep(i, s + 1, u)
                        if u + 2 < CT:
                            history(i, s + 1, u + 2)
                pool.wait_ge(S.states_kept, g1)
                pool.dma_start(c.nst_p[bass.ds(i * 2 + s, 1)].rearrange("a p x -> (a p) x"), hst[:, CH - 1, :]
                               ).then_inc(S.state_stored, 16)
                pool.wait_ge(S.y_summed_up, g1)
                pool.wait_ge(S.state_stored, i * 32 + 16 * (s + 1))
                for j in range(2):
                    ins = pool.tensor_tensor(yt[:, j, :], yt[:, j, :], sz[:, j, :], ALU.mult)
                ins.then_inc(S.gated, 1)
                pool.dma_start(c.nst_s[bass.ds(i * 2 + s, 1)].rearrange("a p x -> (a p) x"),
                               h0.rearrange("p b x -> p (b x)")).then_inc(S.samples_stored, 16)
                if not last:
                    keep(i, s + 1, 3)
                    pool.wait_ge(S.samples_stored, i * 32 + 16 * (s + 1))
                    load_state(i, s + 1)

            steps(pool, step)


def pe_tile_norm(c, pe, u, n, weights):
    pe.wait_ge(c.S[f"tile_squared{u}"], n + 1)
    pe.wait_ge(c.S[f"tile_rooted{u}"], n + FIRST)
    for h in range(2):
        mm = pe.matmul(c.AB[u][:, h, 0:HT], weights, c.tmp[:, u, h * HT:(h + 1) * HT], start=True, stop=True)
    mm.then_inc(c.S[f"tile_summed{u}"], 1)


def act_tile_square(c, act, u, n, src):
    act.wait_ge(c.S[f"tile_summed{u}"], n + FIRST)
    act.activation(halves(c.tmp[:, u, :]), src, ACT.Square).then_inc(c.S[f"tile_squared{u}"], 1)


def act_tile_root(c, act, u, n, width):
    act.wait_ge(c.S[f"tile_summed{u}"], n + 1 + FIRST)
    act.wait_ge(c.S[f"tile_normed{u}"], n + FIRST)
    act.activation(halves(c.rq[:, u, :]), c.AB[u][:, :, 0:HT], ACT.Sqrt, bias=c.eps, scale=1.0 / width
                   ).then_inc(c.S[f"tile_rooted{u}"], 1)


def dve_tile_norm(c, dve, u, n, tile, gain):
    dve.wait_ge(c.S[f"tile_rooted{u}"], n + 1 + FIRST)
    dve.reciprocal(c.rq[:, u, :], c.rq[:, u, :]).then_inc(c.S[f"tile_inverted{u}"], 1)
    dve.wait_ge(c.S[f"tile_inverted{u}"], n + 1)
    dve.scalar_tensor_tensor(out=tile, in0=tile, scalar=gain, in1=c.rq[:, u, :], op0=ALU.mult, op1=ALU.mult
                             ).then_inc(c.S[f"tile_normed{u}"], 1)


def pe_mlp(c, pe, layer):
    for half_ in range(2):
        pe_layer(c, pe, f"up{layer}{half_}", c.hT)
        for u in range(2):
            pe.wait_ge(c.S[f"hidden_ready{u}"], FT // 2 * (2 * layer + half_ + 1) + FIRST)
        pe_layer(c, pe, f"dn{layer}{half_}", c.yT)


def act_mlp(c, act, layer):
    for half_ in range(2):
        _, b0, n, _ = c.stage[f"up{layer}{half_}"]
        t0 = FT * (2 * layer + half_)
        with act.Fori(0, n // 2) as i:
            for u in range(2):
                act.wait_ge(c.S.block_done, i * 2 + b0 + u + 1)
                act.wait_ge(c.S[f"hidden_ready{u}"], i + t0 // 2 + FIRST)
                act.activation(halves(c.tmp[:, u, :]), c.LN[u][:, :, 0:HT], ACT.Relu
                               ).then_inc(c.S[f"pair_free{u}"], 1)


def dve_mlp(c, dve, layer):
    for half_ in range(2):
        s0, _, n, _ = c.stage[f"up{layer}{half_}"]
        with dve.Fori(0, n // 2) as i:
            for u in range(2):
                dve.wait_ge(c.S[f"pair_free{u}"], i + s0 // 2 + 1)
                dve.tensor_tensor(col(c.yT, i * 2 + u), c.tmp[:, u, :], c.tmp[:, u, :], ALU.mult
                                  ).then_inc(c.S[f"hidden_ready{u}"], 1)
        add_layer(c, dve, f"dn{layer}{half_}")


def dense_phase(c):
    nc, S = c.nc, c.S
    b_qkv, t_qkv = c.stage["qkv"][1], c.stage["qkv"][0]
    with ExitStack() as ctx:
        block = ctx.enter_context(nc.Block())

        @block.sync
        def _(sp):
            sp_stream(c, sp, c.stage["out"][1] + SLOTS, c.stage["o"][1] - c.stage["out"][1])

        @block.tensor
        def _(pe):
            for u in range(2):
                pe.sem_inc(S[f"tile_summed{u}"], FIRST)
            pe_layer(c, pe, "out", c.yT)
            pe_norm(c, pe, 1)
            pe.wait_ge(S.h_ready, 2)
            pe_mlp(c, pe, 0)
            pe_norm(c, pe, 2)
            for part in range(2):
                pe.wait_ge(S.h_ready, 3 + part)
                with pe.Fori(0, KT // 4) as i:
                    for u in range(4):
                        pe_tile(c, pe, u % 2, i + (b_qkv + KT * part) // 4, [u], c.hT,
                                i * 2 + (t_qkv + KT * part + u) // 2)
                        if u:
                            pe_tile_norm(c, pe, (u - 1) % 2, i * 2 + (KT * part + u - 1) // 2, c.blk64)
                    pe_tile_norm(c, pe, 1, i * 2 + (KT * part + 3) // 2, c.blk64)
            with pe.Fori(0, KT // 4) as i:
                for u in range(4):
                    pe_tile(c, pe, u % 2, i + (b_qkv + 2 * KT) // 4, [u], c.hT, i * 2 + (t_qkv + 2 * KT + u) // 2)

        @block.scalar
        def _(act):
            for u in range(2):
                act.sem_inc(S[f"tile_rooted{u}"], FIRST)
            act_wait_added(c, act, "out")
            act_norm(c, act, 1)
            act_mlp(c, act, 0)
            act_wait_added(c, act, "dn01")
            act_norm(c, act, 2)

            for part in range(2):
                with act.Fori(0, KT // 4) as i:
                    for u in range(4):
                        ps = c.LN[u % 2][:, :, 0:HT]
                        act.wait_ge(S.block_done, i * 4 + b_qkv + KT * part + u + 1)
                        act_tile_square(c, act, u % 2, i * 2 + (KT * part + u) // 2, ps)
                        act.activation(halves(col(c.yT, i * 4 + KT * part + u)), ps, ACT.Copy
                                       ).then_inc(S[f"pair_free{u % 2}"], 1)
                        if u:
                            act_tile_root(c, act, (u - 1) % 2, i * 2 + (KT * part + u - 1) // 2, 64)
                    act_tile_root(c, act, 1, i * 2 + (KT * part + 3) // 2, 64)
            with act.Fori(0, KT // 2) as i:
                for u in range(2):
                    act.wait_ge(S.block_done, i * 2 + b_qkv + 2 * KT + u + 1)
                    act.activation(halves(col(c.vT, i * 2 + u)), c.LN[u][:, :, 0:HT], ACT.Copy
                                   ).then_inc(S[f"pair_free{u}"], 1)

        @block.vector
        def _(dve):
            for u in range(2):
                dve.sem_inc(S[f"hidden_ready{u}"], FIRST)
                dve.sem_inc(S[f"tile_normed{u}"], FIRST)
            add_layer(c, dve, "out")
            dve_norm(c, dve, 1, G_MA)
            dve_mlp(c, dve, 0)
            dve_norm(c, dve, 2, G_B)
            for part in range(2):
                with dve.Fori(0, KT // 2) as i:
                    for u in range(2):
                        dve_tile_norm(c, dve, u, i + KT // 2 * part, col(c.yT, i * 2 + KT * part + u), c.par[:, G_QN - part:G_QN - part + 1])
                if part == 0:
                    dve_scale(c, dve, G_KV)


def attention_phase(c):
    nc, S = c.nc, c.S
    LN, A, Bp, cst, par, ident, ones = c.LN, c.A, c.Bp, c.cst, c.par, c.ident, c.ones
    NB = SEQ // P
    C64 = 64
    with ExitStack() as ctx:
        def sb(name, *shape):
            return ctx.enter_context(nc.sbuf_tensor(name, list(shape), F32))

        kp = sb("kpage", P, PAGES, NH, P)
        vp = sb("vpage", P, PAGES, NH, P)
        vs = sb("vhead", P, SEQ)
        vtok = sb("vtok", P, NB, P)
        pr = sb("probs", P, 2, 2, SEQ)
        qbd = sb("qbd", P, DB, C64)
        sp_ = sb("sprobs", P, PAGES, C64)
        sn = sb("snew", NS, C64)
        mxp = sb("mxp", P, P)
        mb = sb("mb", P, C64)
        mcol = sb("mcol", C64, 1)
        dg = sb("dg", C64, C64)
        rs = sb("rs", P, C64)
        on = sb("on", P, C64)
        vn = sb("vnew", NS, NH, P)
        mx = sb("mx", P, NB, 2)
        nm = sb("nm", P, NB, 2)
        sm = sb("sm", P, NB, 2)
        lam2 = sb("lam2", 64, 2)
        le = sb("le", P, 2)
        nlam = sb("nlam", P, 1)
        gsub = c.gsub
        qz = c.tmp
        aT = c.rn
        block = ctx.enter_context(nc.Block())

        @block.sync
        def _(sp):
            sp.dma_start(c.k_o, c.yT[:, KT:2 * KT, :]).then_inc(S.stored, 16)
            sp.dma_start(c.v_o, c.vT[:]).then_inc(S.stored, 16)

            sp.wait_ge(S.table_loaded, 16)

            def load(b, first):
                for p in range(PAGES):
                    page = sp.value_load(c.pt[0:1, bass.ds(b * PAGES + p, 1)], min_val=0, max_val=c.n_pool - 1)
                    for buf, src, used, loaded in ((kp, c.ck_d, S.kpage_used, "kpage"), (vp, c.cv_d, S.vpage_used, "vpage")):
                        if not first:
                            sp.wait_ge(used, b * PAGES + (p + 1 - PAGES))
                        sp.dma_start(buf[:, p].rearrange("p h x -> p (h x)"),
                                     src[bass.ds(page, 1)].rearrange("a p x -> (a p) x")
                                     ).then_inc(S[f"{loaded}{p}"], 16)

            load(0, True)
            with sp.Fori(1, DB) as b:
                load(b, False)

        @block.tensor
        def _(pe):
            for first in (S.block_weighed, S.scores_ready, S.v_turned):
                pe.sem_inc(first, FIRST)
            for h in range(NH):
                mm = pe.transpose(LN[0][0:NS, h // 4, (h % 4) * P:(h % 4 + 1) * P], c.vT[:, h, SEQ:T], ident)
            mm.then_inc(S.vnew_turned, 1)
            pe.wait_ge(S.lam_products, 1)
            pe.matmul(A[:, 0, 0:2], ones[0:64, :], lam2[:], start=True, stop=True).then_inc(S.lam_summed, 1)
            pe.wait_ge(S.vnew_kept, 1)
            pe.wait_ge(S.lam_ready, 1)
            pe.wait_ge(S.qbd_ready, 1)

            with pe.Fori(0, NH) as j:
                def scores(i):
                    w = (i + 1) * P
                    pe.wait_ge(S.exps_done, j * NB + i + FIRST)
                    for cc in range(2):
                        k = c.yT[:, bass.ds(j + KT, 1), 0:w].rearrange("p a x -> p (a x)")
                        pe.matmul(A[:, cc, 0:w], qz[:, cc, i * P:(i + 1) * P], k, start=True, stop=False)
                        mm = pe.matmul(A[:, cc, w - P:w], ident, cst[:, C_NEG:C_NEG + P], start=False, stop=True)
                    mm.then_inc(S.scores_ready, 1)

                def weigh(i):
                    pe.wait_ge(S.weights_ready, j * NB + i + 1)
                    for k in range(i + 1):
                        mm = pe.transpose(LN[0][:, i % 2, k * P:(k + 1) * P], pr[:, i % 2, 0, k * P:(k + 1) * P], ident)
                    mm.then_inc(S.weights_turned, 1)
                    pe.wait_ge(S.weights_kept, j * NB + i + 1)
                    for k in range(i + 1):
                        mm = pe.matmul(LN[1][:, 0, i * P:(i + 1) * P], vtok[:, k, :], aT[:, k * P:(k + 1) * P],
                                       start=(k == 0), stop=(k == i))
                    mm.then_inc(S.block_weighed, 1)

                pe.wait_ge(S.head_copied, j + 1 + FIRST)
                for k in range(NB):
                    mm = pe.transpose(LN[1][:, 1, k * P:(k + 1) * P], vs[:, k * P:(k + 1) * P], ident)
                mm.then_inc(S.v_turned, 1)
                scores(0)
                for p in range(PAGES):
                    pe.wait_ge(S[f"kpage{p}"], j * 16 + 16)
                    if p == 0:
                        pe.wait_ge(S.sample_out, j + FIRST)
                    for h in range(NH):
                        mm = pe.matmul(Bp[:, 0, p * C64 + h * 8:p * C64 + h * 8 + 8], kp[:, p, h, :],
                                       qbd[:, bass.ds(j, 1), h * 8:h * 8 + 8].rearrange("p a x -> p (a x)"),
                                       start=True, stop=True)
                    mm.then_inc(S.kpage_used, 1)
                for h in range(NH):
                    mm = pe.matmul(Bp[0:NS, 1, h * 8:h * 8 + 8], c.yT[:, KT + h, SEQ:T],
                                   qbd[:, bass.ds(j, 1), h * 8:h * 8 + 8].rearrange("p a x -> p (a x)"),
                                   start=True, stop=True)
                mm.then_inc(S.sscores_ready, 1)
                scores(1)
                pe.wait_ge(S.page_max, j + 1)
                pe.transpose(Bp[:, 1, 64:64 + P], mxp[:], ident).then_inc(S.max_turned, 1)
                pe.wait_ge(S.v_kept, j + 1)
                pe.wait_ge(S.head_out, j + FIRST)
                weigh(0)
                pe.wait_ge(S.max_diag, j + 1)
                pe.matmul(Bp[:, 1, 192:256], ones[0:C64, :], dg[:], start=True, stop=True).then_inc(S.max_spread, 1)
                scores(2)
                weigh(1)
                pe.wait_ge(S.sexps_done, j + 1)
                for p in range(PAGES):
                    pe.matmul(Bp[:, 1, 256:320], ones, sp_[:, p, :], start=(p == 0), stop=False)
                pe.matmul(Bp[:, 1, 256:320], ones[0:NS, :], sn[:], start=False, stop=True)
                for p in range(PAGES):
                    pe.wait_ge(S[f"vpage{p}"], j * 16 + 16)
                    for h in range(NH):
                        mm = pe.matmul(Bp[:, 1, 320 + h * 8:328 + h * 8], vp[:, p, h, :], sp_[:, p, h * 8:h * 8 + 8],
                                       start=(p == 0 and h == 0), stop=False, skip_group_check=True)
                    mm.then_inc(S.vpage_used, 1)
                for h in range(NH):
                    mm = pe.matmul(Bp[:, 1, 320 + h * 8:328 + h * 8], vn[:, h, :], sn[:, h * 8:h * 8 + 8],
                                   start=False, stop=(h == NH - 1), skip_group_check=True)
                mm.then_inc(S.sample_weighed, 1)
                scores(3)
                weigh(2)
                weigh(3)

        @block.scalar
        def _(act):
            act.sem_inc(S.exps_done, FIRST)
            act.sem_inc(S.head_out, FIRST)
            act.wait_ge(S.vnew_turned, 1)
            act.activation(vn[:].rearrange("p (a h) x -> p a (h x)", a=2), LN[0][0:NS, :, :], ACT.Copy
                           ).then_inc(S.vnew_kept, 1)
            act.wait_ge(S.lam_summed, 1)
            act.activation(le[:], A[:, 0, 0:2], ACT.Exp).then_inc(S.lam_exps, 1)

            with act.Fori(0, NH) as j:
                def exps(i):
                    w = (i + 1) * P
                    act.wait_ge(S.negmax_ready, j * NB + i + 1)
                    if i >= 2:
                        act.wait_ge(S.weights_turned, j * NB + i - 1)
                    for cc in range(2):
                        ins = act.activation(pr[:, i % 2, cc, 0:w], A[:, cc, 0:w], ACT.Exp, bias=nm[:, i, cc:cc + 1],
                                             scale=SCALE, accum_out=sm[:, i, cc:cc + 1])
                    ins.then_inc(S.exps_done, 1)

                def keep_weights(i):
                    act.wait_ge(S.weights_turned, j * NB + i + 1)
                    act.wait_ge(S.block_weighed, j * NB + i + FIRST)
                    act.activation(aT[:, 0:(i + 1) * P], LN[0][:, i % 2, 0:(i + 1) * P], ACT.Copy
                                   ).then_inc(S.weights_kept, 1)

                act.wait_ge(S.v_turned, j + 1 + FIRST)
                act.activation(vtok[:].rearrange("p k x -> p (k x)"), LN[1][:, 1, :], ACT.Copy).then_inc(S.v_kept, 1)
                exps(0)
                exps(1)
                keep_weights(0)
                act.wait_ge(S.max_taken, j + 1)
                act.activation(sp_[:].rearrange("p g x -> p (g x)"), sp_[:].rearrange("p g x -> p (g x)"), ACT.Exp,
                               scale=SCALE)
                act.activation(sn[:], sn[:], ACT.Exp, scale=SCALE).then_inc(S.sexps_done, 1)
                exps(2)
                keep_weights(1)
                exps(3)
                keep_weights(2)
                keep_weights(3)
                act.wait_ge(S.block_weighed, j * NB + NB + FIRST)
                act.activation(c.hT[:, bass.ds(j, 1), 0:SEQ].rearrange("p a x -> p (a x)"), LN[1][:, 0, :], ACT.Copy
                               ).then_inc(S.head_out, 1)

        @block.vector
        def _(dve):
            dve.sem_inc(S.sample_out, FIRST)
            lp = par[0:64, G_LAM:G_LAM + 4].rearrange("p (m two) -> p m two", two=2)
            dve.tensor_tensor(lam2[:], lp[:, :, 0], lp[:, :, 1], ALU.mult).then_inc(S.lam_products, 1)
            dve.tensor_scalar(gsub[:], par[:, G_SUB:G_SUB + 1], 1.0 - LAM_INIT, None, ALU.mult)
            dve.wait_ge(S.lam_exps, 1)
            dve.tensor_tensor(nlam[:], le[:, 1:2], le[:, 0:1], ALU.subtract).then_inc(S.lam_step, 1)
            dve.wait_ge(S.lam_step, 1)
            dve.tensor_scalar(nlam[:], nlam[:], -LAM_INIT, None, ALU.add).then_inc(S.lam_ready, 1)
            dve.wait_ge(S.lam_ready, 1)

            with dve.Fori(0, NH) as j:
                def maxima(i):
                    dve.wait_ge(S.scores_ready, j * NB + i + 1 + FIRST)
                    dve.tensor_reduce(mx[:, i, :], A[:, :, 0:(i + 1) * P], AX.X, ALU.max).then_inc(S.max_ready, 1)
                    dve.wait_ge(S.max_ready, j * NB + i + 1)
                    dve.tensor_scalar(nm[:, i, :], mx[:, i, :], -SCALE, None, ALU.mult).then_inc(S.negmax_ready, 1)

                def combine(i):
                    w = (i + 1) * P
                    n = j * (3 * NB) + 3 * i
                    dve.wait_ge(S.exps_done, j * NB + i + 1 + FIRST)
                    dve.reciprocal(sm[:, i, :], sm[:, i, :]).then_inc(S.combine_step, 1)
                    dve.wait_ge(S.combine_step, n + 1)
                    dve.tensor_scalar(sm[:, i, 1:2], sm[:, i, 1:2], nlam[:, 0:1], None, ALU.mult
                                      ).then_inc(S.combine_step, 1)
                    dve.tensor_scalar(pr[:, i % 2, 0, 0:w], pr[:, i % 2, 0, 0:w], sm[:, i, 0:1], None, ALU.mult
                                      ).then_inc(S.combine_step, 1)
                    dve.wait_ge(S.combine_step, n + 3)
                    dve.scalar_tensor_tensor(out=pr[:, i % 2, 0, 0:w], in0=pr[:, i % 2, 1, 0:w], scalar=sm[:, i, 1:2],
                                             in1=pr[:, i % 2, 0, 0:w], op0=ALU.mult, op1=ALU.add
                                             ).then_inc(S.weights_ready, 1)

                maxima(0)
                combine(0)
                dve.wait_ge(S.sscores_ready, j + 1)
                dve.tensor_reduce(mxp[:, 0:C64], Bp[:, 0, :].rearrange("p (g x) -> p x g", g=PAGES), AX.X, ALU.max)
                dve.tensor_tensor(sn[:], Bp[0:NS, 1, 0:C64],
                                  cst[0:NS, C_NEWM:C_NEWM + DB * C64].rearrange("p (b x) -> p b x", b=DB)
                                  [:, bass.ds(j, 1), :].rearrange("p a x -> p (a x)"), ALU.add
                                  ).then_inc(S.new_masked, 1)
                dve.wait_ge(S.new_masked, j + 1)
                dve.tensor_tensor(mxp[0:NS, 0:C64], mxp[0:NS, 0:C64], sn[:], ALU.max).then_inc(S.page_max, 1)
                maxima(1)
                combine(1)
                dve.wait_ge(S.max_turned, j + 1)
                dve.tensor_reduce(mcol[:], Bp[0:C64, 1, 64:64 + P], AX.X, ALU.max).then_inc(S.max_col, 1)
                dve.wait_ge(S.max_col, j + 1)
                dve.tensor_scalar(dg[:], ident[0:C64, 0:C64], mcol[:, 0:1], None, ALU.mult).then_inc(S.max_diag, 1)
                dve.wait_ge(S.max_spread, j + 1)
                dve.tensor_copy(mb[:], Bp[:, 1, 192:256]).then_inc(S.max_kept, 1)
                dve.wait_ge(S.max_kept, j + 1)
                dve.tensor_tensor(sp_[:], Bp[:, 0, :].rearrange("p (g x) -> p g x", g=PAGES),
                                  mb[:].unsqueeze(1).to_broadcast([P, PAGES, C64]), ALU.subtract)
                dve.tensor_tensor(sn[:], sn[:], mb[0:NS, :], ALU.subtract).then_inc(S.max_taken, 1)
                maxima(2)
                combine(2)
                dve.wait_ge(S.sample_weighed, j + 1)
                dve.reciprocal(rs[:], Bp[:, 1, 256:320]).then_inc(S.sample_step, 1)
                dve.wait_ge(S.sample_step, j * 2 + 1)
                dve.tensor_tensor(on[:], Bp[:, 1, 320:384], rs[:], ALU.mult).then_inc(S.sample_step, 1)
                dve.wait_ge(S.sample_step, j * 2 + 2)
                v = on[:].rearrange("p (h c q) -> p h c q", h=NH, c=2)
                dve.scalar_tensor_tensor(out=c.hT[:, :, bass.ds(j * DS + SEQ, DS)], in0=v[:, :, 1, :],
                                         scalar=nlam[:, 0:1], in1=v[:, :, 0, :], op0=ALU.mult, op1=ALU.add
                                         ).then_inc(S.sample_out, 1)
                maxima(3)
                combine(3)

        @block.gpsimd
        def _(pool):
            pool.sem_inc(S.head_copied, FIRST)
            pool.memset(qz[:], 0.0).then_inc(S.zeroed, 1)
            pool.memset(mxp[:], 0.0)
            pool.memset(qbd[:], 0.0).then_inc(S.zeroed, 1)
            pool.wait_ge(S.zeroed, 2)
            d = qbd[:].rearrange("p b (h c q) -> p b h c q", h=NH, c=2)
            for cc in range(2):
                lo = 64 * cc
                for h in range(NH):
                    ins = pool.tensor_copy(d[lo:lo + 64, :, h, cc, :],
                                           c.yT[lo:lo + 64, h, SEQ:T].rearrange("p (b q) -> p b q", q=DS))
            ins.then_inc(S.qbd_ready, 1)
            pool.wait_ge(S.qbd_ready, 1)
            with pool.Fori(0, NH) as j:
                pool.wait_ge(S.scores_ready, j * NB + FIRST)
                pool.wait_ge(S.v_turned, j + FIRST)
                pool.wait_ge(S.head_copied, j + FIRST)
                for cc in range(2):
                    lo = 64 * cc
                    ins = pool.tensor_copy(qz[lo:lo + 64, cc, 0:SEQ],
                                           c.yT[lo:lo + 64, bass.ds(j, 1), 0:SEQ].rearrange("p a x -> p (a x)"))
                ins.then_inc(S.q_copied, 1)
                pool.wait_ge(S.q_copied, j + 1)
                pool.tensor_copy(vs[:], c.vT[:, bass.ds(j, 1), 0:SEQ].rearrange("p a x -> p (a x)")
                                 ).then_inc(S.head_copied, 1)


def last_phase(c, blocks):
    nc, S = c.nc, c.S
    n0 = KT
    with ExitStack() as ctx:
        block = ctx.enter_context(nc.Block())

        @block.sync
        def _(sp):
            b0 = c.stage["o"][1] + SLOTS
            sp_stream(c, sp, b0, blocks - b0)
            for u in range(2):
                sp.wait_ge(S[f"pair_free{u}"], (c.stage["dn11"][0] + KT) // 2)
            sp.dma_start(c.y_o, c.xT[:]).then_inc(S.stored, 16)
            sp.wait_ge(S.stored, 64)
            sp.wait_ge(S.state_stored, 16 * GROUPS)
            sp.wait_ge(S.samples_stored, 16 * GROUPS)

        @block.tensor
        def _(pe):
            with pe.Fori(0, NH // 2) as i:
                for u in range(2):
                    pe_tile_norm(c, pe, u, i + n0, c.ones)
            for u in range(2):
                pe.wait_ge(S[f"tile_normed{u}"], n0 + NH // 2 + FIRST)
            pe_layer(c, pe, "o", c.hT)
            pe_norm(c, pe, 3)
            pe.wait_ge(S.h_ready, 5)
            pe_mlp(c, pe, 1)

        @block.scalar
        def _(act):
            with act.Fori(0, NH // 2) as i:
                for u in range(2):
                    act_tile_square(c, act, u, i + n0, halves(col(c.hT, i * 2 + u)))
                    act_tile_root(c, act, u, i + n0, P)
            act_wait_added(c, act, "o")
            act_norm(c, act, 3)
            act_mlp(c, act, 1)

        @block.vector
        def _(dve):
            with dve.Fori(0, NH // 2) as i:
                for u in range(2):
                    dve_tile_norm(c, dve, u, i + n0, col(c.hT, i * 2 + u), c.gsub[:, 0:1])
            add_layer(c, dve, "o")
            dve_norm(c, dve, 3, G_MB)
            dve_mlp(c, dve, 1)


OUTS = {
    "y_o": (P, KT, T), "nst_p": (GROUPS, P, R * HP), "nconv_o": (P, 32, 27), "k_o": (P, KT, T), "v_o": (P, KT, T),
    "nst_s": (GROUPS, P, DB * R * HP),
}


def build_program(nc, wblocks, wdt, xin, cst_d, par_d, hist_d, h0_d, ck_d, cv_d, pt_d,
                  y_o, nst_p, nconv_o, k_o, v_o, nst_s):
    with ExitStack() as ctx:
        c = Chip()
        c.nc, c.wblocks, c.wdt, c.xin, c.cst_d, c.par_d, c.hist_d, c.h0_d = nc, wblocks, wdt, xin, cst_d, par_d, hist_d, h0_d
        c.ck_d, c.cv_d, c.y_o, c.nst_p, c.nconv_o, c.k_o, c.v_o, c.nst_s = ck_d, cv_d, y_o, nst_p, nconv_o, k_o, v_o, nst_s
        c.n_pool = ck_d.shape[0]
        c.scr = nc.dram_tensor("decay_scratch", (32, T), F32, kind="Internal").ap()
        c.S = Sems(nc, ctx)
        c.stage, blocks = plan()

        def sb(name, shape, dt=F32):
            return ctx.enter_context(nc.sbuf_tensor(name, shape, dt))

        c.xT = sb("xT", [P, KT, T])
        c.hT = sb("hT", [P, KT, T])
        c.yT = sb("yT", [P, 2 * KT, T])
        c.ring = sb("ring", [P, SLOTS, D])
        c.cst = sb("cst", [P, C_W])
        c.par = sb("par", [P, G_W])
        c.tmp = sb("tmp", [P, 2, T])
        c.rn = sb("rn", [P, T])
        c.gsub = sb("gsub", [P, 1])
        c.pt = sb("pt", [1, DB * PAGES], I32)
        c.LN = [ctx.enter_context(nc.psum_tensor(f"LN{n}", [P, 2, 512], F32)) for n in range(2)]
        c.A = ctx.enter_context(nc.psum_tensor("A", [P, 2, 512], F32))
        c.Bp = ctx.enter_context(nc.psum_tensor("Bp", [P, 2, 512], F32))
        c.AB = [c.A, c.Bp]
        c.ident, c.ones = c.cst[:, C_ID:C_ID + P], c.cst[:, C_ONE:C_ONE + P]
        c.blk64, c.eps = c.cst[:, C_B64:C_B64 + P], c.cst[:, C_EPS:C_EPS + 1]
        c.pt_d = pt_d
        mixer_phase(c)
        with ExitStack() as mid:
            c.vT = mid.enter_context(nc.sbuf_tensor("vT", [P, KT, T], F32))
            with ExitStack() as dense:
                c.rq = dense.enter_context(nc.sbuf_tensor("rq", [P, 2, T], F32))
                dense_phase(c)
            attention_phase(c)
        with ExitStack() as end:
            c.rq = end.enter_context(nc.sbuf_tensor("rq2", [P, 2, T], F32))
            last_phase(c, blocks)


def feature_tiles(a):
    return a.reshape(-1, P).T


def weight_blocks(w):
    k, n = w.shape
    w = w.reshape(k // D, KT, P, n // P, P).transpose(3, 0, 2, 1, 4)
    return w.reshape(-1, P, KT * P)


def kernel(**inputs):
    import concourse.bacc as bacc
    from concourse.bass_utils import run_bass_kernel_spmd

    a = {k: np.asarray(v) for k, v in inputs.items()}
    DI = 2 * D
    w_in = a["w_in_a"][0]
    zc, xcols, bcols, ccols = 0, DI, 2 * DI, 2 * DI + D
    order, conv_order = [], []
    for g in range(GROUPS):
        conv = [xcols + 256 * g, xcols + 256 * g + P, bcols + P * g, ccols + P * g]
        order += conv + [zc + 256 * g, zc + 256 * g + P]
        conv_order += [o - DI for o in conv]
    cols = np.concatenate([np.arange(o, o + P) for o in order])
    ccol = np.concatenate([np.arange(o, o + P) for o in conv_order])
    up, dn = a["w_up"], a["w_down"]
    half = DF // 2
    parts = [weight_blocks(w_in[:, cols]), weight_blocks(a["w_out_a"][0])]
    mlps = []
    for layer in range(2):
        mlps.append([b for h in range(2) for b in (weight_blocks(up[layer][:, h * half:(h + 1) * half]),
                                                   weight_blocks(dn[layer][h * half:(h + 1) * half]))])
    parts += mlps[0] + [weight_blocks(a["w_q"][0]), weight_blocks(a["w_kv"]), weight_blocks(a["w_o"][0])] + mlps[1]
    wblocks = np.concatenate(parts)
    wdt = w_in[:, DI + 2 * DI:].reshape(KT, P, 32).transpose(1, 0, 2).reshape(P, KT * 32)

    x = np.concatenate([a["x_prompt"][0], a["x_sample"].reshape(NS, D)])
    xin = x.T.reshape(KT, P, T).transpose(1, 0, 2)

    par = np.zeros((P, G_W), np.float32)
    for at, v in ((G_A, a["norm_a"][0]), (G_MA, a["norm_m"][0]), (G_KV, a["kv_norm"]), (G_B, a["norm_b"][0]),
                  (G_MB, a["norm_m"][1])):
        par[:, at:at + KT] = feature_tiles(v)
    par[:, G_GN:G_GN + 16] = feature_tiles(a["gnorm_w"][0])
    par[:, G_DSK:G_DSK + 16] = feature_tiles(np.repeat(a["d_skip"][0], HP))
    par[:, G_CW:G_CW + P] = a["conv_w"][0][:, ccol].reshape(4, 32, P).transpose(2, 1, 0).reshape(P, P)
    par[:, G_CBI:G_CBI + 32] = a["conv_b"][0][ccol].reshape(32, P).T
    par[:, G_KN] = np.tile(a["k_norm"], 2)
    par[:, G_QN] = np.tile(a["q_norm"][0], 2)
    par[:, G_SUB] = a["subln"][0]
    par[:32, G_DTB] = a["dt_bias"][0]
    par[:32, G_ALOG] = a["a_log"][0]
    for n, k in enumerate(("lam_q1", "lam_k1", "lam_q2", "lam_k2")):
        par[:64, G_LAM + n] = a[k][0]

    hist = a["state_conv"][0][:, :, ccol].reshape(DB, 3, 32, P).transpose(3, 2, 0, 1).reshape(P, 32, 24)
    h0 = a["state_ssm"][0].reshape(DB, GROUPS, R * HP, P).transpose(1, 3, 0, 2).reshape(GROUPS, P, DB * R * HP)
    n_pool = a["cache_k"].shape[0]
    ck = a["cache_k"].reshape(n_pool, P, NH, P).transpose(0, 3, 2, 1).reshape(n_pool, P, NH * P)
    cv = a["cache_v"].reshape(n_pool, P, NH * P)

    arrays = {
        "wblocks": wblocks, "wdt": wdt, "xin": xin, "cst_d": constants(), "par_d": par, "hist_d": hist, "h0_d": h0,
        "ck_d": ck, "cv_d": cv, "pt_d": a["page_table"].reshape(1, DB * PAGES),
    }
    arrays = {k: np.ascontiguousarray(v) for k, v in arrays.items()}
    nc = bacc.Bacc("TRN2", target_bir_lowering=False, num_devices=1)
    aps = {k: nc.dram_tensor(k, v.shape, mybir.dt.from_np(v.dtype), kind="ExternalInput").ap()
           for k, v in arrays.items()}
    aps |= {k: nc.dram_tensor(k, s, F32, kind="ExternalOutput").ap() for k, s in OUTS.items()}
    build_program(nc, **aps)
    r = run_bass_kernel_spmd(nc, [arrays], core_ids=[0]).results[0]

    def tokens(o):
        t = o.transpose(2, 1, 0).reshape(T, D)
        return t[:SEQ], t[SEQ:].reshape(DB, DS, D)

    y_p, y_s = tokens(r["y_o"])
    k_p, k_s = tokens(r["k_o"])
    v_p, v_s = tokens(r["v_o"])
    ssm_p = r["nst_p"].transpose(0, 2, 1).reshape(1, 1, 32, HP, P)
    ssm_s = r["nst_s"].reshape(GROUPS, P, DB, R * HP).transpose(2, 0, 3, 1).reshape(1, DB, 32, HP, P)
    back = np.argsort(ccol)
    conv = r["nconv_o"].transpose(2, 1, 0).reshape(27, 32 * P)[:, back]
    return (
        y_p.reshape(1, SEQ, D), y_s, ssm_p, conv[:3].reshape(1, 1, 3, -1), k_p.reshape(1, SEQ, NH, 2, 64),
        v_p.reshape(1, SEQ, NH, P), ssm_s, conv[3:].reshape(DB, 3, -1)[None], k_s.reshape(DB, DS, NH, 2, 64),
        v_s.reshape(DB, DS, NH, P),
    )
```

```python
from contextlib import ExitStack

import numpy as np

import concourse.bass as bass
from concourse import mybir

F32 = mybir.dt.float32
I32 = mybir.dt.int32
ACT = mybir.ActivationFunctionType
ALU = mybir.AluOpType
AX = mybir.AxisListType

P = 128
D = 1024
KT = D // P
SEQ = 512
DB, DS = 8, 4
NS = DB * DS
T = SEQ + NS
HT = T // 2
GROUPS = 8
R = 4
HP = 64
CH = SEQ // P
GT = 6
CT = 4
NH = 8
DF = 4096
FT = DF // P // 2
PAGES = 8
PAST = P * PAGES
SLOTS = 4
NEG = -1.0e30
SCALE = 64 ** -0.5
LAM_INIT = 0.8 - 0.6 * float(np.exp(-0.3))
EPS = 1e-6
CB = 3 + SEQ + DB * 7
FIRST = 1
CO = CB - 3

C_ID, C_ONE, C_B64, C_CAU, C_NEG, C_ELAST = (P * n for n in range(6))
C_SAMP = 6 * P
C_SELE = C_SAMP + NS
C_LAST = C_SELE + NS
C_BLK = C_LAST + DB
C_RST = C_BLK + DB
C_NEWM = C_RST + T
C_PAT = C_NEWM + DB * NS
C_COMP = C_PAT + 32
C_EPS = C_COMP + 2
C_W = C_EPS + 1

G_A, G_MA, G_KV, G_B, G_MB = (KT * n for n in range(5))
G_GN = 5 * KT
G_DSK = G_GN + 16
G_CW = G_DSK + 16
G_CBI = G_CW + 32 * 4
G_KN = G_CBI + 32
G_QN = G_KN + 1
G_SUB = G_QN + 1
G_DTB = G_SUB + 1
G_ALOG = G_DTB + 1
G_LAM = G_ALOG + 1
G_W = G_LAM + 4


def constants():
    c = np.zeros((P, C_W), np.float32)
    i = np.arange(P)
    c[:, C_ID:C_ID + P] = np.eye(P)
    c[:, C_ONE:C_ONE + P] = 1
    c[:, C_B64:C_B64 + P] = (i[:, None] // 64 == i[None] // 64)
    c[:, C_CAU:C_CAU + P] = (i[None] >= i[:, None])
    c[:, C_NEG:C_NEG + P] = np.where(i[None] > i[:, None], NEG, 0)
    c[P - 1, C_ELAST:C_ELAST + P] = 1
    s = np.arange(NS)
    same = s[:, None] // DS == s[None] // DS
    c[:NS, C_SAMP:C_SAMP + NS] = same & (s[None] >= s[:, None])
    c[:NS, C_SELE:C_SELE + NS] = s[:, None] == DS * (s[None] // DS) + DS - 1
    b = np.arange(DB)
    c[:NS, C_LAST:C_LAST + DB] = s[:, None] == DS * b[None] + DS - 1
    c[:NS, C_BLK:C_BLK + DB] = s[:, None] // DS == b[None]
    t = np.arange(T)
    c[:NS, C_RST:C_RST + T] = np.where(t < SEQ, t % P != 0, (t - SEQ) % DS != 0)
    q = i % DS
    ok = (s[None, None] // DS == b[None, :, None]) & (s[None, None] % DS <= q[:, None, None])
    c[:, C_NEWM:C_NEWM + DB * NS] = np.where(ok, 0, NEG).reshape(P, -1)
    used = i % 32 < 16
    column = 8 * (i // 32) + 4 * (i % 16 // 8) + q
    c[:, C_PAT:C_PAT + 32] = used[:, None] & (column[:, None] == np.arange(32)[None])
    c[:, C_COMP] = i // 4 % 2 == 0
    c[:, C_COMP + 1] = i // 4 % 2 == 1
    c[:, C_EPS] = EPS
    return c


class Sems:

    def __init__(self, nc, ctx):
        self.nc, self.ctx, self.made = nc, ctx, {}

    def __getattr__(self, name):
        return self[name]

    def __getitem__(self, name):
        if name not in self.made:
            self.made[name] = self.ctx.enter_context(self.nc.semaphore(name))
        return self.made[name]


class Chip:
    pass


def col(t, k):
    return t[:, bass.ds(k, 1), :].rearrange("p a x -> p (a x)")


def one(t, c):
    return t[:, bass.ds(c, 1)]


def halves(ap):
    return ap.rearrange("p (h t) -> p h t", h=2)


def plan():
    stage, tiles, blocks = {}, 0, 0
    for name, n, nb in [("in", GT * GROUPS, 1), ("out", KT, 2), ("up00", FT, 1), ("dn00", KT, 2), ("up01", FT, 1),
                        ("dn01", KT, 2), ("qkv", 3 * KT, 1), ("o", KT, 1), ("up10", FT, 1), ("dn10", KT, 2),
                        ("up11", FT, 1), ("dn11", KT, 2)]:
        stage[name] = (tiles, blocks, n, nb)
        tiles += n
        blocks += n * nb
    return stage, blocks


def sp_stream(c, sp, b0, n):
    with sp.Fori(b0 // SLOTS, (b0 + n) // SLOTS) as i:
        for u in range(SLOTS):
            sp.wait_ge(c.S.block_done, i * SLOTS + (u + 1 - SLOTS))
            sp.dma_start(c.ring[:, u, :], c.wblocks[bass.ds(i * SLOTS + u, 1)].rearrange("a p n -> (a p) n")
                         ).then_inc(c.S[f"slot_loaded{u}"], 16)


def pe_tile(c, pe, pair, turn, slots, src, free, src_k=0):
    pe.wait_ge(c.S[f"pair_free{pair}"], free)
    for n, u in enumerate(slots):
        pe.wait_ge(c.S[f"slot_loaded{u}"], turn * 16 + 16)
        for k in range(KT):
            for h in range(2):
                mm = pe.matmul(c.LN[pair][:, h, 0:HT], c.ring[:, u, k * P:(k + 1) * P],
                               src[:, src_k + n * KT + k, h * HT:(h + 1) * HT],
                               start=(n == 0 and k == 0), stop=(n == len(slots) - 1 and k == KT - 1))
        mm.then_inc(c.S.block_done, 1)


def pe_layer(c, pe, name, src):
    t0, b0, n, nb = c.stage[name]
    per = SLOTS // nb
    with pe.Fori(0, n // per) as i:
        for u in range(per):
            pe_tile(c, pe, u % 2, i + b0 // SLOTS, range(u * nb, u * nb + nb), src, i * (per // 2) + (t0 + u) // 2)


def add_layer(c, dve, name):
    t0, b0, n, nb = c.stage[name]
    with dve.Fori(0, n // 2) as i:
        for u in range(2):
            dve.wait_ge(c.S.block_done, i * (2 * nb) + b0 + (u + 1) * nb)
            x = halves(col(c.xT, i * 2 + u))
            dve.tensor_tensor(x, x, c.LN[u][:, :, 0:HT], ALU.add).then_inc(c.S[f"pair_free{u}"], 1)


def act_wait_added(c, act, name):
    t0, _, n, _ = c.stage[name]
    for u in range(2):
        act.wait_ge(c.S[f"pair_free{u}"], (t0 + n) // 2)


def act_norm(c, act, n):
    for k in range(KT):
        if k >= 2 or n:
            act.wait_ge(c.S.square_summed, n * KT + k - 1)
        act.activation(c.tmp[:, k % 2, :], c.xT[:, k, :], ACT.Square).then_inc(c.S.squared, 1)
    act.wait_ge(c.S.square_summed, (n + 1) * KT)
    act.activation(halves(c.rn[:]), c.A[:, :, 0:HT], ACT.Sqrt, bias=c.eps, scale=1.0 / D).then_inc(c.S.rooted, 1)


def pe_norm(c, pe, n):
    for k in range(KT):
        pe.wait_ge(c.S.squared, n * KT + k + 1)
        for h in range(2):
            mm = pe.matmul(c.A[:, h, 0:HT], c.ones, c.tmp[:, k % 2, h * HT:(h + 1) * HT],
                           start=(k == 0), stop=(k == KT - 1))
        mm.then_inc(c.S.square_summed, 1)


def dve_norm(c, dve, n, gains):
    dve.wait_ge(c.S.rooted, n + 1)
    dve.reciprocal(c.rn[:], c.rn[:]).then_inc(c.S.inverted, 1)
    dve.wait_ge(c.S.inverted, n + 1)
    dve_scale(c, dve, gains)


def dve_scale(c, dve, gains):
    for k in range(KT):
        ins = dve.scalar_tensor_tensor(out=c.hT[:, k, :], in0=c.xT[:, k, :], scalar=c.par[:, gains + k:gains + k + 1],
                                       in1=c.rn[:], op0=ALU.mult, op1=ALU.mult)
    ins.then_inc(c.S.h_ready, 1)


def mixer_phase(c):
    nc, S = c.nc, c.S
    with ExitStack() as ctx:
        arena = ctx.enter_context(nc.sbuf_tensor("mixer_arena", [P, 22560], F32))
        top = [0]

        def carve(*shape, at=None):
            n = int(np.prod(shape))
            lo = top[0] if at is None else at
            if at is None:
                top[0] += n
                assert top[0] <= 22560, top[0]
            v = arena[:, lo:lo + n]
            if len(shape) > 1:
                names = "abcd"[:len(shape)]
                v = v.rearrange(f"p ({' '.join(names)}) -> p {' '.join(names)}", **dict(zip(names, shape)))
            return v

        cb = carve(2, CB)
        acc = carve(CO)
        xc = carve(2, CT, T)
        sz = carve(2, T)
        abc = carve(R, T)
        dt_at = top[0]
        M = carve(R, SEQ)
        Ms = carve(R, NS)
        ea = carve(R, T)
        xdt = carve(CH + 1, R * HP)
        xw = carve(CH + 1, R * HP)
        Btok = carve(CH, P)
        Bm = carve(DB, P)
        CBm = carve(CH, P)
        CBs = carve(NS)
        hst = carve(CH, R * HP)
        h0 = carve(DB, R * HP)
        yt = carve(2, T)
        yoff = carve(2, NS)
        dtf = carve(4, T, at=dt_at)[0:32]
        dtw = ctx.enter_context(nc.sbuf_tensor("dtw", [P, KT * 32], F32))
        dtt = ctx.enter_context(nc.sbuf_tensor("dtt", [P, CH + 1, 32], F32))
        acst = ctx.enter_context(nc.sbuf_tensor("acst", [P, CH + 1, 32], F32))
        xws = ctx.enter_context(nc.sbuf_tensor("xws", [P, CH + 1, 32], F32))
        cdec = ctx.enter_context(nc.sbuf_tensor("cdec", [P, CH, 32], F32))
        sdec = ctx.enter_context(nc.sbuf_tensor("sdec", [P, DB, 32], F32))
        zl = ctx.enter_context(nc.sbuf_tensor("zl", [NS, DB, 32], F32))
        hist = ctx.enter_context(nc.sbuf_tensor("hist", [P, 32, 24], F32))
        ncv = ctx.enter_context(nc.sbuf_tensor("ncv", [P, 32, 27], F32))
        nega = ctx.enter_context(nc.sbuf_tensor("nega", [32, 1], F32))
        A, Bp, LN, cst, par = c.A, c.Bp, c.LN, c.cst, c.par
        ident, ones = c.ident, c.ones

        def heads(t, n0, n1, i, s, rows=P):
            return t[0:rows, n0:n1, bass.ds(i * (2 * R) + s * R, R)]

        def head(t, n, i, s, r):
            return t[:, n, bass.ds(i * (2 * R) + (s * R + r), 1)]

        def over(ap, n):
            return ap.unsqueeze(len(ap.shape)).to_broadcast(list(ap.shape) + [n])

        block = ctx.enter_context(nc.Block())

        def steps(eng, step):
            with eng.Fori(0, GROUPS // 2 - 1) as i:
                step(i, 0)
                step(i, 1)
            step(0, GROUPS - 2)
            step(0, GROUPS - 1)

        @block.sync
        def _(sp):
            sp.dma_start(c.cst[:], c.cst_d).then_inc(S.const_loaded, 16)
            sp.dma_start(c.xT[:], c.xin).then_inc(S.x_loaded, 16)
            sp.dma_start(c.par[:], c.par_d).then_inc(S.par_loaded, 16)
            sp.dma_start(dtw[:], c.wdt).then_inc(S.dtw_loaded, 16)
            sp.dma_start(c.pt[:], c.pt_d).then_inc(S.table_loaded, 16)
            for u in range(SLOTS):
                sp.dma_start(c.ring[:, u, :], c.wblocks[u]).then_inc(S[f"slot_loaded{u}"], 16)
            sp.dma_start(hist[:], c.hist_d).then_inc(S.hist_loaded, 16)
            sp_stream(c, sp, SLOTS, GT * GROUPS)
            sp.wait_ge(S.history_out, 4 * GROUPS)
            sp.dma_start(c.nconv_o, ncv[:]).then_inc(S.stored, 16)

        @block.tensor
        def _(pe):
            def tile(i, s, u):
                pe_tile(c, pe, u % 2, i * 3 + (GT * s + u) // SLOTS, [(GT * s + u) % SLOTS], c.hT,
                        i * GT + (GT * s + u) // 2)

            pe.wait_ge(S.const_loaded, 16)
            pe_norm(c, pe, 0)
            pe.wait_ge(S.h_ready, 1)
            pe.wait_ge(S.dtw_loaded, 16)
            for k in range(KT):
                for h in range(2):
                    mm = pe.matmul(Bp[0:32, h, 0:HT], dtw[:, k * 32:(k + 1) * 32], c.hT[:, k, h * HT:(h + 1) * HT],
                                   start=(k == 0), stop=(k == KT - 1))
            mm.then_inc(S.dt_projected, 1)
            for u in range(3):
                tile(0, 0, u)
            pe.wait_ge(S.decay_summed, 1)
            for n in range(CH + 1):
                m = P if n < CH else NS
                pe.transpose(A[0:m, 0, n * 32:(n + 1) * 32], dtf[:, 1, n * P:n * P + m], ident[0:32, 0:32])
                mm = pe.transpose(A[0:m, 1, n * 32:(n + 1) * 32], dtf[:, 2, n * P:n * P + m], ident[0:32, 0:32])
            mm.then_inc(S.dt_turned, 1)
            pe.wait_ge(S.dt_kept, 2)
            pe.matmul(Bp[:, 0, 0:CH * 32], cst[:, C_ELAST:C_ELAST + P], acst[:, 0:CH, :].rearrange("p c h -> p (c h)"),
                      start=True, stop=True)
            pe.matmul(Bp[0:NS, 0, 128:160], cst[0:NS, C_SELE:C_SELE + NS], acst[0:NS, CH, :], start=True, stop=True)
            pe.wait_ge(S.last_kept, 1)
            pe.matmul(Bp[:, 1, 0:DB * 32], ones[0:NS, :], zl[:].rearrange("p b h -> p (b h)"),
                      start=True, stop=True).then_inc(S.ends_ready, 1)
            for u in range(3, GT):
                tile(0, 0, u)

            def step(i, s):
                par_ = s % 2
                g1 = i * 2 + (s + 1)
                X = xc[:, par_]
                pe.wait_ge(S.conv_done, i * 8 + 4 * s + 4)
                pe.wait_ge(S.group_done, i * 2 + s + FIRST)
                if s == 0:
                    pe.wait_ge(S.dt_scaled, 1)
                for n in range(CH):
                    for j in range(2):
                        mm = pe.transpose(A[:, n // 2, (n % 2) * 256 + j * P:(n % 2) * 256 + (j + 1) * P],
                                          X[:, j, n * P:(n + 1) * P], ident)
                mm.then_inc(S.x_turned, 1)
                for n in range(CH):
                    mm = pe.transpose(Bp[:, 0, n * P:(n + 1) * P], X[:, 2, n * P:(n + 1) * P], ident)
                mm.then_inc(S.b_turned, 1)
                for n in range(CH):
                    mm = pe.matmul(Bp[:, 1, n * P:(n + 1) * P], X[:, 2, n * P:(n + 1) * P], X[:, 3, n * P:(n + 1) * P],
                                   start=True, stop=True)
                mm.then_inc(S.cb_ready, 1)
                pe.wait_ge(S.x_scaled, g1)
                for j in range(2):
                    pe.transpose(A[0:NS, 0, j * P:(j + 1) * P], X[:, j, SEQ:T], ident)
                pe.transpose(A[0:NS, 1, 0:P], X[:, 2, SEQ:T], ident)
                pe.matmul(A[0:NS, 1, P:P + NS], X[:, 2, SEQ:T], X[:, 3, SEQ:T], start=True, stop=True)
                pe.wait_ge(S.h0_loaded, i * 32 + 16 * (s + 1))
                for b in range(DB):
                    for j in range(2):
                        lo = 192 + j * NS + DS * b
                        mm = pe.matmul(A[:, 1, lo:lo + DS], h0[:, b, j * P:(j + 1) * P],
                                       X[:, 3, SEQ + DS * b:SEQ + DS * (b + 1)], start=True, stop=True)
                mm.then_inc(S.sample_ready, 1)
                last = s == GROUPS - 1
                if not last:
                    for u in range(3):
                        tile(i, s + 1, u)
                pe.wait_ge(S.b_kept, g1)
                pe.wait_ge(S.sample_kept, g1)
                for n in range(CH):
                    mm = pe.matmul(A[:, n // 2, (n % 2) * 256:(n % 2) * 256 + 256], Btok[:, n, :], xw[:, n, :],
                                   start=True, stop=True)
                mm.then_inc(S.states_ready, 1)
                for q in range(2):
                    if q:
                        pe.wait_ge(S.state_added, i * 4 + 2 * s + 1)
                    for b in range(4 * q, 4 * q + 4):
                        mm = pe.matmul(Bp[:, (b // 2) % 2, (b % 2) * 256:(b % 2) * 256 + 256], Bm[0:NS, b, :],
                                       xw[0:NS, CH, :], start=True, stop=True)
                    mm.then_inc(S.update_ready, 1)
                    if q == 0:
                        pe.wait_ge(S.states_kept, g1)
                        for j in range(2):
                            for n in range(CH):
                                for r in (2 * j, 2 * j + 1):
                                    out = A[64 * (r % 2):64 * (r % 2) + 64, j, n * P:(n + 1) * P]
                                    mm = pe.matmul(out, xdt[:, n, r * HP:(r + 1) * HP], M[:, r, n * P:(n + 1) * P],
                                                   start=True, stop=(n == 0))
                                    if n:
                                        mm = pe.matmul(out, hst[:, n - 1, r * HP:(r + 1) * HP],
                                                       ea[:, r, n * P:(n + 1) * P], start=False, stop=True)
                        mm.then_inc(S.y_ready, 1)
                pe.wait_ge(S.state_added, i * 4 + 2 * s + 2)
                for r in range(R):
                    mm = pe.matmul(Bp[64 * (r % 2):64 * (r % 2) + 64, 0, (r // 2) * NS:(r // 2 + 1) * NS],
                                   xdt[0:NS, CH, r * HP:(r + 1) * HP], Ms[0:NS, r, :], start=True, stop=True)
                mm.then_inc(S.ys_ready, 1)
                if not last:
                    tile(i, s + 1, 3)
                    tile(i, s + 1, 4)
                pe.wait_ge(S.y_squared, g1)
                for j in range(2):
                    for h in range(2):
                        mm = pe.matmul(A[:, h, 0:HT], ones, c.tmp[:, j, h * HT:(h + 1) * HT],
                                       start=(j == 0), stop=(j == 1))
                mm.then_inc(S.y_summed, 1)
                if not last:
                    tile(i, s + 1, 5)

            steps(pe, step)

        @block.scalar
        def _(act):
            def tile(i, s, u):
                act.wait_ge(S.block_done, i * (2 * GT) + GT * s + u + 1)
                ps = LN[u % 2]
                if u >= CT:
                    if s or not isinstance(i, int):
                        act.wait_ge(S.gated, i * 2 + s)
                    act.activation(halves(sz[:, u - CT, :]), ps[:, :, 0:HT], ACT.Silu
                                   ).then_inc(S[f"pair_free{u % 2}"], 1)
                    return
                n = CT * s + u
                act.wait_ge(S.history_in, i * 8 + n + 1)
                b = cb[:, u % 2, :]
                act.activation(b[:, 3:3 + HT], ps[:, 0, 0:HT], ACT.Copy)
                act.activation(b[:, 3 + HT:3 + SEQ], ps[:, 1, 0:SEQ - HT], ACT.Copy)
                act.activation(b[:, 3 + SEQ:].rearrange("p (b t) -> p b t", t=7)[:, :, 3:7],
                               ps[:, 1, SEQ - HT:HT].rearrange("p (b t) -> p b t", t=DS), ACT.Copy
                               ).then_inc(S[f"pair_free{u % 2}"], 1)

            def silu(i, s, u):
                n = CT * s + u
                act.wait_ge(S.conv_summed, i * 8 + n + 1)
                act.activation(xc[:, s % 2, u, 0:SEQ], acc[:, 0:SEQ], ACT.Silu)
                act.activation(xc[:, s % 2, u, SEQ:T].rearrange("p (b t) -> p b t", t=DS), sample_sums(), ACT.Silu
                               ).then_inc(S.conv_done, 1)

            def sample_sums():
                v = arena[:, 2 * CB + SEQ + 3:2 * CB + SEQ + 3 + 56]
                return v.rearrange("p (b t) -> p b t", t=7)[:, :, 0:DS]

            act.wait_ge(S.x_loaded, 16)
            act.wait_ge(S.const_loaded, 16)
            act_norm(c, act, 0)
            act.wait_ge(S.par_loaded, 16)
            act.activation(nega[:], par[0:32, G_ALOG:G_ALOG + 1], ACT.Exp).then_inc(S.a_ready, 1)
            act.wait_ge(S.dt_folded, 2)
            act.activation(dtf[:, 3, :], dtf[:, 3, :], ACT.Exp).then_inc(S.dt_logged, 1)
            act.wait_ge(S.dt_logged, 1)
            act.activation(dtf[:, 3, :], dtf[:, 3, :], ACT.Ln, bias=ones[0:32, 0:1]).then_inc(S.dt_logged, 1)
            for u in range(3):
                tile(0, 0, u)
                silu(0, 0, u)
            act.wait_ge(S.to_end, 1)
            act.activation(cdec[:].rearrange("p c h -> p (c h)"), Bp[:, 0, 0:CH * 32], ACT.Exp)
            act.activation(sdec[:].rearrange("p b h -> p (b h)"), Bp[:, 1, 0:DB * 32], ACT.Exp)
            act.activation(xws[:, 0:CH, :], xws[:, 0:CH, :], ACT.Exp)
            act.activation(xws[0:NS, CH, :], xws[0:NS, CH, :], ACT.Exp).then_inc(S.end_decay, 1)
            for u in range(3, GT):
                tile(0, 0, u)
                if u < CT:
                    silu(0, 0, u)

            def step(i, s):
                g1 = i * 2 + (s + 1)
                last = s == GROUPS - 1
                act.wait_ge(S.b_turned, g1)
                act.activation(Btok.rearrange("p c n -> p (c n)"), Bp[:, 0, :], ACT.Copy).then_inc(S.b_kept, 1)
                act.wait_ge(S.decay_loaded, i * 32 + 16 * (s + 1))
                act.activation(ea.rearrange("p r t -> p (r t)"), abc.rearrange("p r t -> p (r t)"), ACT.Exp
                               ).then_inc(S.ea_ready, 1)
                act.wait_ge(S.seg_ready, g1)
                act.activation(M.rearrange("p r t -> p (r t)"), M.rearrange("p r t -> p (r t)"), ACT.Exp)
                act.activation(Ms[0:NS], Ms[0:NS], ACT.Exp).then_inc(S.decay_ready, 1)
                if not last:
                    for u in range(3):
                        tile(i, s + 1, u)
                        silu(i, s + 1, u)
                    tile(i, s + 1, 3)
                    silu(i, s + 1, 3)
                    tile(i, s + 1, 4)
                act.wait_ge(S.gated, g1)
                act.activation(c.tmp[:].rearrange("p j t -> p (j t)"), yt.rearrange("p j t -> p (j t)"), ACT.Square
                               ).then_inc(S.y_squared, 1)
                act.wait_ge(S.y_summed, g1)
                act.activation(halves(c.rn[:]), A[:, :, 0:HT], ACT.Sqrt, bias=c.eps, scale=1.0 / 256
                               ).then_inc(S.y_rooted, 1)
                if not last:
                    tile(i, s + 1, 5)

            steps(act, step)

        @block.vector
        def _(dve):
            def conv(i, s, u):
                n = CT * s + u
                dve.wait_ge(S[f"pair_free{u % 2}"], i * GT + (GT * s + u) // 2 + 1)
                if n:
                    dve.wait_ge(S.conv_done, i * 8 + n)
                w = (i * 8 + n)
                b = cb[:, u % 2, :]
                dve.tensor_scalar(acc, b[:, 0:CO], one(par, w * 4 + G_CW), one(par, w + G_CBI), ALU.mult, ALU.add
                                  ).then_inc(S.tap_added, 1)
                for k in range(1, 4):
                    dve.wait_ge(S.tap_added, w * 3 + k)
                    ins = dve.scalar_tensor_tensor(out=acc, in0=b[:, k:k + CO], scalar=one(par, w * 4 + (G_CW + k)),
                                                   in1=acc, op0=ALU.mult, op1=ALU.add)
                    ins.then_inc(S.tap_added if k < 3 else S.conv_summed, 1)

            dve.sem_inc(S.group_done, FIRST)
            dve.memset(cb[:, 0, 0:3], 0.0)
            dve.memset(cb[:, 1, 0:3], 0.0).then_inc(S.zero_history, 1)
            dve.wait_ge(S.par_loaded, 16)
            dve_norm(c, dve, 0, G_A)
            dve.wait_ge(S.dt_projected, 1)
            u_, dt_, cs_, w_ = (dtf[:, n, :] for n in range(4))
            dve.tensor_scalar(halves(u_), Bp[0:32, :, 0:HT], par[0:32, G_DTB:G_DTB + 1], None, ALU.add
                              ).then_inc(S.dt_folded, 1)
            dve.wait_ge(S.dt_folded, 1)
            dve.scalar_tensor_tensor(out=w_, in0=u_, scalar=-1.0, in1=u_, op0=ALU.mult, op1=ALU.min
                                     ).then_inc(S.dt_folded, 1)
            dve.wait_ge(S.dt_logged, 2)
            dve.wait_ge(S.a_ready, 1)
            dve.scalar_tensor_tensor(out=dt_, in0=u_, scalar=0.0, in1=w_, op0=ALU.max, op1=ALU.add
                                     ).then_inc(S.dt_step, 1)
            dve.wait_ge(S.dt_step, 1)
            dve.tensor_scalar(u_, dt_, nega[:, 0:1], -1.0, ALU.mult, ALU.mult).then_inc(S.dt_step, 1)
            dve.wait_ge(S.dt_step, 2)
            dve.tensor_tensor_scan(cs_, cst[0:32, C_RST:C_RST + T], u_, 0.0, ALU.mult, ALU.add
                                   ).then_inc(S.decay_summed, 1)
            dve.wait_ge(S.dt_turned, 1)
            for k, t in enumerate((dtt, acst)):
                dve.tensor_copy(t[:, 0:CH, :].rearrange("p c h -> p (c h)"), A[:, k, 0:CH * 32])
                dve.tensor_copy(t[0:NS, CH, :], A[0:NS, k, CH * 32:(CH + 1) * 32]).then_inc(S.dt_kept, 1)
            dve.wait_ge(S.dt_kept, 2)
            dve.tensor_tensor(zl[:], acst[0:NS, CH:CH + 1, :].to_broadcast([NS, DB, 32]),
                              cst[0:NS, C_LAST:C_LAST + DB].unsqueeze(2).to_broadcast([NS, DB, 32]), ALU.mult
                              ).then_inc(S.last_kept, 1)
            for u in range(3):
                conv(0, 0, u)
            dve.wait_ge(S.ends_ready, 1)
            dve.tensor_tensor(xws[:, 0:CH, :].rearrange("p c h -> p (c h)"), Bp[:, 0, 0:CH * 32],
                              acst[:, 0:CH, :].rearrange("p c h -> p (c h)"), ALU.subtract)
            dve.tensor_tensor(xws[0:NS, CH, :], Bp[0:NS, 0, 128:160], acst[0:NS, CH, :], ALU.subtract
                              ).then_inc(S.to_end, 1)
            dve.wait_ge(S.end_decay, 1)
            dve.tensor_tensor(xws[:, 0:CH, :], xws[:, 0:CH, :], dtt[:, 0:CH, :], ALU.mult)
            dve.tensor_tensor(xws[0:NS, CH, :], xws[0:NS, CH, :], dtt[0:NS, CH, :], ALU.mult).then_inc(S.dt_scaled, 1)
            conv(0, 0, 3)
            dve.wait_ge(S.dt_scaled, 1)

            def step(i, s):
                par_ = s % 2
                g1 = i * 2 + (s + 1)
                X = xc[:, par_]
                last = s == GROUPS - 1
                dve.wait_ge(S.decay_loaded, i * 32 + 16 * (s + 1))
                for r in range(R):
                    for n in range(CH):
                        dve.tensor_scalar(M[:, r, n * P:(n + 1) * P], abc[:, r, n * P:(n + 1) * P],
                                          head(acst, n, i, s, r), 0.0, ALU.subtract, ALU.min)
                    ins = dve.tensor_scalar(Ms[0:NS, r, :], abc[0:NS, r, SEQ:T], head(acst, CH, i, s, r)[0:NS], 0.0,
                                            ALU.subtract, ALU.min)
                ins.then_inc(S.seg_ready, 1)
                dve.wait_ge(S.x_turned, g1)
                for k, (dst, sc) in enumerate(((xdt, dtt), (xw, xws))):
                    for n in range(CH):
                        ins = dve.tensor_tensor(
                            dst[:, n, :].rearrange("p (r d) -> p r d", r=R),
                            A[:, n // 2, (n % 2) * 256:(n % 2) * 256 + 256].rearrange("p (r d) -> p r d", r=R),
                            over(heads(sc, n, n + 1, i, s).rearrange("p c r -> p (c r)"), HP), ALU.mult)
                ins.then_inc(S.x_scaled, 1)
                dve.wait_ge(S.cb_ready, g1)
                dve.tensor_tensor(CBm, Bp[:, 1, :].rearrange("p (c n) -> p c n", c=CH),
                                  cst[:, C_CAU:C_CAU + P].unsqueeze(1).to_broadcast([P, CH, P]), ALU.mult
                                  ).then_inc(S.cb_masked, 1)
                dve.wait_ge(S.cb_masked, g1)
                dve.wait_ge(S.decay_ready, g1)
                dve.tensor_tensor(M, M, CBm.rearrange("p c n -> p (c n)").unsqueeze(1).to_broadcast([P, R, SEQ]), ALU.mult)
                dve.tensor_tensor(ea[:, :, P:SEQ], ea[:, :, P:SEQ], X[:, 3:4, P:SEQ].to_broadcast([P, R, SEQ - P]),
                                  ALU.mult)
                dve.wait_ge(S.sample_ready, g1)
                for dst, sc in ((xdt, dtt), (xw, xws)):
                    dve.tensor_tensor(dst[0:NS, CH, :].rearrange("p (r d) -> p r d", r=R),
                                      A[0:NS, 0, 0:256].rearrange("p (r d) -> p r d", r=R),
                                      over(heads(sc, CH, CH + 1, i, s, NS).rearrange("p c r -> p (c r)"), HP),
                                      ALU.mult)
                dve.tensor_tensor(Bm[0:NS], A[0:NS, 1:2, 0:P].to_broadcast([NS, DB, P]),
                                  cst[0:NS, C_BLK:C_BLK + DB].unsqueeze(2).to_broadcast([NS, DB, P]), ALU.mult)
                dve.tensor_tensor(CBs[0:NS, :], A[0:NS, 1, P:P + NS], cst[0:NS, C_SAMP:C_SAMP + NS], ALU.mult
                                  ).then_inc(S.cbs_masked, 1)
                for r in range(R):
                    lo = 64 * (r % 2)
                    dve.tensor_tensor(yoff[lo:lo + 64, r // 2, :], A[lo:lo + 64, 1, 192 + (r // 2) * NS:192 + (r // 2 + 1) * NS],
                                      ea[lo:lo + 64, r, SEQ:T], ALU.mult)
                dve.wait_ge(S.cbs_masked, g1)
                dve.tensor_tensor(Ms[0:NS], Ms[0:NS], CBs[0:NS, :].unsqueeze(1).to_broadcast([NS, R, NS]), ALU.mult
                                  ).then_inc(S.sample_kept, 1)
                if not last:
                    for u in range(3):
                        conv(i, s + 1, u)
                dve.wait_ge(S.states_ready, g1)
                dve.tensor_copy(hst[:, 0, :], A[:, 0, 0:256]).then_inc(S.state_step, 1)
                for n in range(1, CH):
                    v = hst[:, n, :]
                    dve.wait_ge(S.state_step, i * 12 + (6 * s + 2 * n - 1))
                    dve.tensor_tensor(v.rearrange("p (r d) -> p r d", r=R),
                                      hst[:, n - 1, :].rearrange("p (r d) -> p r d", r=R),
                                      over(heads(cdec, n, n + 1, i, s).rearrange("p c r -> p (c r)"), HP),
                                      ALU.mult).then_inc(S.state_step, 1)
                    dve.wait_ge(S.state_step, i * 12 + (6 * s + 2 * n))
                    dve.tensor_tensor(v, v, A[:, n // 2, (n % 2) * 256:(n % 2) * 256 + 256], ALU.add
                                      ).then_inc(S.state_step if n < CH - 1 else S.states_kept, 1)
                dve.wait_ge(S.h0_decayed, g1)
                for q in range(2):
                    dve.wait_ge(S.update_ready, i * 4 + 2 * s + q + 1)
                    v = h0[:, 4 * q:4 * q + 4, :].rearrange("p (a b) x -> p a (b x)", a=2)
                    dve.tensor_tensor(v, v, Bp[:, :, :], ALU.add).then_inc(S.state_added, 1)
                dve.wait_ge(S.y_ready, g1)
                for j in range(2):
                    dve.scalar_tensor_tensor(out=yt[:, j, 0:SEQ], in0=X[:, j, 0:SEQ], scalar=one(par, g1 * 2 + (G_DSK + j - 2)),
                                             in1=A[:, j, :], op0=ALU.mult, op1=ALU.add)
                dve.wait_ge(S.ys_ready, g1)
                for j in range(2):
                    ins = dve.scalar_tensor_tensor(out=yt[:, j, SEQ:T], in0=X[:, j, SEQ:T],
                                                   scalar=one(par, g1 * 2 + (G_DSK + j - 2)),
                                                   in1=Bp[:, 0, j * NS:(j + 1) * NS], op0=ALU.mult, op1=ALU.add)
                ins.then_inc(S.y_skip, 1)
                dve.wait_ge(S.y_skip, g1)
                dve.tensor_tensor(yt[:, :, SEQ:T], yt[:, :, SEQ:T], yoff, ALU.add).then_inc(S.y_summed_up, 1)
                if not last:
                    conv(i, s + 1, 3)
                dve.wait_ge(S.y_rooted, g1)
                dve.reciprocal(c.rn[:], c.rn[:]).then_inc(S.y_inverted, 1)
                dve.wait_ge(S.y_inverted, g1)
                for j in range(2):
                    ins = dve.scalar_tensor_tensor(out=col(c.yT, g1 * 2 + (j - 2)), in0=yt[:, j, :],
                                                   scalar=one(par, g1 * 2 + (G_GN + j - 2)), in1=c.rn[:],
                                                   op0=ALU.mult, op1=ALU.mult)
                ins.then_inc(S.group_done, 1)

            steps(dve, step)

        @block.gpsimd
        def _(pool):
            def history(i, s, u):
                n = CT * s + u
                if n >= 2:
                    pool.wait_ge(S.conv_summed, i * 8 + n - 1)
                    pool.wait_ge(S.history_out, i * 8 + n - 1)
                pool.tensor_copy(cb[:, u % 2, 3 + SEQ:].rearrange("p (b t) -> p b t", t=7)[:, :, 0:3],
                                 col(hist, i * 8 + n).rearrange("p (b t) -> p b t", t=3)).then_inc(S.history_in, 1)

            def keep(i, s, u):
                n = CT * s + u
                pool.wait_ge(S[f"pair_free{u % 2}"], i * GT + (GT * s + u) // 2 + 1)
                v = col(ncv, i * 8 + n)
                pool.tensor_copy(v[:, 0:3], cb[:, u % 2, SEQ:SEQ + 3])
                pool.tensor_copy(v[:, 3:27].rearrange("p (b t) -> p b t", t=3),
                                 cb[:, u % 2, 3 + SEQ:].rearrange("p (b t) -> p b t", t=7)[:, :, 4:7]
                                 ).then_inc(S.history_out, 1)

            def load_state(i, s):
                pool.dma_start(h0.rearrange("p b x -> p (b x)"),
                               c.h0_d[bass.ds(i * 2 + s, 1)].rearrange("a p x -> (a p) x")).then_inc(S.h0_loaded, 16)

            def load_decay(i, s):
                pool.dma_start(abc, c.scr[bass.ds(i * (2 * R) + s * R, R)].unsqueeze(0).to_broadcast([P, R, T])
                               ).then_inc(S.decay_loaded, 16)

            load_state(0, 0)
            pool.wait_ge(S.decay_summed, 1)
            pool.dma_start(c.scr, dtf[:, 2, :]).then_inc(S.decay_written, 16)
            pool.wait_ge(S.hist_loaded, 16)
            history(0, 0, 0)
            history(0, 0, 1)
            pool.wait_ge(S.decay_written, 16)
            load_decay(0, 0)
            for u in range(CT):
                keep(0, 0, u)
                if u + 2 < CT:
                    history(0, 0, u + 2)

            def step(i, s):
                g1 = i * 2 + (s + 1)
                last = s == GROUPS - 1
                if not last:
                    history(i, s + 1, 0)
                    history(i, s + 1, 1)
                pool.wait_ge(S.sample_ready, g1)
                for b in range(DB):
                    v = h0[:, b, :].rearrange("p (r d) -> p r d", r=R)
                    ins = pool.tensor_tensor(v, v, over(heads(sdec, b, b + 1, i, s).rearrange("p c r -> p (c r)"), HP),
                                             ALU.mult)
                ins.then_inc(S.h0_decayed, 1)
                if not last:
                    pool.wait_ge(S.seg_ready, g1)
                    pool.wait_ge(S.ea_ready, g1)
                    load_decay(i, s + 1)
                    for u in range(3):
                        keep(i, s + 1, u)
                        if u + 2 < CT:
                            history(i, s + 1, u + 2)
                pool.wait_ge(S.states_kept, g1)
                pool.dma_start(c.nst_p[bass.ds(i * 2 + s, 1)].rearrange("a p x -> (a p) x"), hst[:, CH - 1, :]
                               ).then_inc(S.state_stored, 16)
                pool.wait_ge(S.y_summed_up, g1)
                pool.wait_ge(S.state_stored, i * 32 + 16 * (s + 1))
                for j in range(2):
                    ins = pool.tensor_tensor(yt[:, j, :], yt[:, j, :], sz[:, j, :], ALU.mult)
                ins.then_inc(S.gated, 1)
                pool.dma_start(c.nst_s[bass.ds(i * 2 + s, 1)].rearrange("a p x -> (a p) x"),
                               h0.rearrange("p b x -> p (b x)")).then_inc(S.samples_stored, 16)
                if not last:
                    keep(i, s + 1, 3)
                    pool.wait_ge(S.samples_stored, i * 32 + 16 * (s + 1))
                    load_state(i, s + 1)

            steps(pool, step)


def pe_tile_norm(c, pe, u, n, weights):
    pe.wait_ge(c.S[f"tile_squared{u}"], n + 1)
    pe.wait_ge(c.S[f"tile_rooted{u}"], n + FIRST)
    for h in range(2):
        mm = pe.matmul(c.AB[u][:, h, 0:HT], weights, c.tmp[:, u, h * HT:(h + 1) * HT], start=True, stop=True)
    mm.then_inc(c.S[f"tile_summed{u}"], 1)


def act_tile_square(c, act, u, n, src):
    act.wait_ge(c.S[f"tile_summed{u}"], n + FIRST)
    act.activation(halves(c.tmp[:, u, :]), src, ACT.Square).then_inc(c.S[f"tile_squared{u}"], 1)


def act_tile_root(c, act, u, n, width):
    act.wait_ge(c.S[f"tile_summed{u}"], n + 1 + FIRST)
    act.wait_ge(c.S[f"tile_normed{u}"], n + FIRST)
    act.activation(halves(c.rq[:, u, :]), c.AB[u][:, :, 0:HT], ACT.Sqrt, bias=c.eps, scale=1.0 / width
                   ).then_inc(c.S[f"tile_rooted{u}"], 1)


def dve_tile_norm(c, dve, u, n, tile, gain):
    dve.wait_ge(c.S[f"tile_rooted{u}"], n + 1 + FIRST)
    dve.reciprocal(c.rq[:, u, :], c.rq[:, u, :]).then_inc(c.S[f"tile_inverted{u}"], 1)
    dve.wait_ge(c.S[f"tile_inverted{u}"], n + 1)
    dve.scalar_tensor_tensor(out=tile, in0=tile, scalar=gain, in1=c.rq[:, u, :], op0=ALU.mult, op1=ALU.mult
                             ).then_inc(c.S[f"tile_normed{u}"], 1)


def pe_mlp(c, pe, layer):
    for half_ in range(2):
        pe_layer(c, pe, f"up{layer}{half_}", c.hT)
        for u in range(2):
            pe.wait_ge(c.S[f"hidden_ready{u}"], FT // 2 * (2 * layer + half_ + 1) + FIRST)
        pe_layer(c, pe, f"dn{layer}{half_}", c.yT)


def act_mlp(c, act, layer):
    for half_ in range(2):
        _, b0, n, _ = c.stage[f"up{layer}{half_}"]
        t0 = FT * (2 * layer + half_)
        with act.Fori(0, n // 2) as i:
            for u in range(2):
                act.wait_ge(c.S.block_done, i * 2 + b0 + u + 1)
                act.wait_ge(c.S[f"hidden_ready{u}"], i + t0 // 2 + FIRST)
                act.activation(halves(c.tmp[:, u, :]), c.LN[u][:, :, 0:HT], ACT.Relu
                               ).then_inc(c.S[f"pair_free{u}"], 1)


def dve_mlp(c, dve, layer):
    for half_ in range(2):
        s0, _, n, _ = c.stage[f"up{layer}{half_}"]
        with dve.Fori(0, n // 2) as i:
            for u in range(2):
                dve.wait_ge(c.S[f"pair_free{u}"], i + s0 // 2 + 1)
                dve.tensor_tensor(col(c.yT, i * 2 + u), c.tmp[:, u, :], c.tmp[:, u, :], ALU.mult
                                  ).then_inc(c.S[f"hidden_ready{u}"], 1)
        add_layer(c, dve, f"dn{layer}{half_}")


def dense_phase(c):
    nc, S = c.nc, c.S
    b_qkv, t_qkv = c.stage["qkv"][1], c.stage["qkv"][0]
    with ExitStack() as ctx:
        block = ctx.enter_context(nc.Block())

        @block.sync
        def _(sp):
            sp_stream(c, sp, c.stage["out"][1] + SLOTS, c.stage["o"][1] - c.stage["out"][1])

        @block.tensor
        def _(pe):
            for u in range(2):
                pe.sem_inc(S[f"tile_summed{u}"], FIRST)
            pe_layer(c, pe, "out", c.yT)
            pe_norm(c, pe, 1)
            pe.wait_ge(S.h_ready, 2)
            pe_mlp(c, pe, 0)
            pe_norm(c, pe, 2)
            for part in range(2):
                pe.wait_ge(S.h_ready, 3 + part)
                with pe.Fori(0, KT // 4) as i:
                    for u in range(4):
                        pe_tile(c, pe, u % 2, i + (b_qkv + KT * part) // 4, [u], c.hT,
                                i * 2 + (t_qkv + KT * part + u) // 2)
                        if u:
                            pe_tile_norm(c, pe, (u - 1) % 2, i * 2 + (KT * part + u - 1) // 2, c.blk64)
                    pe_tile_norm(c, pe, 1, i * 2 + (KT * part + 3) // 2, c.blk64)
            with pe.Fori(0, KT // 4) as i:
                for u in range(4):
                    pe_tile(c, pe, u % 2, i + (b_qkv + 2 * KT) // 4, [u], c.hT, i * 2 + (t_qkv + 2 * KT + u) // 2)

        @block.scalar
        def _(act):
            for u in range(2):
                act.sem_inc(S[f"tile_rooted{u}"], FIRST)
            act_wait_added(c, act, "out")
            act_norm(c, act, 1)
            act_mlp(c, act, 0)
            act_wait_added(c, act, "dn01")
            act_norm(c, act, 2)

            for part in range(2):
                with act.Fori(0, KT // 4) as i:
                    for u in range(4):
                        ps = c.LN[u % 2][:, :, 0:HT]
                        act.wait_ge(S.block_done, i * 4 + b_qkv + KT * part + u + 1)
                        act_tile_square(c, act, u % 2, i * 2 + (KT * part + u) // 2, ps)
                        act.activation(halves(col(c.yT, i * 4 + KT * part + u)), ps, ACT.Copy
                                       ).then_inc(S[f"pair_free{u % 2}"], 1)
                        if u:
                            act_tile_root(c, act, (u - 1) % 2, i * 2 + (KT * part + u - 1) // 2, 64)
                    act_tile_root(c, act, 1, i * 2 + (KT * part + 3) // 2, 64)
            with act.Fori(0, KT // 2) as i:
                for u in range(2):
                    act.wait_ge(S.block_done, i * 2 + b_qkv + 2 * KT + u + 1)
                    act.activation(halves(col(c.vT, i * 2 + u)), c.LN[u][:, :, 0:HT], ACT.Copy
                                   ).then_inc(S[f"pair_free{u}"], 1)

        @block.vector
        def _(dve):
            for u in range(2):
                dve.sem_inc(S[f"hidden_ready{u}"], FIRST)
                dve.sem_inc(S[f"tile_normed{u}"], FIRST)
            add_layer(c, dve, "out")
            dve_norm(c, dve, 1, G_MA)
            dve_mlp(c, dve, 0)
            dve_norm(c, dve, 2, G_B)
            for part in range(2):
                with dve.Fori(0, KT // 2) as i:
                    for u in range(2):
                        dve_tile_norm(c, dve, u, i + KT // 2 * part, col(c.yT, i * 2 + KT * part + u), c.par[:, G_QN - part:G_QN - part + 1])
                if part == 0:
                    dve_scale(c, dve, G_KV)


def attention_phase(c):
    nc, S = c.nc, c.S
    A, Bp, cst, par, ident, ones = c.A, c.Bp, c.cst, c.par, c.ident, c.ones
    turned, heads_out = c.LN[0][:, 0, :], c.LN[0][:, 1, :]
    keyed, weighed = c.LN[1][:, 0, :], c.LN[1][:, 1, :]
    NB = SEQ // P
    with ExitStack() as ctx:
        def sb(name, *shape):
            return ctx.enter_context(nc.sbuf_tensor(name, list(shape), F32))

        kp = sb("kpage", P, PAGES, NH, P)
        vp = sb("vpage", P, PAGES, NH, P)
        vs = sb("vhead", P, SEQ)
        vtok = sb("vtok", P, NB, P)
        pr = [sb("probs0", P, 2, SEQ - P), sb("probs1", P, 2, SEQ)]
        qst = [sb(f"qsample{n}", P, NH, 32) for n in range(2)]
        spr = sb("sprobs", P, PAST)
        sn = sb("snew", P, NS)
        cmb = sb("cmb", P, 32)
        aTs = sb("saT", P, (PAGES + 1) * 32)
        osb = sb("osb", P, 2 * P)
        vn = sb("vnew", NS, NH, P)
        mx = sb("mx", P, NB, 2)
        nm = sb("nm", P, NB, 2)
        sm = sb("sm", P, NB, 2)
        smx = sb("smx", P, 2)
        snm = sb("snm", P, 1)
        ssm = sb("ssm", P, 2)
        sden = sb("sden", P, 1)
        cf = sb("cf", P, 1)
        lam2 = sb("lam2", 64, 2)
        le = sb("le", P, 2)
        nlam = sb("nlam", P, 1)
        qz = [c.tmp, sb("qhead1", P, 2, T)]
        aT = c.rn
        block = ctx.enter_context(nc.Block())

        def turns(eng, turn):
            with eng.Fori(0, NH // 2) as i:
                turn(i * 2, 0)
                turn(i * 2 + 1, 1)

        @block.sync
        def _(sp):
            sp.dma_start(c.k_o, c.yT[:, KT:2 * KT, :]).then_inc(S.stored, 16)
            sp.dma_start(c.v_o, c.vT[:]).then_inc(S.stored, 16)
            sp.wait_ge(S.table_loaded, 16)

            def load(b, first):
                pages = [sp.value_load(c.pt[0:1, bass.ds(b * PAGES + p, 1)], min_val=0, max_val=c.n_pool - 1)
                         for p in range(PAGES)]
                for p, page in enumerate(pages):
                    if not first:
                        sp.wait_ge(S.keys_used, b * 2 + (p // 4 - 1))
                    sp.dma_start(kp[:, p].rearrange("p h x -> p (h x)"),
                                 c.ck_d[bass.ds(page, 1)].rearrange("a p x -> (a p) x")).then_inc(S[f"kpage{p}"], 16)
                for p, page in enumerate(pages):
                    if not first:
                        sp.wait_ge(S.vpage_used, b * PAGES + (p + 1 - PAGES))
                    sp.dma_start(vp[:, p].rearrange("p h x -> p (h x)"),
                                 c.cv_d[bass.ds(page, 1)].rearrange("a p x -> (a p) x")).then_inc(S[f"vpage{p}"], 16)

            load(0, True)
            with sp.Fori(1, DB) as b:
                load(b, False)

        @block.tensor
        def _(pe):
            for first in (S.block_weighed, S.v_turned, S.samples_scored):
                pe.sem_inc(first, FIRST)
            for first in (S.scores_ready0, S.scores_ready1):
                pe.sem_inc(first, FIRST)
            for h in range(NH):
                mm = pe.transpose(c.LN[0][0:NS, h // 4, (h % 4) * P:(h % 4 + 1) * P], c.vT[:, h, SEQ:T], ident)
            pe.matmul(weighed[:, 0:2 * P], ident, cst[:, 0:2 * P], start=True, stop=True)
            mm = pe.transpose(c.LN[0][0:NS, 1, 3 * P:4 * P], c.vT[:, NH - 1, SEQ:T], ident)
            mm.then_inc(S.vnew_turned, 1)
            pe.wait_ge(S.lam_products, 1)
            pe.matmul(A[:, 0, 0:2], ones[0:64, :], lam2[:], start=True, stop=True).then_inc(S.lam_summed, 1)
            pe.wait_ge(S.vnew_kept, 1)
            pe.wait_ge(S.lam_ready, 1)

            def turn(j, par_):
                q_ = qz[par_]

                def scores(i):
                    w = (i + 1) * P
                    pe.wait_ge(S.exps_done, j * NB + i + FIRST)
                    for cc in range(2):
                        k = c.yT[:, bass.ds(j + KT, 1), 0:w].rearrange("p a x -> p (a x)")
                        pe.matmul(A[:, cc, 0:w], q_[:, cc, i * P:(i + 1) * P], k, start=True, stop=False)
                        mm = pe.matmul(A[:, cc, w - P:w], ident, cst[:, C_NEG:C_NEG + P], start=False, stop=True)
                    mm.then_inc(S[f"scores_ready{par_}"], 1)

                def weigh(i):
                    pe.wait_ge(S.weights_ready, j * NB + i + 1)
                    for k in range(i + 1):
                        mm = pe.transpose(turned[:, k * P:(k + 1) * P], pr[i % 2][:, 0, k * P:(k + 1) * P], ident)
                    mm.then_inc(S.weights_turned, 1)
                    pe.wait_ge(S.weights_kept, j * NB + i + 1)
                    for k in range(i + 1):
                        mm = pe.matmul(heads_out[:, i * P:(i + 1) * P], vtok[:, k, :], aT[:, k * P:(k + 1) * P],
                                       start=(k == 0), stop=(k == i))
                    mm.then_inc(S.block_weighed, 1)

                def sample_scores():
                    q = qst[par_]
                    for half_ in range(2):
                        for p in range(4 * half_, 4 * half_ + 4):
                            pe.wait_ge(S[f"kpage{p}"], j * 16 + 16)
                        for hh in range(2):
                            for t in range(4):
                                mm = pe.matmul(Bp[32 * t:32 * t + 32, half_, :], q[:, 4 * hh + t, :],
                                               kp[:, 4 * half_:4 * half_ + 4, 4 * hh + t, :],
                                               start=(hh == 0), stop=(hh == 1))
                        mm.then_inc(S.keys_used, 1)
                    for hh in range(2):
                        for t in range(4):
                            mm = pe.matmul(keyed[32 * t:32 * t + 32, 0:NS], q[:, 4 * hh + t, :],
                                           c.yT[:, KT + 4 * hh + t, SEQ:T], start=(hh == 0), stop=(hh == 1))
                    mm.then_inc(S.samples_scored, 1)

                def sample_turn():
                    pe.wait_ge(S.cmb_ready, j + 1)
                    for p in range(PAGES):
                        pe.matmul(keyed[:, p * 32:(p + 1) * 32], spr[:, p * P:(p + 1) * P], cmb[:], start=True, stop=True)
                    pe.matmul(keyed[0:NS, PAGES * 32:(PAGES + 1) * 32], sn[:], cmb[:], start=True, stop=True
                              ).then_inc(S.sweights_turned, 1)

                def sample_weigh():
                    pe.wait_ge(S.sweights_kept, j + 1)
                    pe.wait_ge(S.sample_out, j + FIRST)
                    for p in range(PAGES):
                        pe.wait_ge(S[f"vpage{p}"], j * 16 + 16)
                        for hh in range(2):
                            for t in range(4):
                                mm = pe.matmul(weighed[32 * t:32 * t + 8, hh * P:(hh + 1) * P],
                                               aTs[:, p * 32 + 8 * t:p * 32 + 8 * t + 8], vp[:, p, 4 * hh + t, :],
                                               start=(p == 0 and hh == 0), stop=False, skip_group_check=True)
                        mm.then_inc(S.vpage_used, 1)
                    for hh in range(2):
                        for t in range(4):
                            mm = pe.matmul(weighed[32 * t:32 * t + 8, hh * P:(hh + 1) * P],
                                           aTs[0:NS, PAGES * 32 + 8 * t:PAGES * 32 + 8 * t + 8], vn[:, 4 * hh + t, :],
                                           start=False, stop=True, skip_group_check=True)
                    mm.then_inc(S.sample_weighed, 1)

                def sample_back():
                    pe.wait_ge(S.sample_kept_out, j + 1)
                    for hh in range(2):
                        mm = pe.transpose(weighed[:, (2 + hh) * P:(3 + hh) * P], osb[:, hh * P:(hh + 1) * P], ident)
                    mm.then_inc(S.sample_back, 1)

                pe.wait_ge(S.head_copied, j + 1 + FIRST)
                for k in range(NB):
                    mm = pe.transpose(turned[:, k * P:(k + 1) * P], vs[:, k * P:(k + 1) * P], ident)
                mm.then_inc(S.v_turned, 1)
                scores(0)
                sample_scores()
                scores(1)
                pe.wait_ge(S.v_kept, j + 1)
                pe.wait_ge(S.head_out, j + FIRST)
                weigh(0)
                scores(2)
                sample_turn()
                weigh(1)
                scores(3)
                sample_weigh()
                weigh(2)
                sample_back()
                weigh(3)

            turns(pe, turn)

        @block.scalar
        def _(act):
            act.sem_inc(S.exps_done, FIRST)
            act.sem_inc(S.head_out, FIRST)
            act.wait_ge(S.vnew_turned, 1)
            act.activation(vn[:].rearrange("p (a h) x -> p a (h x)", a=2), c.LN[0][0:NS, :, :], ACT.Copy
                           ).then_inc(S.vnew_kept, 1)
            act.wait_ge(S.lam_summed, 1)
            act.activation(le[:], A[:, 0, 0:2], ACT.Exp).then_inc(S.lam_exps, 1)

            def turn(j, par_):
                def exps(i):
                    w = (i + 1) * P
                    act.wait_ge(S.negmax_ready, j * NB + i + 1)
                    if i >= 2:
                        act.wait_ge(S.weights_turned, j * NB + i - 1)
                    for cc in range(2):
                        ins = act.activation(pr[i % 2][:, cc, 0:w], A[:, cc, 0:w], ACT.Exp, bias=nm[:, i, cc:cc + 1],
                                             scale=SCALE, accum_out=sm[:, i, cc:cc + 1])
                    ins.then_inc(S.exps_done, 1)

                def keep_weights(i):
                    act.wait_ge(S.weights_turned, j * NB + i + 1)
                    act.wait_ge(S.block_weighed, j * NB + i + FIRST)
                    act.activation(aT[:, 0:(i + 1) * P], turned[:, 0:(i + 1) * P], ACT.Copy).then_inc(S.weights_kept, 1)

                act.wait_ge(S.v_turned, j + 1 + FIRST)
                act.activation(vtok[:].rearrange("p k x -> p (k x)"), turned, ACT.Copy).then_inc(S.v_kept, 1)
                exps(0)
                act.wait_ge(S.snegmax_ready, j + 1)
                act.activation(spr[:], Bp[:].rearrange("p a x -> p (a x)"), ACT.Exp, bias=snm[:], scale=SCALE,
                               accum_out=ssm[:, 0:1])
                act.activation(sn[:], sn[:], ACT.Exp, bias=snm[:], scale=SCALE, accum_out=ssm[:, 1:2]
                               ).then_inc(S.sexps_done, 1)
                exps(1)
                keep_weights(0)
                exps(2)
                act.wait_ge(S.sweights_turned, j + 1)
                act.activation(aTs[:, 0:PAGES * 32], keyed[:, 0:PAGES * 32], ACT.Copy)
                act.activation(aTs[0:NS, PAGES * 32:], keyed[0:NS, PAGES * 32:(PAGES + 1) * 32], ACT.Copy
                               ).then_inc(S.sweights_kept, 1)
                keep_weights(1)
                exps(3)
                keep_weights(2)
                keep_weights(3)
                act.wait_ge(S.block_weighed, j * NB + NB + FIRST)
                act.activation(c.hT[:, bass.ds(j, 1), 0:SEQ].rearrange("p a x -> p (a x)"), heads_out, ACT.Copy
                               ).then_inc(S.head_out, 1)

            turns(act, turn)

        @block.vector
        def _(dve):
            dve.sem_inc(S.sample_out, FIRST)
            lp = par[0:64, G_LAM:G_LAM + 4].rearrange("p (m two) -> p m two", two=2)
            dve.tensor_tensor(lam2[:], lp[:, :, 0], lp[:, :, 1], ALU.mult).then_inc(S.lam_products, 1)
            dve.tensor_scalar(c.gsub[:], par[:, G_SUB:G_SUB + 1], 1.0 - LAM_INIT, None, ALU.mult)
            dve.wait_ge(S.lam_exps, 1)
            dve.tensor_tensor(nlam[:], le[:, 1:2], le[:, 0:1], ALU.subtract).then_inc(S.lam_step, 1)
            dve.wait_ge(S.lam_step, 1)
            dve.tensor_scalar(nlam[:], nlam[:], -LAM_INIT, None, ALU.add).then_inc(S.lam_ready, 1)
            dve.wait_ge(S.lam_ready, 1)
            dve.scalar_tensor_tensor(out=cf[:], in0=cst[:, C_COMP + 1:C_COMP + 2], scalar=nlam[:, 0:1],
                                     in1=cst[:, C_COMP:C_COMP + 1], op0=ALU.mult, op1=ALU.add).then_inc(S.cf_ready, 1)
            dve.wait_ge(S.cf_ready, 1)

            def turn(j, par_):
                def maxima(i):
                    dve.wait_ge(S[f"scores_ready{par_}"], (j - par_) * (NB // 2) + i + 1 + FIRST)
                    dve.tensor_reduce(mx[:, i, :], A[:, :, 0:(i + 1) * P], AX.X, ALU.max).then_inc(S.max_ready, 1)
                    dve.wait_ge(S.max_ready, j * NB + i + 1)
                    dve.tensor_scalar(nm[:, i, :], mx[:, i, :], -SCALE, None, ALU.mult).then_inc(S.negmax_ready, 1)

                def combine(i):
                    w = (i + 1) * P
                    n = j * (3 * NB) + 3 * i
                    p_ = pr[i % 2]
                    dve.wait_ge(S.exps_done, j * NB + i + 1 + FIRST)
                    dve.reciprocal(sm[:, i, :], sm[:, i, :]).then_inc(S.combine_step, 1)
                    dve.wait_ge(S.combine_step, n + 1)
                    dve.tensor_scalar(sm[:, i, 1:2], sm[:, i, 1:2], nlam[:, 0:1], None, ALU.mult
                                      ).then_inc(S.combine_step, 1)
                    dve.tensor_scalar(p_[:, 0, 0:w], p_[:, 0, 0:w], sm[:, i, 0:1], None, ALU.mult
                                      ).then_inc(S.combine_step, 1)
                    dve.wait_ge(S.combine_step, n + 3)
                    dve.scalar_tensor_tensor(out=p_[:, 0, 0:w], in0=p_[:, 1, 0:w], scalar=sm[:, i, 1:2],
                                             in1=p_[:, 0, 0:w], op0=ALU.mult, op1=ALU.add).then_inc(S.weights_ready, 1)

                maxima(0)
                combine(0)
                dve.wait_ge(S.samples_scored, j + 1 + FIRST)
                dve.tensor_reduce(smx[:, 0:1], Bp[:].rearrange("p a x -> p (a x)"), AX.X, ALU.max)
                dve.tensor_tensor(sn[:], keyed[:, 0:NS],
                                  cst[:, C_NEWM:C_NEWM + DB * NS].rearrange("p (b x) -> p b x", b=DB)
                                  [:, bass.ds(j, 1), :].rearrange("p a x -> p (a x)"), ALU.add
                                  ).then_inc(S.new_masked, 1)
                dve.wait_ge(S.new_masked, j + 1)
                dve.tensor_reduce(smx[:, 1:2], sn[:], AX.X, ALU.max).then_inc(S.smax_ready, 1)
                dve.wait_ge(S.smax_ready, j + 1)
                dve.tensor_scalar(snm[:], smx[:, 0:1], smx[:, 1:2], -SCALE, ALU.max, ALU.mult
                                  ).then_inc(S.snegmax_ready, 1)
                maxima(1)
                dve.wait_ge(S.sexps_done, j + 1)
                dve.tensor_tensor(sden[:], ssm[:, 0:1], ssm[:, 1:2], ALU.add).then_inc(S.sample_step, 1)
                dve.wait_ge(S.sample_step, j * 2 + 1)
                dve.reciprocal(sden[:], sden[:]).then_inc(S.sample_step, 1)
                dve.wait_ge(S.sample_step, j * 2 + 2)
                dve.tensor_scalar(cmb[:], cst[:, C_PAT:C_PAT + 32], sden[:, 0:1], cf[:, 0:1], ALU.mult, ALU.mult
                                  ).then_inc(S.cmb_ready, 1)
                combine(1)
                maxima(2)
                combine(2)
                maxima(3)
                combine(3)
                dve.wait_ge(S.sample_weighed, j + 1)
                dve.tensor_copy(osb[:], weighed[:, 0:2 * P]).then_inc(S.sample_kept_out, 1)
                dve.wait_ge(S.sample_back, j + 1)
                for hh in range(2):
                    v = weighed[:, (2 + hh) * P:(3 + hh) * P].rearrange("p (t x) -> p t x", t=4)
                    ins = dve.tensor_copy(c.hT[:, 4 * hh:4 * hh + 4, bass.ds(j * DS + SEQ, DS)],
                                          v[:, :, 4 * hh:4 * hh + DS])
                ins.then_inc(S.sample_out, 1)

            turns(dve, turn)

        @block.gpsimd
        def _(pool):
            pool.sem_inc(S.head_copied, FIRST)
            for n in range(2):
                pool.memset(qz[n][:], 0.0)
                ins = pool.memset(qst[n][:], 0.0)
            ins.then_inc(S.zeroed, 1)
            pool.wait_ge(S.zeroed, 1)

            def turn(j, par_):
                pool.wait_ge(S[f"scores_ready{par_}"], (j - par_) * (NB // 2) + FIRST)
                if par_:
                    pool.wait_ge(S.samples_scored, j - 1 + FIRST)
                pool.wait_ge(S.head_copied, j + FIRST)
                for cc in range(2):
                    lo = 64 * cc
                    for hh in range(2):
                        pool.tensor_copy(qst[par_][lo:lo + 64, 4 * hh:4 * hh + 4, 8 * hh + 4 * cc:8 * hh + 4 * cc + DS],
                                         c.yT[lo:lo + 64, 4 * hh:4 * hh + 4, bass.ds(j * DS + SEQ, DS)])
                    ins = pool.tensor_copy(qz[par_][lo:lo + 64, cc, 0:SEQ],
                                           c.yT[lo:lo + 64, bass.ds(j, 1), 0:SEQ].rearrange("p a x -> p (a x)"))
                ins.then_inc(S.q_copied, 1)
                pool.wait_ge(S.q_copied, j + 1)
                pool.wait_ge(S.v_turned, j + FIRST)
                pool.tensor_copy(vs[:], c.vT[:, bass.ds(j, 1), 0:SEQ].rearrange("p a x -> p (a x)")
                                 ).then_inc(S.head_copied, 1)

            turns(pool, turn)


def last_phase(c, blocks):
    nc, S = c.nc, c.S
    n0 = KT
    with ExitStack() as ctx:
        block = ctx.enter_context(nc.Block())

        @block.sync
        def _(sp):
            b0 = c.stage["o"][1] + SLOTS
            sp_stream(c, sp, b0, blocks - b0)
            for u in range(2):
                sp.wait_ge(S[f"pair_free{u}"], (c.stage["dn11"][0] + KT) // 2)
            sp.dma_start(c.y_o, c.xT[:]).then_inc(S.stored, 16)
            sp.wait_ge(S.stored, 64)
            sp.wait_ge(S.state_stored, 16 * GROUPS)
            sp.wait_ge(S.samples_stored, 16 * GROUPS)

        @block.tensor
        def _(pe):
            with pe.Fori(0, NH // 2) as i:
                for u in range(2):
                    pe_tile_norm(c, pe, u, i + n0, c.ones)
            for u in range(2):
                pe.wait_ge(S[f"tile_normed{u}"], n0 + NH // 2 + FIRST)
            pe_layer(c, pe, "o", c.hT)
            pe_norm(c, pe, 3)
            pe.wait_ge(S.h_ready, 5)
            pe_mlp(c, pe, 1)

        @block.scalar
        def _(act):
            with act.Fori(0, NH // 2) as i:
                for u in range(2):
                    act_tile_square(c, act, u, i + n0, halves(col(c.hT, i * 2 + u)))
                    act_tile_root(c, act, u, i + n0, P)
            act_wait_added(c, act, "o")
            act_norm(c, act, 3)
            act_mlp(c, act, 1)

        @block.vector
        def _(dve):
            with dve.Fori(0, NH // 2) as i:
                for u in range(2):
                    dve_tile_norm(c, dve, u, i + n0, col(c.hT, i * 2 + u), c.gsub[:, 0:1])
            add_layer(c, dve, "o")
            dve_norm(c, dve, 3, G_MB)
            dve_mlp(c, dve, 1)


OUTS = {
    "y_o": (P, KT, T), "nst_p": (GROUPS, P, R * HP), "nconv_o": (P, 32, 27), "k_o": (P, KT, T), "v_o": (P, KT, T),
    "nst_s": (GROUPS, P, DB * R * HP),
}


def build_program(nc, wblocks, wdt, xin, cst_d, par_d, hist_d, h0_d, ck_d, cv_d, pt_d,
                  y_o, nst_p, nconv_o, k_o, v_o, nst_s):
    with ExitStack() as ctx:
        c = Chip()
        c.nc, c.wblocks, c.wdt, c.xin, c.cst_d, c.par_d, c.hist_d, c.h0_d = nc, wblocks, wdt, xin, cst_d, par_d, hist_d, h0_d
        c.ck_d, c.cv_d, c.y_o, c.nst_p, c.nconv_o, c.k_o, c.v_o, c.nst_s = ck_d, cv_d, y_o, nst_p, nconv_o, k_o, v_o, nst_s
        c.n_pool = ck_d.shape[0]
        c.scr = nc.dram_tensor("decay_scratch", (32, T), F32, kind="Internal").ap()
        c.S = Sems(nc, ctx)
        c.stage, blocks = plan()

        def sb(name, shape, dt=F32):
            return ctx.enter_context(nc.sbuf_tensor(name, shape, dt))

        c.xT = sb("xT", [P, KT, T])
        c.hT = sb("hT", [P, KT, T])
        c.yT = sb("yT", [P, 2 * KT, T])
        c.ring = sb("ring", [P, SLOTS, D])
        c.cst = sb("cst", [P, C_W])
        c.par = sb("par", [P, G_W])
        c.tmp = sb("tmp", [P, 2, T])
        c.rn = sb("rn", [P, T])
        c.gsub = sb("gsub", [P, 1])
        c.pt = sb("pt", [1, DB * PAGES], I32)
        c.LN = [ctx.enter_context(nc.psum_tensor(f"LN{n}", [P, 2, 512], F32)) for n in range(2)]
        c.A = ctx.enter_context(nc.psum_tensor("A", [P, 2, 512], F32))
        c.Bp = ctx.enter_context(nc.psum_tensor("Bp", [P, 2, 512], F32))
        c.AB = [c.A, c.Bp]
        c.ident, c.ones = c.cst[:, C_ID:C_ID + P], c.cst[:, C_ONE:C_ONE + P]
        c.blk64, c.eps = c.cst[:, C_B64:C_B64 + P], c.cst[:, C_EPS:C_EPS + 1]
        c.pt_d = pt_d
        mixer_phase(c)
        with ExitStack() as mid:
            c.vT = mid.enter_context(nc.sbuf_tensor("vT", [P, KT, T], F32))
            with ExitStack() as dense:
                c.rq = dense.enter_context(nc.sbuf_tensor("rq", [P, 2, T], F32))
                dense_phase(c)
            attention_phase(c)
        with ExitStack() as end:
            c.rq = end.enter_context(nc.sbuf_tensor("rq2", [P, 2, T], F32))
            last_phase(c, blocks)


def feature_tiles(a):
    return a.reshape(-1, P).T


def weight_blocks(w):
    k, n = w.shape
    w = w.reshape(k // D, KT, P, n // P, P).transpose(3, 0, 2, 1, 4)
    return w.reshape(-1, P, KT * P)


def kernel(**inputs):
    import concourse.bacc as bacc
    from concourse.bass_utils import run_bass_kernel_spmd

    a = {k: np.asarray(v) for k, v in inputs.items()}
    DI = 2 * D
    w_in = a["w_in_a"][0]
    zc, xcols, bcols, ccols = 0, DI, 2 * DI, 2 * DI + D
    order, conv_order = [], []
    for g in range(GROUPS):
        conv = [xcols + 256 * g, xcols + 256 * g + P, bcols + P * g, ccols + P * g]
        order += conv + [zc + 256 * g, zc + 256 * g + P]
        conv_order += [o - DI for o in conv]
    cols = np.concatenate([np.arange(o, o + P) for o in order])
    ccol = np.concatenate([np.arange(o, o + P) for o in conv_order])
    up, dn = a["w_up"], a["w_down"]
    half = DF // 2
    parts = [weight_blocks(w_in[:, cols]), weight_blocks(a["w_out_a"][0])]
    mlps = []
    for layer in range(2):
        mlps.append([b for h in range(2) for b in (weight_blocks(up[layer][:, h * half:(h + 1) * half]),
                                                   weight_blocks(dn[layer][h * half:(h + 1) * half]))])
    parts += mlps[0] + [weight_blocks(a["w_q"][0]), weight_blocks(a["w_kv"]), weight_blocks(a["w_o"][0])] + mlps[1]
    wblocks = np.concatenate(parts)
    wdt = w_in[:, DI + 2 * DI:].reshape(KT, P, 32).transpose(1, 0, 2).reshape(P, KT * 32)

    x = np.concatenate([a["x_prompt"][0], a["x_sample"].reshape(NS, D)])
    xin = x.T.reshape(KT, P, T).transpose(1, 0, 2)

    par = np.zeros((P, G_W), np.float32)
    for at, v in ((G_A, a["norm_a"][0]), (G_MA, a["norm_m"][0]), (G_KV, a["kv_norm"]), (G_B, a["norm_b"][0]),
                  (G_MB, a["norm_m"][1])):
        par[:, at:at + KT] = feature_tiles(v)
    par[:, G_GN:G_GN + 16] = feature_tiles(a["gnorm_w"][0])
    par[:, G_DSK:G_DSK + 16] = feature_tiles(np.repeat(a["d_skip"][0], HP))
    par[:, G_CW:G_CW + P] = a["conv_w"][0][:, ccol].reshape(4, 32, P).transpose(2, 1, 0).reshape(P, P)
    par[:, G_CBI:G_CBI + 32] = a["conv_b"][0][ccol].reshape(32, P).T
    par[:, G_KN] = np.tile(a["k_norm"], 2)
    par[:, G_QN] = np.tile(a["q_norm"][0], 2)
    par[:, G_SUB] = a["subln"][0]
    par[:32, G_DTB] = a["dt_bias"][0]
    par[:32, G_ALOG] = a["a_log"][0]
    for n, k in enumerate(("lam_q1", "lam_k1", "lam_q2", "lam_k2")):
        par[:64, G_LAM + n] = a[k][0]

    hist = a["state_conv"][0][:, :, ccol].reshape(DB, 3, 32, P).transpose(3, 2, 0, 1).reshape(P, 32, 24)
    h0 = a["state_ssm"][0].reshape(DB, GROUPS, R * HP, P).transpose(1, 3, 0, 2).reshape(GROUPS, P, DB * R * HP)
    n_pool = a["cache_k"].shape[0]
    ck = a["cache_k"].reshape(n_pool, P, NH, P).transpose(0, 3, 2, 1).reshape(n_pool, P, NH * P)
    cv = a["cache_v"].reshape(n_pool, P, NH * P)

    arrays = {
        "wblocks": wblocks, "wdt": wdt, "xin": xin, "cst_d": constants(), "par_d": par, "hist_d": hist, "h0_d": h0,
        "ck_d": ck, "cv_d": cv, "pt_d": a["page_table"].reshape(1, DB * PAGES),
    }
    arrays = {k: np.ascontiguousarray(v) for k, v in arrays.items()}
    nc = bacc.Bacc("TRN2", target_bir_lowering=False, num_devices=1)
    aps = {k: nc.dram_tensor(k, v.shape, mybir.dt.from_np(v.dtype), kind="ExternalInput").ap()
           for k, v in arrays.items()}
    aps |= {k: nc.dram_tensor(k, s, F32, kind="ExternalOutput").ap() for k, s in OUTS.items()}
    build_program(nc, **aps)
    r = run_bass_kernel_spmd(nc, [arrays], core_ids=[0]).results[0]

    def tokens(o):
        t = o.transpose(2, 1, 0).reshape(T, D)
        return t[:SEQ], t[SEQ:].reshape(DB, DS, D)

    y_p, y_s = tokens(r["y_o"])
    k_p, k_s = tokens(r["k_o"])
    v_p, v_s = tokens(r["v_o"])
    ssm_p = r["nst_p"].transpose(0, 2, 1).reshape(1, 1, 32, HP, P)
    ssm_s = r["nst_s"].reshape(GROUPS, P, DB, R * HP).transpose(2, 0, 3, 1).reshape(1, DB, 32, HP, P)
    back = np.argsort(ccol)
    conv = r["nconv_o"].transpose(2, 1, 0).reshape(27, 32 * P)[:, back]
    return (
        y_p.reshape(1, SEQ, D), y_s, ssm_p, conv[:3].reshape(1, 1, 3, -1), k_p.reshape(1, SEQ, NH, 2, 64),
        v_p.reshape(1, SEQ, NH, P), ssm_s, conv[3:].reshape(DB, 3, -1)[None], k_s.reshape(DB, DS, NH, 2, 64),
        v_s.reshape(DB, DS, NH, P),
    )
```

```python
from contextlib import ExitStack

import numpy as np

import concourse.bass as bass
from concourse import mybir

F32 = mybir.dt.float32
F32R = mybir.dt.float32r
I32 = mybir.dt.int32
ACT = mybir.ActivationFunctionType
ALU = mybir.AluOpType
AX = mybir.AxisListType

P = 128
D = 1024
KT = D // P
SEQ = 512
DB, DS = 8, 4
NS = DB * DS
T = SEQ + NS
HT = T // 2
GROUPS = 8
R = 4
HP = 64
CH = SEQ // P
GT = 6
CT = 4
NH = 8
DF = 4096
FT = DF // P // 2
PAGES = 8
PAST = P * PAGES
SLOTS = 4
NEG = -1.0e30
SCALE = 64 ** -0.5
LAM_INIT = 0.8 - 0.6 * float(np.exp(-0.3))
EPS = 1e-6
CB = 3 + SEQ + DB * 7
FIRST = 1
CO = CB - 3

C_ID, C_ONE, C_B64, C_CAU, C_NEG, C_ELAST = (P * n for n in range(6))
C_SAMP = 6 * P
C_SELE = C_SAMP + NS
C_LAST = C_SELE + NS
C_BLK = C_LAST + DB
C_RST = C_BLK + DB
C_NEWM = C_RST + T
C_PAT = C_NEWM + DB * NS
C_COMP = C_PAT + 32
C_EPS = C_COMP + 2
C_W = C_EPS + 1

G_A, G_MA, G_KV, G_B, G_MB = (KT * n for n in range(5))
G_GN = 5 * KT
G_DSK = G_GN + 16
G_CW = G_DSK + 16
G_CBI = G_CW + 32 * 4
G_KN = G_CBI + 32
G_QN = G_KN + 1
G_SUB = G_QN + 1
G_DTB = G_SUB + 1
G_ALOG = G_DTB + 1
G_LAM = G_ALOG + 1
G_W = G_LAM + 4


def constants():
    c = np.zeros((P, C_W), np.float32)
    i = np.arange(P)
    c[:, C_ID:C_ID + P] = np.eye(P)
    c[:, C_ONE:C_ONE + P] = 1
    c[:, C_B64:C_B64 + P] = (i[:, None] // 64 == i[None] // 64)
    c[:, C_CAU:C_CAU + P] = (i[None] >= i[:, None])
    c[:, C_NEG:C_NEG + P] = np.where(i[None] > i[:, None], NEG, 0)
    c[P - 1, C_ELAST:C_ELAST + P] = 1
    s = np.arange(NS)
    same = s[:, None] // DS == s[None] // DS
    c[:NS, C_SAMP:C_SAMP + NS] = same & (s[None] >= s[:, None])
    c[:NS, C_SELE:C_SELE + NS] = s[:, None] == DS * (s[None] // DS) + DS - 1
    b = np.arange(DB)
    c[:NS, C_LAST:C_LAST + DB] = s[:, None] == DS * b[None] + DS - 1
    c[:NS, C_BLK:C_BLK + DB] = s[:, None] // DS == b[None]
    t = np.arange(T)
    c[:NS, C_RST:C_RST + T] = np.where(t < SEQ, t % P != 0, (t - SEQ) % DS != 0)
    q = i % DS
    ok = (s[None, None] // DS == b[None, :, None]) & (s[None, None] % DS <= q[:, None, None])
    c[:, C_NEWM:C_NEWM + DB * NS] = np.where(ok, 0, NEG).reshape(P, -1)
    used = i % 32 < 16
    column = 8 * (i // 32) + 4 * (i % 16 // 8) + q
    c[:, C_PAT:C_PAT + 32] = used[:, None] & (column[:, None] == np.arange(32)[None])
    c[:, C_COMP] = i // 4 % 2 == 0
    c[:, C_COMP + 1] = i // 4 % 2 == 1
    c[:, C_EPS] = EPS
    return c


class Sems:

    def __init__(self, nc, ctx):
        self.nc, self.ctx, self.made = nc, ctx, {}

    def __getattr__(self, name):
        return self[name]

    def __getitem__(self, name):
        if name not in self.made:
            self.made[name] = self.ctx.enter_context(self.nc.semaphore(name))
        return self.made[name]


class Chip:
    pass


def col(t, k):
    return t[:, bass.ds(k, 1), :].rearrange("p a x -> p (a x)")


def one(t, c):
    return t[:, bass.ds(c, 1)]


def halves(ap):
    return ap.rearrange("p (h t) -> p h t", h=2)


def plan():
    stage, tiles, blocks = {}, 0, 0
    for name, n, nb in [("in", GT * GROUPS, 1), ("out", KT, 2), ("up00", FT, 1), ("dn00", KT, 2), ("up01", FT, 1),
                        ("dn01", KT, 2), ("k", KT, 1), ("q", KT, 1), ("v", KT, 1), ("o", KT, 1), ("up10", FT, 1), ("dn10", KT, 2),
                        ("up11", FT, 1), ("dn11", KT, 2)]:
        stage[name] = (tiles, blocks, n, nb)
        tiles += n
        blocks += n * nb
    return stage, blocks


def split_buffers(nc, ctx, name, n, m):
    return [ctx.enter_context(nc.sbuf_tensor(f"{name}_{part}", [P, n, m], F32R)) for part in ("high", "low")]


def act_split(c, act, i, n):
    act.wait_ge(c.S[f"slot_loaded{n % SLOTS}"], i * 16 + 16 * (n // SLOTS + 1))
    act.wait_ge(c.S.block_done, i * SLOTS + n - 1)
    act.activation(c.Wh[:, n % 2, :], c.ring[:, n % SLOTS, :], ACT.Copy).then_inc(c.S.block_high, 1)


def dve_split(c, dve, i, n):
    dve.wait_ge(c.S.block_high, i * SLOTS + n + 1)
    dve.tensor_tensor(c.Wl[:, n % 2, :], c.ring[:, n % SLOTS, :], c.Wh[:, n % 2, :].bitcast(F32), ALU.subtract
                      ).then_inc(c.S.block_split, 1)


def sp_stream_split(c, sp, b0, n):
    with sp.Fori(b0 // SLOTS, (b0 + n) // SLOTS) as i:
        for u in range(SLOTS):
            sp.wait_ge(c.S.block_split, i * SLOTS + (u + 1 - SLOTS))
            sp.dma_start(c.ring[:, u, :], c.wblocks[bass.ds(i * SLOTS + u, 1)].rearrange("a p n -> (a p) n")
                         ).then_inc(c.S[f"slot_loaded{u}"], 16)


def pe_layer(c, pe, name, src, ready, after=None):
    t0, b0, n, nb = c.stage[name]
    per = SLOTS // nb
    high, low = src
    with pe.Fori(0, n // per) as i:
        for u in range(per):
            pe.wait_ge(c.S[f"pair_free{u % 2}"], i * (per // 2) + (t0 + u) // 2)
            for m in range(nb):
                s = u * nb + m
                pe.wait_ge(c.S.block_split, i * SLOTS + b0 + s + 1)
                for kk in range(KT):
                    k = m * KT + kk
                    if u == 0:
                        pe.wait_ge(*ready(k))
                    for p, (w, x) in enumerate(((c.Wh, high), (c.Wh, low), (c.Wl, high))):
                        for h in range(2):
                            mm = pe.matmul(c.LN[u % 2][:, h, 0:HT], w[:, s % 2, kk * P:(kk + 1) * P],
                                           x[:, k, h * HT:(h + 1) * HT], start=(k == 0 and p == 0),
                                           stop=(k == nb * KT - 1 and p == 2))
                mm.then_inc(c.S.block_done, 1)
            if after:
                after(i, u)


def split_turns(c, eng, name, split, step, ends):
    _, b0, n, nb = c.stage[name]
    turns = n * nb // SLOTS

    def turn(i, last):
        for u in range(SLOTS):
            if not (last and u == SLOTS - 1):
                split(c, eng, i, b0 + u + 1)
            if (u + 1) % nb == 0:
                step(i, u // nb)

    with eng.Fori(0, turns - 1 if ends else turns) as i:
        turn(i, False)
    if ends:
        turn(turns - 1, True)


def dve_add_layer(c, dve, name, ends=False):
    _, b0, _, nb = c.stage[name]
    per = SLOTS // nb

    def step(i, u):
        dve.wait_ge(c.S.block_done, i * SLOTS + b0 + (u + 1) * nb)
        x = halves(col(c.xT, i * per + u))
        dve.tensor_tensor(x, x, c.LN[u % 2][:, :, 0:HT], ALU.add).then_inc(c.S[f"pair_free{u % 2}"], 1)

    split_turns(c, dve, name, dve_split, step, ends)


def act_idle_layer(c, act, name, ends=False):
    split_turns(c, act, name, act_split, lambda i, u: None, ends)


def act_wait_added(c, act, name):
    t0, _, n, _ = c.stage[name]
    for u in range(2):
        act.wait_ge(c.S[f"pair_free{u}"], (t0 + n) // 2)


def act_norm(c, act, n):
    for k in range(KT):
        if k >= 2 or n:
            act.wait_ge(c.S.square_summed, n * KT + k - 1)
        act.activation(c.tmp[:, k % 2, :], c.xT[:, k, :], ACT.Square).then_inc(c.S.squared, 1)
    act.wait_ge(c.S.square_summed, (n + 1) * KT)
    act.activation(halves(c.rn[:]), c.A[:, :, 0:HT], ACT.Ln, bias=c.eps, scale=1.0 / D).then_inc(c.S.mean_logged, 1)
    act.wait_ge(c.S.mean_logged, n + 1)
    act.activation(c.rn[:], c.rn[:], ACT.Exp, scale=-0.5).then_inc(c.S.inverted, 1)


def pe_norm(c, pe, n):
    for k in range(KT):
        pe.wait_ge(c.S.squared, n * KT + k + 1)
        for h in range(2):
            mm = pe.matmul(c.A[:, h, 0:HT], c.ones, c.tmp[:, k % 2, h * HT:(h + 1) * HT],
                           start=(k == 0), stop=(k == KT - 1))
        mm.then_inc(c.S.square_summed, 1)


def dve_scale(c, dve, first, gains):
    def full(k):
        if k >= 2 or first:
            dve.wait_ge(c.S.tile_split, first + k - 1)
        dve.scalar_tensor_tensor(out=c.full[:, k % 2, :], in0=c.xT[:, k, :], scalar=c.par[:, gains + k:gains + k + 1],
                                 in1=c.rn[:], op0=ALU.mult, op1=ALU.mult).then_inc(c.S.tile_scaled, 1)

    full(0)
    for k in range(KT):
        if k + 1 < KT:
            full(k + 1)
        dve.wait_ge(c.S.tile_high, first + k + 1)
        dve.tensor_tensor(c.Hl[:, k, :], c.full[:, k % 2, :], c.Hh[:, k, :].bitcast(F32), ALU.subtract
                          ).then_inc(c.S.tile_split, 1)


def act_scale(c, act, first):
    for k in range(KT):
        act.wait_ge(c.S.tile_scaled, first + k + 1)
        act.activation(c.Hh[:, k, :], c.full[:, k % 2, :], ACT.Copy).then_inc(c.S.tile_high, 1)


def pe_tile_norm(c, pe, u, n, weights):
    pe.wait_ge(c.S[f"tile_squared{u}"], n + 1)
    pe.wait_ge(c.S[f"tile_logged{u}"], n + FIRST)
    for h in range(2):
        mm = pe.matmul(c.AB[u][:, h, 0:HT], weights, c.tmp[:, u, h * HT:(h + 1) * HT], start=True, stop=True)
    mm.then_inc(c.S[f"tile_summed{u}"], 1)


def act_tile_square(c, act, u, n, src):
    act.wait_ge(c.S[f"tile_summed{u}"], n + FIRST)
    act.activation(halves(c.tmp[:, u, :]), src, ACT.Square).then_inc(c.S[f"tile_squared{u}"], 1)


def act_tile_invert(c, act, u, n, width):
    act.wait_ge(c.S[f"tile_summed{u}"], n + 1 + FIRST)
    act.wait_ge(c.S[f"tile_normed{u}"], n + FIRST)
    act.activation(halves(c.rq[:, u, :]), c.AB[u][:, :, 0:HT], ACT.Ln, bias=c.eps, scale=1.0 / width
                   ).then_inc(c.S[f"tile_logged{u}"], 1)
    act.wait_ge(c.S[f"tile_logged{u}"], n + 1 + FIRST)
    act.activation(c.rq[:, u, :], c.rq[:, u, :], ACT.Exp, scale=-0.5).then_inc(c.S[f"tile_inverted{u}"], 1)


def dve_tile_norm(c, dve, u, n, tile, gain):
    dve.wait_ge(c.S[f"tile_inverted{u}"], n + 1)
    dve.scalar_tensor_tensor(out=tile, in0=tile, scalar=gain, in1=c.rq[:, u, :],
                             op0=ALU.mult, op1=ALU.mult).then_inc(c.S[f"tile_normed{u}"], 1)


def pe_mlp(c, pe, layer, first):
    for half_ in range(2):
        pe_layer(c, pe, f"up{layer}{half_}", (c.Hh, c.Hl), lambda k: (c.S.tile_split, first + k + 1))
        n0 = FT // 2 * (2 * layer + half_) + FIRST
        pe_layer(c, pe, f"dn{layer}{half_}", (c.Yh, c.Yl), lambda k: (c.S[f"hidden_split{k % 2}"], n0 + k // 2 + 1))


def act_mlp(c, act, layer):
    for half_ in range(2):
        name = f"up{layer}{half_}"
        t0, b0, _, _ = c.stage[name]
        n0 = FT // 2 * (2 * layer + half_) + FIRST

        def step(i, u):
            v = u % 2
            act.wait_ge(c.S.block_done, i * SLOTS + b0 + u + 1)
            act.wait_ge(c.S[f"hidden_split{v}"], i * 2 + u // 2 + n0)
            act.activation(halves(c.tmp[:, v, :]), c.LN[v][:, :, 0:HT], ACT.Relu).then_inc(c.S[f"pair_free{v}"], 1)
            act.wait_ge(c.S[f"pair_free{v}"], i * 2 + (t0 + u) // 2 + 1)
            act.activation(col(c.Yh, i * 4 + u), c.tmp[:, v, :], ACT.Square).then_inc(c.S[f"hidden_high{v}"], 1)

        split_turns(c, act, name, act_split, step, False)
        act_idle_layer(c, act, f"dn{layer}{half_}", ends=(half_ == 1))


def dve_mlp(c, dve, layer):
    for half_ in range(2):
        name = f"up{layer}{half_}"
        t0, _, _, _ = c.stage[name]
        n0 = FT // 2 * (2 * layer + half_)

        def step(i, u):
            v = u % 2
            dve.wait_ge(c.S[f"pair_free{v}"], i * 2 + (t0 + u) // 2 + 1)
            dve.wait_ge(c.S[f"hidden_split{v}"], i * 2 + u // 2 + n0 + FIRST)
            dve.tensor_tensor(c.full[:, v, :], c.tmp[:, v, :], c.tmp[:, v, :], ALU.mult
                              ).then_inc(c.S[f"hidden_full{v}"], 1)
            dve.wait_ge(c.S[f"hidden_full{v}"], i * 2 + u // 2 + n0 + 1)
            dve.wait_ge(c.S[f"hidden_high{v}"], i * 2 + u // 2 + n0 + 1)
            dve.tensor_tensor(col(c.Yl, i * 4 + u), c.full[:, v, :], col(c.Yh, i * 4 + u).bitcast(F32), ALU.subtract
                              ).then_inc(c.S[f"hidden_split{v}"], 1)

        split_turns(c, dve, name, dve_split, step, False)
        dve_add_layer(c, dve, f"dn{layer}{half_}", ends=(half_ == 1))


def mixer_phase(c):
    nc, S = c.nc, c.S
    with ExitStack() as ctx:
        arena = ctx.enter_context(nc.sbuf_tensor("mixer_arena", [P, 20384], F32))
        top = [0]

        def carve(*shape, at=None):
            n = int(np.prod(shape))
            lo = top[0] if at is None else at
            if at is None:
                top[0] += n
                assert top[0] <= 20384, top[0]
            v = arena[:, lo:lo + n]
            if len(shape) > 1:
                names = "abcd"[:len(shape)]
                v = v.rearrange(f"p ({' '.join(names)}) -> p {' '.join(names)}", **dict(zip(names, shape)))
            return v

        cb = carve(2, CB)
        acc = carve(CO)
        xc = carve(2, CT, T)
        sz = carve(2, T)
        dt_at = top[0]
        M = carve(R, SEQ)
        Ms = carve(R, NS)
        ea = carve(R, T)
        abc = ea
        xdt = carve(CH + 1, R * HP)
        xw = carve(CH + 1, R * HP)
        Btok = carve(CH, P)
        Bm = carve(DB, P)
        CBm = carve(CH, P)
        CBs = carve(NS)
        hst = carve(CH, R * HP)
        h0 = carve(DB, R * HP)
        yt = carve(2, T)
        yoff = carve(2, NS)
        dtf = carve(4, T, at=dt_at)[0:32]
        dtw = ctx.enter_context(nc.sbuf_tensor("dtw", [P, KT * 32], F32))
        dtwh, dtwl = split_buffers(nc, ctx, "dtw", 1, KT * 32)
        Wh, Wl = split_buffers(nc, ctx, "W0", 2, D)
        hh, hl = split_buffers(nc, ctx, "H0", KT, T)
        dtt = ctx.enter_context(nc.sbuf_tensor("dtt", [P, CH + 1, 32], F32))
        acst = ctx.enter_context(nc.sbuf_tensor("acst", [P, CH + 1, 32], F32))
        xws = ctx.enter_context(nc.sbuf_tensor("xws", [P, CH + 1, 32], F32))
        cdec = ctx.enter_context(nc.sbuf_tensor("cdec", [P, CH, 32], F32))
        sdec = ctx.enter_context(nc.sbuf_tensor("sdec", [P, DB, 32], F32))
        zl = ctx.enter_context(nc.sbuf_tensor("zl", [NS, DB, 32], F32))
        hist = ctx.enter_context(nc.sbuf_tensor("hist", [P, 32, 24], F32))
        ncv = ctx.enter_context(nc.sbuf_tensor("ncv", [P, 32, 27], F32))
        nega = ctx.enter_context(nc.sbuf_tensor("nega", [32, 1], F32))
        A, Bp, LN, cst, par = c.A, c.Bp, c.LN, c.cst, c.par
        ident, ones = c.ident, c.ones

        def heads(t, n0, n1, i, s, rows=P):
            return t[0:rows, n0:n1, bass.ds(i * (2 * R) + s * R, R)]

        def head(t, n, i, s, r):
            return t[:, n, bass.ds(i * (2 * R) + (s * R + r), 1)]

        def over(ap, n):
            return ap.unsqueeze(len(ap.shape)).to_broadcast(list(ap.shape) + [n])

        block = ctx.enter_context(nc.Block())

        def split_high(act, i, n):
            act.wait_ge(S[f"slot_loaded{n % SLOTS}"], i * 48 + 16 * (n // SLOTS + 1))
            if n >= 2:
                act.wait_ge(S.block_done, i * (2 * GT) + n - 1)
            act.activation(Wh[:, n % 2, :], c.ring[:, n % SLOTS, :], ACT.Copy).then_inc(S.block_high, 1)

        def split_low(dve, i, n):
            dve.wait_ge(S.block_high, i * (2 * GT) + n + 1)
            dve.tensor_tensor(Wl[:, n % 2, :], c.ring[:, n % SLOTS, :], Wh[:, n % 2, :].bitcast(F32), ALU.subtract
                              ).then_inc(S.block_split, 1)

        def steps(eng, step):
            with eng.Fori(0, GROUPS // 2 - 1) as i:
                step(i, 0)
                step(i, 1)
            step(0, GROUPS - 2)
            step(0, GROUPS - 1)

        @block.sync
        def _(sp):
            sp.dma_start(c.cst[:], c.cst_d).then_inc(S.const_loaded, 16)
            sp.dma_start(c.xT, c.xin).then_inc(S.x_loaded, 16)
            sp.dma_start(c.par[:], c.par_d).then_inc(S.par_loaded, 16)
            sp.dma_start(dtw[:], c.wdt).then_inc(S.dtw_loaded, 16)
            sp.dma_start(c.pt[:], c.pt_d).then_inc(S.table_loaded, 16)
            for u in range(SLOTS):
                sp.dma_start(c.ring[:, u, :], c.wblocks[u]).then_inc(S[f"slot_loaded{u}"], 16)
            sp.dma_start(hist[:], c.hist_d).then_inc(S.hist_loaded, 16)
            sp_stream_split(c, sp, SLOTS, GT * GROUPS)
            sp.wait_ge(S.history_out, 4 * GROUPS)
            sp.dma_start(c.nconv_o, ncv[:]).then_inc(S.stored, 16)

        @block.tensor
        def _(pe):
            def tile(i, s, u):
                n = GT * s + u
                if n >= 2 or not isinstance(i, int):
                    pe.wait_ge(S[f"pair_free{u % 2}"], i * GT + n // 2)
                pe.wait_ge(S.block_split, i * (2 * GT) + n + 1)
                for k in range(KT):
                    for p, (w, x) in enumerate(((Wh[:, n % 2], hh), (Wh[:, n % 2], hl), (Wl[:, n % 2], hh))):
                        for h in range(2):
                            mm = pe.matmul(LN[u % 2][:, h, 0:HT], w[:, k * P:(k + 1) * P], x[:, k, h * HT:(h + 1) * HT],
                                           start=(k == 0 and p == 0), stop=(k == KT - 1 and p == 2))
                mm.then_inc(S.block_done, 1)

            pe.wait_ge(S.const_loaded, 16)
            pe_norm(c, pe, 0)
            pe.wait_ge(S.dtw_split, 1)
            for k in range(KT):
                pe.wait_ge(S.input_split, k + 1)
                for p, (w, x) in enumerate(((dtwh, hh), (dtwh, hl), (dtwl, hh))):
                    for h in range(2):
                        mm = pe.matmul(Bp[0:32, h, 0:HT], w[:, 0, k * 32:(k + 1) * 32], x[:, k, h * HT:(h + 1) * HT],
                                       start=(k == 0 and p == 0), stop=(k == KT - 1 and p == 2))
            mm.then_inc(S.dt_projected, 1)
            for u in range(2):
                tile(0, 0, u)
            pe.wait_ge(S.decay_summed, 1)
            for n in range(CH + 1):
                m = P if n < CH else NS
                pe.transpose(A[0:m, 0, n * 32:(n + 1) * 32], dtf[:, 1, n * P:n * P + m], ident[0:32, 0:32])
                mm = pe.transpose(A[0:m, 1, n * 32:(n + 1) * 32], dtf[:, 2, n * P:n * P + m], ident[0:32, 0:32])
            mm.then_inc(S.dt_turned, 1)
            pe.wait_ge(S.dt_kept, 2)
            pe.matmul(Bp[:, 0, 0:CH * 32], cst[:, C_ELAST:C_ELAST + P], acst[:, 0:CH, :].rearrange("p c h -> p (c h)"),
                      start=True, stop=True)
            pe.matmul(Bp[0:NS, 0, 128:160], cst[0:NS, C_SELE:C_SELE + NS], acst[0:NS, CH, :], start=True, stop=True)
            pe.wait_ge(S.last_kept, 1)
            pe.matmul(Bp[:, 1, 0:DB * 32], ones[0:NS, :], zl[:].rearrange("p b h -> p (b h)"),
                      start=True, stop=True).then_inc(S.ends_ready, 1)
            for u in range(2, GT - 1):
                tile(0, 0, u)

            def step(i, s):
                par_ = s % 2
                g1 = i * 2 + (s + 1)
                X = xc[:, par_]
                pe.wait_ge(S.conv_done, i * 8 + 4 * s + 4)
                pe.wait_ge(S.group_done, i * 2 + s + FIRST)
                if s == 0:
                    pe.wait_ge(S.dt_scaled, 1)
                for n in range(CH):
                    for j in range(2):
                        mm = pe.transpose(A[:, n // 2, (n % 2) * 256 + j * P:(n % 2) * 256 + (j + 1) * P],
                                          X[:, j, n * P:(n + 1) * P], ident)
                mm.then_inc(S.x_turned, 1)
                for n in range(CH):
                    mm = pe.transpose(Bp[:, 0, n * P:(n + 1) * P], X[:, 2, n * P:(n + 1) * P], ident)
                mm.then_inc(S.b_turned, 1)
                for n in range(CH):
                    mm = pe.matmul(Bp[:, 1, n * P:(n + 1) * P], X[:, 2, n * P:(n + 1) * P], X[:, 3, n * P:(n + 1) * P],
                                   start=True, stop=True)
                mm.then_inc(S.cb_ready, 1)
                tile(i, s, 5)
                pe.wait_ge(S.x_scaled, g1)
                for j in range(2):
                    pe.transpose(A[0:NS, 0, j * P:(j + 1) * P], X[:, j, SEQ:T], ident)
                pe.transpose(A[0:NS, 1, 0:P], X[:, 2, SEQ:T], ident)
                pe.matmul(A[0:NS, 1, P:P + NS], X[:, 2, SEQ:T], X[:, 3, SEQ:T], start=True, stop=True)
                pe.wait_ge(S.h0_loaded, i * 32 + 16 * (s + 1))
                for b in range(DB):
                    for j in range(2):
                        lo = 192 + j * NS + DS * b
                        mm = pe.matmul(A[:, 1, lo:lo + DS], h0[:, b, j * P:(j + 1) * P],
                                       X[:, 3, SEQ + DS * b:SEQ + DS * (b + 1)], start=True, stop=True)
                mm.then_inc(S.sample_ready, 1)
                last = s == GROUPS - 1
                if not last:
                    tile(i, s + 1, 0)
                pe.wait_ge(S.b_kept, g1)
                pe.wait_ge(S.sample_kept, g1)
                for n in range(CH):
                    mm = pe.matmul(A[:, n // 2, (n % 2) * 256:(n % 2) * 256 + 256], Btok[:, n, :], xw[:, n, :],
                                   start=True, stop=True)
                mm.then_inc(S.states_ready, 1)

                def update(q):
                    for b in range(4 * q, 4 * q + 4):
                        mm = pe.matmul(Bp[:, (b // 2) % 2, (b % 2) * 256:(b % 2) * 256 + 256], Bm[0:NS, b, :],
                                       xw[0:NS, CH, :], start=True, stop=True)
                    mm.then_inc(S.update_ready, 1)

                update(0)
                if not last:
                    tile(i, s + 1, 1)
                pe.wait_ge(S.states_kept, g1)
                for j in range(2):
                    for n in range(CH):
                        for r in (2 * j, 2 * j + 1):
                            out = A[64 * (r % 2):64 * (r % 2) + 64, j, n * P:(n + 1) * P]
                            mm = pe.matmul(out, xdt[:, n, r * HP:(r + 1) * HP], M[:, r, n * P:(n + 1) * P],
                                           start=True, stop=(n == 0))
                            if n:
                                mm = pe.matmul(out, hst[:, n - 1, r * HP:(r + 1) * HP],
                                               ea[:, r, n * P:(n + 1) * P], start=False, stop=True)
                mm.then_inc(S.y_ready, 1)
                pe.wait_ge(S.state_added, i * 4 + 2 * s + 1)
                update(1)
                if not last:
                    tile(i, s + 1, 2)
                pe.wait_ge(S.state_added, i * 4 + 2 * s + 2)
                for r in range(R):
                    mm = pe.matmul(Bp[64 * (r % 2):64 * (r % 2) + 64, 0, (r // 2) * NS:(r // 2 + 1) * NS],
                                   xdt[0:NS, CH, r * HP:(r + 1) * HP], Ms[0:NS, r, :], start=True, stop=True)
                mm.then_inc(S.ys_ready, 1)
                if not last:
                    tile(i, s + 1, 3)
                pe.wait_ge(S.y_squared, g1)
                for j in range(2):
                    for h in range(2):
                        mm = pe.matmul(A[:, h, 0:HT], ones, c.tmp[:, j, h * HT:(h + 1) * HT],
                                       start=(j == 0), stop=(j == 1))
                mm.then_inc(S.y_summed, 1)
                if not last:
                    tile(i, s + 1, 4)

            steps(pe, step)

        @block.scalar
        def _(act):
            def tile(i, s, u):
                take(i, s, u)
                if GT * s + u + 2 < GT * GROUPS:
                    split_high(act, i, GT * s + u + 2)

            def take(i, s, u):
                act.wait_ge(S.block_done, i * (2 * GT) + GT * s + u + 1)
                ps = LN[u % 2]
                if u >= CT:
                    if u == CT and s:
                        act.wait_ge(S.gated, i * 2 + s)
                    act.activation(halves(sz[:, u - CT, :]), ps[:, :, 0:HT], ACT.Silu
                                   ).then_inc(S[f"pair_free{u % 2}"], 1)
                    return
                n = CT * s + u
                act.wait_ge(S.history_in, i * 8 + n + 1)
                b = cb[:, u % 2, :]
                act.activation(b[:, 3:3 + HT], ps[:, 0, 0:HT], ACT.Copy)
                act.activation(b[:, 3 + HT:3 + SEQ], ps[:, 1, 0:SEQ - HT], ACT.Copy)
                act.activation(b[:, 3 + SEQ:].rearrange("p (b t) -> p b t", t=7)[:, :, 3:7],
                               ps[:, 1, SEQ - HT:HT].rearrange("p (b t) -> p b t", t=DS), ACT.Copy
                               ).then_inc(S[f"pair_free{u % 2}"], 1)

            def silu(i, s, u):
                n = CT * s + u
                act.wait_ge(S.conv_summed, i * 8 + n + 1)
                act.activation(xc[:, s % 2, u, 0:SEQ], acc[:, 0:SEQ], ACT.Silu)
                act.activation(xc[:, s % 2, u, SEQ:T].rearrange("p (b t) -> p b t", t=DS), sample_sums(), ACT.Silu
                               ).then_inc(S.conv_done, 1)

            def sample_sums():
                v = arena[:, 2 * CB + SEQ + 3:2 * CB + SEQ + 3 + 56]
                return v.rearrange("p (b t) -> p b t", t=7)[:, :, 0:DS]

            act.wait_ge(S.x_loaded, 16)
            act.wait_ge(S.const_loaded, 16)
            act_norm(c, act, 0)
            split_high(act, 0, 0)
            act.wait_ge(S.dtw_loaded, 16)
            act.activation(dtwh[:, 0, :], dtw[:], ACT.Copy).then_inc(S.dtw_high, 1)
            for k in range(KT):
                act.wait_ge(S.input_scaled, k + 1)
                act.activation(hh[:, k, :], c.xT[:, k, :], ACT.Copy).then_inc(S.input_high, 1)
            split_high(act, 0, 1)
            act.wait_ge(S.par_loaded, 16)
            act.activation(nega[:], par[0:32, G_ALOG:G_ALOG + 1], ACT.Exp).then_inc(S.a_ready, 1)
            act.wait_ge(S.dt_folded, 2)
            act.activation(dtf[:, 3, :], dtf[:, 3, :], ACT.Exp).then_inc(S.dt_logged, 1)
            act.wait_ge(S.dt_logged, 1)
            act.activation(dtf[:, 3, :], dtf[:, 3, :], ACT.Ln, bias=ones[0:32, 0:1]).then_inc(S.dt_logged, 1)
            for u in range(3):
                tile(0, 0, u)
                silu(0, 0, u)
            act.wait_ge(S.to_end, 1)
            act.activation(cdec[:].rearrange("p c h -> p (c h)"), Bp[:, 0, 0:CH * 32], ACT.Exp)
            act.activation(sdec[:].rearrange("p b h -> p (b h)"), Bp[:, 1, 0:DB * 32], ACT.Exp)
            act.activation(xws[:, 0:CH, :], xws[:, 0:CH, :], ACT.Exp)
            act.activation(xws[0:NS, CH, :], xws[0:NS, CH, :], ACT.Exp).then_inc(S.end_decay, 1)
            for u in range(3, GT - 1):
                tile(0, 0, u)
                if u < CT:
                    silu(0, 0, u)

            def step(i, s):
                g1 = i * 2 + (s + 1)
                last = s == GROUPS - 1
                act.wait_ge(S.b_turned, g1)
                act.activation(Btok.rearrange("p c n -> p (c n)"), Bp[:, 0, :], ACT.Copy).then_inc(S.b_kept, 1)
                act.wait_ge(S.seg_ready, g1)
                act.activation(ea.rearrange("p r t -> p (r t)"), abc.rearrange("p r t -> p (r t)"), ACT.Exp)
                act.activation(M.rearrange("p r t -> p (r t)"), M.rearrange("p r t -> p (r t)"), ACT.Exp)
                act.activation(Ms[0:NS], Ms[0:NS], ACT.Exp).then_inc(S.decay_ready, 1)
                tile(i, s, 5)
                if not last:
                    for u in range(2):
                        tile(i, s + 1, u)
                        silu(i, s + 1, u)
                    tile(i, s + 1, 2)
                act.wait_ge(S.gated, g1)
                act.activation(c.tmp[:].rearrange("p j t -> p (j t)"), yt.rearrange("p j t -> p (j t)"), ACT.Square
                               ).then_inc(S.y_squared, 1)
                if not last:
                    silu(i, s + 1, 2)
                    tile(i, s + 1, 3)
                act.wait_ge(S.y_summed, g1)
                act.activation(halves(c.rn[:]), A[:, :, 0:HT], ACT.Ln, bias=c.eps, scale=1.0 / 256
                               ).then_inc(S.y_logged, 1)
                act.wait_ge(S.y_logged, g1)
                act.activation(c.rn[:], c.rn[:], ACT.Exp, scale=-0.5).then_inc(S.y_inverted, 1)
                if not last:
                    silu(i, s + 1, 3)
                    tile(i, s + 1, 4)

            steps(act, step)

        @block.vector
        def _(dve):
            def conv(i, s, u):
                n = CT * s + u
                dve.wait_ge(S[f"pair_free{u % 2}"], i * GT + (GT * s + u) // 2 + 1)
                if n:
                    dve.wait_ge(S.conv_done, i * 8 + n)
                w = (i * 8 + n)
                b = cb[:, u % 2, :]
                dve.tensor_scalar(acc, b[:, 0:CO], one(par, w * 4 + G_CW), one(par, w + G_CBI), ALU.mult, ALU.add
                                  ).then_inc(S.tap_added, 1)
                for k in range(1, 4):
                    dve.wait_ge(S.tap_added, w * 3 + k)
                    ins = dve.scalar_tensor_tensor(out=acc, in0=b[:, k:k + CO], scalar=one(par, w * 4 + (G_CW + k)),
                                                   in1=acc, op0=ALU.mult, op1=ALU.add)
                    ins.then_inc(S.tap_added if k < 3 else S.conv_summed, 1)

            dve.sem_inc(S.group_done, FIRST)
            dve.memset(cb[:, 0, 0:3], 0.0)
            dve.memset(cb[:, 1, 0:3], 0.0).then_inc(S.zero_history, 1)
            dve.wait_ge(S.par_loaded, 16)
            dve.wait_ge(S.inverted, 1)
            split_low(dve, 0, 0)
            dve.wait_ge(S.dtw_high, 1)
            dve.tensor_tensor(dtwl[:, 0, :], dtw[:], dtwh[:, 0, :].bitcast(F32), ALU.subtract).then_inc(S.dtw_split, 1)
            for k in range(KT + 1):
                if k < KT:
                    dve.scalar_tensor_tensor(out=c.xT[:, k, :], in0=c.xT[:, k, :], scalar=par[:, G_A + k:G_A + k + 1],
                                             in1=c.rn[:], op0=ALU.mult, op1=ALU.mult).then_inc(S.input_scaled, 1)
                if k:
                    dve.wait_ge(S.input_high, k)
                    dve.tensor_tensor(hl[:, k - 1, :], c.xT[:, k - 1, :], hh[:, k - 1, :].bitcast(F32), ALU.subtract
                                      ).then_inc(S.input_split, 1)
            split_low(dve, 0, 1)
            dve.wait_ge(S.dt_projected, 1)
            u_, dt_, cs_, w_ = (dtf[:, n, :] for n in range(4))
            dve.tensor_scalar(halves(u_), Bp[0:32, :, 0:HT], par[0:32, G_DTB:G_DTB + 1], None, ALU.add
                              ).then_inc(S.dt_folded, 1)
            dve.wait_ge(S.dt_folded, 1)
            dve.scalar_tensor_tensor(out=w_, in0=u_, scalar=-1.0, in1=u_, op0=ALU.mult, op1=ALU.min
                                     ).then_inc(S.dt_folded, 1)
            dve.wait_ge(S.dt_logged, 2)
            dve.wait_ge(S.a_ready, 1)
            dve.scalar_tensor_tensor(out=dt_, in0=u_, scalar=0.0, in1=w_, op0=ALU.max, op1=ALU.add
                                     ).then_inc(S.dt_step, 1)
            dve.wait_ge(S.dt_step, 1)
            dve.tensor_scalar(u_, dt_, nega[:, 0:1], -1.0, ALU.mult, ALU.mult).then_inc(S.dt_step, 1)
            dve.wait_ge(S.dt_step, 2)
            dve.tensor_tensor_scan(cs_, cst[0:32, C_RST:C_RST + T], u_, 0.0, ALU.mult, ALU.add
                                   ).then_inc(S.decay_summed, 1)
            dve.wait_ge(S.dt_turned, 1)
            for k, t in enumerate((dtt, acst)):
                dve.tensor_copy(t[:, 0:CH, :].rearrange("p c h -> p (c h)"), A[:, k, 0:CH * 32])
                dve.tensor_copy(t[0:NS, CH, :], A[0:NS, k, CH * 32:(CH + 1) * 32]).then_inc(S.dt_kept, 1)
            dve.wait_ge(S.dt_kept, 2)
            dve.tensor_tensor(zl[:], acst[0:NS, CH:CH + 1, :].to_broadcast([NS, DB, 32]),
                              cst[0:NS, C_LAST:C_LAST + DB].unsqueeze(2).to_broadcast([NS, DB, 32]), ALU.mult
                              ).then_inc(S.last_kept, 1)
            for u in range(3):
                if u:
                    split_low(dve, 0, u + 1)
                conv(0, 0, u)
            dve.wait_ge(S.ends_ready, 1)
            dve.tensor_tensor(xws[:, 0:CH, :].rearrange("p c h -> p (c h)"), Bp[:, 0, 0:CH * 32],
                              acst[:, 0:CH, :].rearrange("p c h -> p (c h)"), ALU.subtract)
            dve.tensor_tensor(xws[0:NS, CH, :], Bp[0:NS, 0, 128:160], acst[0:NS, CH, :], ALU.subtract
                              ).then_inc(S.to_end, 1)
            dve.wait_ge(S.end_decay, 1)
            dve.tensor_tensor(xws[:, 0:CH, :], xws[:, 0:CH, :], dtt[:, 0:CH, :], ALU.mult)
            dve.tensor_tensor(xws[0:NS, CH, :], xws[0:NS, CH, :], dtt[0:NS, CH, :], ALU.mult).then_inc(S.dt_scaled, 1)
            split_low(dve, 0, 4)
            conv(0, 0, 3)
            split_low(dve, 0, 5)
            dve.wait_ge(S.dt_scaled, 1)

            def step(i, s):
                par_ = s % 2
                g1 = i * 2 + (s + 1)
                X = xc[:, par_]
                last = s == GROUPS - 1
                dve.wait_ge(S.decay_loaded, i * 32 + 16 * (s + 1))
                for r in range(R):
                    for n in range(CH):
                        dve.tensor_scalar(M[:, r, n * P:(n + 1) * P], abc[:, r, n * P:(n + 1) * P],
                                          head(acst, n, i, s, r), 0.0, ALU.subtract, ALU.min)
                    ins = dve.tensor_scalar(Ms[0:NS, r, :], abc[0:NS, r, SEQ:T], head(acst, CH, i, s, r)[0:NS], 0.0,
                                            ALU.subtract, ALU.min)
                ins.then_inc(S.seg_ready, 1)
                if not last:
                    split_low(dve, i, GT * (s + 1))
                dve.wait_ge(S.x_turned, g1)
                for k, (dst, sc) in enumerate(((xdt, dtt), (xw, xws))):
                    for n in range(CH):
                        ins = dve.tensor_tensor(
                            dst[:, n, :].rearrange("p (r d) -> p r d", r=R),
                            A[:, n // 2, (n % 2) * 256:(n % 2) * 256 + 256].rearrange("p (r d) -> p r d", r=R),
                            over(heads(sc, n, n + 1, i, s).rearrange("p c r -> p (c r)"), HP), ALU.mult)
                ins.then_inc(S.x_scaled, 1)
                dve.wait_ge(S.cb_ready, g1)
                dve.tensor_tensor(CBm, Bp[:, 1, :].rearrange("p (c n) -> p c n", c=CH),
                                  cst[:, C_CAU:C_CAU + P].unsqueeze(1).to_broadcast([P, CH, P]), ALU.mult
                                  ).then_inc(S.cb_masked, 1)
                dve.wait_ge(S.cb_masked, g1)
                dve.wait_ge(S.decay_ready, g1)
                dve.tensor_tensor(M, M, CBm.rearrange("p c n -> p (c n)").unsqueeze(1).to_broadcast([P, R, SEQ]), ALU.mult)
                dve.tensor_tensor(ea[:, :, P:SEQ], ea[:, :, P:SEQ], X[:, 3:4, P:SEQ].to_broadcast([P, R, SEQ - P]),
                                  ALU.mult)
                dve.wait_ge(S.sample_ready, g1)
                for dst, sc in ((xdt, dtt), (xw, xws)):
                    dve.tensor_tensor(dst[0:NS, CH, :].rearrange("p (r d) -> p r d", r=R),
                                      A[0:NS, 0, 0:256].rearrange("p (r d) -> p r d", r=R),
                                      over(heads(sc, CH, CH + 1, i, s, NS).rearrange("p c r -> p (c r)"), HP),
                                      ALU.mult)
                dve.tensor_tensor(Bm[0:NS], A[0:NS, 1:2, 0:P].to_broadcast([NS, DB, P]),
                                  cst[0:NS, C_BLK:C_BLK + DB].unsqueeze(2).to_broadcast([NS, DB, P]), ALU.mult)
                dve.tensor_tensor(CBs[0:NS, :], A[0:NS, 1, P:P + NS], cst[0:NS, C_SAMP:C_SAMP + NS], ALU.mult
                                  ).then_inc(S.cbs_masked, 1)
                for r in range(R):
                    lo = 64 * (r % 2)
                    dve.tensor_tensor(yoff[lo:lo + 64, r // 2, :], A[lo:lo + 64, 1, 192 + (r // 2) * NS:192 + (r // 2 + 1) * NS],
                                      ea[lo:lo + 64, r, SEQ:T], ALU.mult)
                dve.wait_ge(S.cbs_masked, g1)
                dve.tensor_tensor(Ms[0:NS], Ms[0:NS], CBs[0:NS, :].unsqueeze(1).to_broadcast([NS, R, NS]), ALU.mult
                                  ).then_inc(S.sample_kept, 1)
                if not last:
                    split_low(dve, i, GT * (s + 1) + 1)
                    conv(i, s + 1, 0)
                dve.wait_ge(S.states_ready, g1)
                dve.tensor_copy(hst[:, 0, :], A[:, 0, 0:256]).then_inc(S.state_step, 1)
                for n in range(1, CH):
                    v = hst[:, n, :]
                    dve.wait_ge(S.state_step, i * 12 + (6 * s + 2 * n - 1))
                    dve.tensor_tensor(v.rearrange("p (r d) -> p r d", r=R),
                                      hst[:, n - 1, :].rearrange("p (r d) -> p r d", r=R),
                                      over(heads(cdec, n, n + 1, i, s).rearrange("p c r -> p (c r)"), HP),
                                      ALU.mult).then_inc(S.state_step, 1)
                    dve.wait_ge(S.state_step, i * 12 + (6 * s + 2 * n))
                    dve.tensor_tensor(v, v, A[:, n // 2, (n % 2) * 256:(n % 2) * 256 + 256], ALU.add
                                      ).then_inc(S.state_step if n < CH - 1 else S.states_kept, 1)

                def add_update(q):
                    dve.wait_ge(S.update_ready, i * 4 + 2 * s + q + 1)
                    v = h0[:, 4 * q:4 * q + 4, :].rearrange("p (a b) x -> p a (b x)", a=2)
                    dve.tensor_tensor(v, v, Bp[:, :, :], ALU.add).then_inc(S.state_added, 1)

                dve.wait_ge(S.h0_decayed, g1)
                add_update(0)
                if not last:
                    split_low(dve, i, GT * (s + 1) + 2)
                    conv(i, s + 1, 1)
                dve.wait_ge(S.y_ready, g1)
                for j in range(2):
                    dve.scalar_tensor_tensor(out=yt[:, j, 0:SEQ], in0=X[:, j, 0:SEQ], scalar=one(par, g1 * 2 + (G_DSK + j - 2)),
                                             in1=A[:, j, :], op0=ALU.mult, op1=ALU.add)
                add_update(1)
                if not last:
                    split_low(dve, i, GT * (s + 1) + 3)
                dve.wait_ge(S.ys_ready, g1)
                for j in range(2):
                    ins = dve.scalar_tensor_tensor(out=yt[:, j, SEQ:T], in0=X[:, j, SEQ:T],
                                                   scalar=one(par, g1 * 2 + (G_DSK + j - 2)),
                                                   in1=Bp[:, 0, j * NS:(j + 1) * NS], op0=ALU.mult, op1=ALU.add)
                ins.then_inc(S.y_skip, 1)
                dve.wait_ge(S.y_skip, g1)
                dve.tensor_tensor(yt[:, :, SEQ:T], yt[:, :, SEQ:T], yoff, ALU.add).then_inc(S.y_summed_up, 1)
                if not last:
                    conv(i, s + 1, 2)
                    split_low(dve, i, GT * (s + 1) + 4)
                    conv(i, s + 1, 3)
                    split_low(dve, i, GT * (s + 1) + 5)
                dve.wait_ge(S.y_inverted, g1)
                for j in range(2):
                    ins = dve.scalar_tensor_tensor(out=col(c.yT, g1 * 2 + (j - 2)), in0=yt[:, j, :],
                                                   scalar=one(par, g1 * 2 + (G_GN + j - 2)), in1=c.rn[:],
                                                   op0=ALU.mult, op1=ALU.mult)
                ins.then_inc(S.group_done, 1)

            steps(dve, step)

        @block.gpsimd
        def _(pool):
            def history(i, s, u):
                n = CT * s + u
                if n >= 2:
                    pool.wait_ge(S.conv_summed, i * 8 + n - 1)
                    pool.wait_ge(S.history_out, i * 8 + n - 1)
                pool.tensor_copy(cb[:, u % 2, 3 + SEQ:].rearrange("p (b t) -> p b t", t=7)[:, :, 0:3],
                                 col(hist, i * 8 + n).rearrange("p (b t) -> p b t", t=3)).then_inc(S.history_in, 1)

            def keep(i, s, u):
                n = CT * s + u
                pool.wait_ge(S[f"pair_free{u % 2}"], i * GT + (GT * s + u) // 2 + 1)
                v = col(ncv, i * 8 + n)
                pool.tensor_copy(v[:, 0:3], cb[:, u % 2, SEQ:SEQ + 3])
                pool.tensor_copy(v[:, 3:27].rearrange("p (b t) -> p b t", t=3),
                                 cb[:, u % 2, 3 + SEQ:].rearrange("p (b t) -> p b t", t=7)[:, :, 4:7]
                                 ).then_inc(S.history_out, 1)

            def load_state(i, s):
                pool.dma_start(h0.rearrange("p b x -> p (b x)"),
                               c.h0_d[bass.ds(i * 2 + s, 1)].rearrange("a p x -> (a p) x")).then_inc(S.h0_loaded, 16)

            def load_decay(i, s):
                pool.dma_start(abc, c.scr[bass.ds(i * (2 * R) + s * R, R)].unsqueeze(0).to_broadcast([P, R, T])
                               ).then_inc(S.decay_loaded, 16)

            load_state(0, 0)
            pool.wait_ge(S.decay_summed, 1)
            pool.dma_start(c.scr, dtf[:, 2, :]).then_inc(S.decay_written, 16)
            pool.wait_ge(S.hist_loaded, 16)
            history(0, 0, 0)
            history(0, 0, 1)
            pool.wait_ge(S.decay_written, 16)
            load_decay(0, 0)
            for u in range(CT):
                keep(0, 0, u)
                if u + 2 < CT:
                    history(0, 0, u + 2)

            def step(i, s):
                g1 = i * 2 + (s + 1)
                last = s == GROUPS - 1
                if not last:
                    history(i, s + 1, 0)
                    history(i, s + 1, 1)
                pool.wait_ge(S.sample_ready, g1)
                for b in range(DB):
                    v = h0[:, b, :].rearrange("p (r d) -> p r d", r=R)
                    ins = pool.tensor_tensor(v, v, over(heads(sdec, b, b + 1, i, s).rearrange("p c r -> p (c r)"), HP),
                                             ALU.mult)
                ins.then_inc(S.h0_decayed, 1)
                if not last:
                    keep(i, s + 1, 0)
                    history(i, s + 1, 2)
                pool.wait_ge(S.states_kept, g1)
                pool.dma_start(c.nst_p[bass.ds(i * 2 + s, 1)].rearrange("a p x -> (a p) x"), hst[:, CH - 1, :]
                               ).then_inc(S.state_stored, 16)
                if not last:
                    keep(i, s + 1, 1)
                    history(i, s + 1, 3)
                    keep(i, s + 1, 2)
                pool.wait_ge(S.y_summed_up, g1)
                if not last:
                    load_decay(i, s + 1)
                pool.wait_ge(S.pair_free1, i * GT + (GT * s + 5) // 2 + 1)
                pool.wait_ge(S.state_stored, i * 32 + 16 * (s + 1))
                for j in range(2):
                    ins = pool.tensor_tensor(yt[:, j, :], yt[:, j, :], sz[:, j, :], ALU.mult)
                ins.then_inc(S.gated, 1)
                pool.dma_start(c.nst_s[bass.ds(i * 2 + s, 1)].rearrange("a p x -> (a p) x"),
                               h0.rearrange("p b x -> p (b x)")).then_inc(S.samples_stored, 16)
                if not last:
                    keep(i, s + 1, 3)
                    pool.wait_ge(S.samples_stored, i * 32 + 16 * (s + 1))
                    load_state(i, s + 1)

            steps(pool, step)


def out_phase(c):
    nc, S = c.nc, c.S
    with ExitStack() as ctx:
        c.Wh, c.Wl = split_buffers(nc, ctx, "W1", 2, D)
        Yh, Yl = split_buffers(nc, ctx, "Y1", 2 * KT, T)
        block = ctx.enter_context(nc.Block())
        b0 = c.stage["out"][1]

        @block.sync
        def _(sp):
            sp.wait_ge(S.mixed_split, KT)
            sp.dma_start(c.xT, c.xin).then_inc(S.x_loaded, 16)
            sp_stream_split(c, sp, b0 + SLOTS, 2 * KT)

        @block.tensor
        def _(pe):
            pe_layer(c, pe, "out", (Yh, Yl), lambda k: (S.mixed_split, k + 1))

        @block.scalar
        def _(act):
            act_split(c, act, 0, b0)
            for k in range(2 * KT):
                act.activation(Yh[:, k, :], c.yT[:, k, :], ACT.Copy).then_inc(S.mixed_high, 1)
            act_idle_layer(c, act, "out", ends=True)

        @block.vector
        def _(dve):
            dve_split(c, dve, 0, b0)
            for k in range(2 * KT):
                dve.wait_ge(S.mixed_high, k + 1)
                dve.tensor_tensor(Yl[:, k, :], c.yT[:, k, :], Yh[:, k, :].bitcast(F32), ALU.subtract
                                  ).then_inc(S.mixed_split, 1)
            dve.wait_ge(S.x_loaded, 32)
            dve_add_layer(c, dve, "out", ends=True)


def mlp_phase(c):
    nc, S = c.nc, c.S
    with ExitStack() as ctx:
        c.Wh, c.Wl = split_buffers(nc, ctx, "W2", 2, D)
        c.Hh, c.Hl = split_buffers(nc, ctx, "H2", KT, T)
        c.Yh, c.Yl = split_buffers(nc, ctx, "Y2", 2 * KT, T)
        c.full = ctx.enter_context(nc.sbuf_tensor("full2", [P, 2, T], F32))
        block = ctx.enter_context(nc.Block())
        b0 = c.stage["up00"][1]

        @block.sync
        def _(sp):
            sp_stream_split(c, sp, b0 + SLOTS, 8 * KT)

        @block.tensor
        def _(pe):
            pe_norm(c, pe, 1)
            pe_mlp(c, pe, 0, 0)

        @block.scalar
        def _(act):
            act_norm(c, act, 1)
            act_split(c, act, 0, b0)
            act_scale(c, act, 0)
            act_mlp(c, act, 0)

        @block.vector
        def _(dve):
            for u in range(2):
                dve.sem_inc(S[f"hidden_split{u}"], FIRST)
            dve_split(c, dve, 0, b0)
            dve.wait_ge(S.inverted, 2)
            dve_scale(c, dve, 0, G_MA)
            dve_mlp(c, dve, 0)


def qkv_phase(c):
    nc, S = c.nc, c.S
    with ExitStack() as ctx:
        c.Wh, c.Wl = split_buffers(nc, ctx, "W3", 2, D)
        Kh, Kl = split_buffers(nc, ctx, "H3", KT, T)
        Qh, Ql = split_buffers(nc, ctx, "H4", KT, T)
        c.full = ctx.enter_context(nc.sbuf_tensor("full3", [P, 2, T], F32))
        c.rq = ctx.enter_context(nc.sbuf_tensor("rq3", [P, 2, T], F32))
        block = ctx.enter_context(nc.Block())
        b0 = c.stage["k"][1]

        @block.sync
        def _(sp):
            sp_stream_split(c, sp, b0 + SLOTS, 3 * KT)

        @block.tensor
        def _(pe):
            for u in range(2):
                pe.sem_inc(S[f"tile_summed{u}"], FIRST)
            pe_norm(c, pe, 2)
            for name, src, first, n0 in (("k", (Kh, Kl), KT, None), ("q", (Qh, Ql), 2 * KT, 0), ("v", (Kh, Kl), KT, KT // 2)):
                def sums(i, u):
                    pe_tile_norm(c, pe, u % 2, i * 2 + n0 + u // 2, c.blk64)

                pe_layer(c, pe, name, src, lambda k: (S.tile_split, first + k + 1), None if n0 is None else sums)

        @block.scalar
        def _(act):
            for u in range(2):
                act.sem_inc(S[f"tile_logged{u}"], FIRST)
            act_norm(c, act, 2)
            act_split(c, act, 0, b0)
            c.Hh = Kh
            act_scale(c, act, KT)

            def k_step(i, u):
                act.wait_ge(S.block_done, i * SLOTS + c.stage["k"][1] + u + 1)
                act.activation(halves(col(c.qk, i * 4 + KT + u)), c.LN[u % 2][:, :, 0:HT], ACT.Copy
                               ).then_inc(S[f"pair_free{u % 2}"], 1)
                act.wait_ge(S.tile_scaled, i * 4 + 2 * KT + u + 1)
                act.activation(col(Qh, i * 4 + u), c.full[:, u % 2, :], ACT.Copy).then_inc(S.tile_high, 1)

            def copy_and_norm(name, dst, dst0, src0, n0):
                t0, b, _, _ = c.stage[name]

                def step(i, u):
                    n = i * 2 + n0 + u // 2
                    act.wait_ge(S[f"pair_free{u % 2}"], i * 2 + (t0 + u) // 2)
                    act_tile_square(c, act, u % 2, n, halves(col(c.qk, i * 4 + src0 + u)))
                    act.wait_ge(S.block_done, i * SLOTS + b + u + 1)
                    act.activation(halves(col(dst, i * 4 + dst0 + u)), c.LN[u % 2][:, :, 0:HT], ACT.Copy
                                   ).then_inc(S[f"pair_free{u % 2}"], 1)
                    act_tile_invert(c, act, u % 2, n, 64)

                split_turns(c, act, name, act_split, step, name == "v")

            split_turns(c, act, "k", act_split, k_step, False)
            copy_and_norm("q", c.qk, 0, KT, 0)
            copy_and_norm("v", c.vT, 0, 0, KT // 2)

        @block.vector
        def _(dve):
            for u in range(2):
                dve.sem_inc(S[f"tile_normed{u}"], FIRST)
            dve_split(c, dve, 0, b0)
            dve.wait_ge(S.inverted, 3)
            c.Hh, c.Hl = Kh, Kl
            dve_scale(c, dve, KT, G_KV)

            def k_step(i, u):
                dve.wait_ge(S.tile_split, i * 4 + 2 * KT + u - 1)
                dve.scalar_tensor_tensor(out=c.full[:, u % 2, :], in0=col(c.xT, i * 4 + u),
                                         scalar=one(c.par, i * 4 + G_B + u), in1=c.rn[:], op0=ALU.mult, op1=ALU.mult
                                         ).then_inc(S.tile_scaled, 1)
                dve.wait_ge(S.tile_high, i * 4 + 2 * KT + u + 1)
                dve.tensor_tensor(col(Ql, i * 4 + u), c.full[:, u % 2, :], col(Qh, i * 4 + u).bitcast(F32), ALU.subtract
                                  ).then_inc(S.tile_split, 1)

            def norm_before(name, src0, n0, gain):
                def step(i, u):
                    dve_tile_norm(c, dve, u % 2, i * 2 + n0 + u // 2, col(c.qk, i * 4 + src0 + u),
                                  c.par[:, gain:gain + 1])

                split_turns(c, dve, name, dve_split, step, name == "v")

            split_turns(c, dve, "k", dve_split, k_step, False)
            norm_before("q", KT, 0, G_KN)
            norm_before("v", 0, KT // 2, G_QN)


def attention_phase(c):
    nc, S = c.nc, c.S
    A, Bp, cst, par, ident, ones = c.A, c.Bp, c.cst, c.par, c.ident, c.ones
    turned, heads_out = c.LN[0][:, 0, :], c.LN[0][:, 1, :]
    keyed, weighed = c.LN[1][:, 0, :], c.LN[1][:, 1, :]
    NB = SEQ // P
    with ExitStack() as ctx:
        def sb(name, *shape):
            return ctx.enter_context(nc.sbuf_tensor(name, list(shape), F32))

        kp = sb("kpage", P, PAGES, NH, P)
        vp = sb("vpage", P, PAGES, NH, P)
        vs = sb("vhead", P, SEQ)
        vtok = sb("vtok", P, NB, P)
        pr = [sb("probs0", P, 2, SEQ - P), sb("probs1", P, 2, SEQ)]
        qst = [sb(f"qsample{n}", P, NH, 32) for n in range(2)]
        spr = sb("sprobs", P, PAST)
        sn = sb("snew", P, NS)
        cmb = sb("cmb", P, 32)
        aTs = sb("saT", P, (PAGES + 1) * 32)
        osb = sb("osb", P, 2 * P)
        vn = sb("vnew", NS, NH, P)
        mx = sb("mx", P, NB, 2)
        nm = sb("nm", P, NB, 2)
        sm = sb("sm", P, NB, 2)
        smx = sb("smx", P, 2)
        snm = sb("snm", P, 1)
        ssm = sb("ssm", P, 2)
        sden = sb("sden", P, 1)
        cf = sb("cf", P, 1)
        lam2 = sb("lam2", 64, 2)
        le = sb("le", P, 2)
        nlam = sb("nlam", P, 1)
        qz = [c.tmp, sb("qhead1", P, 2, T)]
        aT = c.rn
        block = ctx.enter_context(nc.Block())

        def turns(eng, turn):
            with eng.Fori(0, NH // 2) as i:
                turn(i * 2, 0)
                turn(i * 2 + 1, 1)

        @block.sync
        def _(sp):
            sp.wait_ge(S.table_loaded, 16)

            def load(b, first):
                pages = [sp.value_load(c.pt[0:1, bass.ds(b * PAGES + p, 1)], min_val=0, max_val=c.n_pool - 1)
                         for p in range(PAGES)]
                for p, page in enumerate(pages):
                    if not first:
                        sp.wait_ge(S.keys_used, b * 2 + (p // 4 - 1))
                    sp.dma_start(kp[:, p].rearrange("p h x -> p (h x)"),
                                 c.ck_d[bass.ds(page, 1)].rearrange("a p x -> (a p) x")).then_inc(S[f"kpage{p}"], 16)
                for p, page in enumerate(pages):
                    if not first:
                        sp.wait_ge(S.vpage_used, b * PAGES + (p + 1 - PAGES))
                    sp.dma_start(vp[:, p].rearrange("p h x -> p (h x)"),
                                 c.cv_d[bass.ds(page, 1)].rearrange("a p x -> (a p) x")).then_inc(S[f"vpage{p}"], 16)

            load(0, True)
            with sp.Fori(1, DB) as b:
                load(b, False)
            sp.dma_start(c.k_o, c.qk[:, KT:2 * KT, :]).then_inc(S.stored, 16)
            sp.dma_start(c.v_o, c.vT[:]).then_inc(S.stored, 16)
            sp.wait_ge(S.stored, 48)

        @block.tensor
        def _(pe):
            for first in (S.block_weighed, S.v_turned, S.samples_scored):
                pe.sem_inc(first, FIRST)
            for first in (S.scores_ready0, S.scores_ready1):
                pe.sem_inc(first, FIRST)
            for h in range(NH):
                mm = pe.transpose(c.LN[0][0:NS, h // 4, (h % 4) * P:(h % 4 + 1) * P], c.vT[:, h, SEQ:T], ident)
            pe.matmul(weighed[:, 0:2 * P], ident, cst[:, 0:2 * P], start=True, stop=True)
            mm = pe.transpose(c.LN[0][0:NS, 1, 3 * P:4 * P], c.vT[:, NH - 1, SEQ:T], ident)
            mm.then_inc(S.vnew_turned, 1)
            pe.wait_ge(S.lam_products, 1)
            pe.matmul(A[:, 0, 0:2], ones[0:64, :], lam2[:], start=True, stop=True).then_inc(S.lam_summed, 1)
            pe.wait_ge(S.vnew_kept, 1)
            pe.wait_ge(S.lam_ready, 1)

            def turn(j, par_):
                q_ = qz[par_]

                def scores(i):
                    w = (i + 1) * P
                    pe.wait_ge(S.exps_done, j * NB + i + FIRST)
                    for cc in range(2):
                        k = c.qk[:, bass.ds(j + KT, 1), 0:w].rearrange("p a x -> p (a x)")
                        pe.matmul(A[:, cc, 0:w], q_[:, cc, i * P:(i + 1) * P], k, start=True, stop=False)
                        mm = pe.matmul(A[:, cc, w - P:w], ident, cst[:, C_NEG:C_NEG + P], start=False, stop=True)
                    mm.then_inc(S[f"scores_ready{par_}"], 1)

                def turn_weights(i):
                    pe.wait_ge(S.weights_ready, j * NB + i + 1)
                    for k in range(i + 1):
                        mm = pe.transpose(turned[:, k * P:(k + 1) * P], pr[i % 2][:, 0, k * P:(k + 1) * P], ident)
                    mm.then_inc(S.weights_turned, 1)

                def weigh(i):
                    pe.wait_ge(S.weights_kept, j * NB + i + 1)
                    for k in range(i + 1):
                        mm = pe.matmul(heads_out[:, i * P:(i + 1) * P], vtok[:, k, :], aT[:, k * P:(k + 1) * P],
                                       start=(k == 0), stop=(k == i))
                    mm.then_inc(S.block_weighed, 1)

                def sample_scores():
                    q = qst[par_]
                    for half_ in range(2):
                        for p in range(4 * half_, 4 * half_ + 4):
                            pe.wait_ge(S[f"kpage{p}"], j * 16 + 16)
                        for hh in range(2):
                            for t in range(4):
                                mm = pe.matmul(Bp[32 * t:32 * t + 32, half_, :], q[:, 4 * hh + t, :],
                                               kp[:, 4 * half_:4 * half_ + 4, 4 * hh + t, :],
                                               start=(hh == 0), stop=(hh == 1))
                        mm.then_inc(S.keys_used, 1)
                    for hh in range(2):
                        for t in range(4):
                            mm = pe.matmul(keyed[32 * t:32 * t + 32, 0:NS], q[:, 4 * hh + t, :],
                                           c.qk[:, KT + 4 * hh + t, SEQ:T], start=(hh == 0), stop=(hh == 1))
                    mm.then_inc(S.samples_scored, 1)

                def sample_turn():
                    pe.wait_ge(S.cmb_ready, j + 1)
                    for p in range(PAGES):
                        pe.matmul(keyed[:, p * 32:(p + 1) * 32], spr[:, p * P:(p + 1) * P], cmb[:], start=True, stop=True)
                    pe.matmul(keyed[0:NS, PAGES * 32:(PAGES + 1) * 32], sn[:], cmb[:], start=True, stop=True
                              ).then_inc(S.sweights_turned, 1)

                def sample_weigh(half_):
                    if half_ == 0:
                        pe.wait_ge(S.sweights_kept, j + 1)
                        pe.wait_ge(S.sample_out, j + FIRST)
                    for p in range(4 * half_, 4 * half_ + 4):
                        pe.wait_ge(S[f"vpage{p}"], j * 16 + 16)
                        for hh in range(2):
                            for t in range(4):
                                mm = pe.matmul(weighed[32 * t:32 * t + 8, hh * P:(hh + 1) * P],
                                               aTs[:, p * 32 + 8 * t:p * 32 + 8 * t + 8], vp[:, p, 4 * hh + t, :],
                                               start=(p == 0 and hh == 0), stop=False, skip_group_check=True)
                        mm.then_inc(S.vpage_used, 1)
                    if half_ == 0:
                        return
                    for hh in range(2):
                        for t in range(4):
                            mm = pe.matmul(weighed[32 * t:32 * t + 8, hh * P:(hh + 1) * P],
                                           aTs[0:NS, PAGES * 32 + 8 * t:PAGES * 32 + 8 * t + 8], vn[:, 4 * hh + t, :],
                                           start=False, stop=True, skip_group_check=True)
                    mm.then_inc(S.sample_weighed, 1)

                def sample_back():
                    pe.wait_ge(S.sample_kept_out, j + 1)
                    for hh in range(2):
                        mm = pe.transpose(weighed[:, (2 + hh) * P:(3 + hh) * P], osb[:, hh * P:(hh + 1) * P], ident)
                    mm.then_inc(S.sample_back, 1)

                pe.wait_ge(S.head_copied, j + 1 + FIRST)
                for k in range(NB):
                    mm = pe.transpose(turned[:, k * P:(k + 1) * P], vs[:, k * P:(k + 1) * P], ident)
                mm.then_inc(S.v_turned, 1)
                scores(0)
                sample_scores()
                pe.wait_ge(S.v_kept, j + 1)
                turn_weights(0)
                scores(1)
                pe.wait_ge(S.head_out, j + FIRST)
                weigh(0)
                sample_turn()
                scores(2)
                turn_weights(1)
                weigh(1)
                sample_weigh(0)
                scores(3)
                turn_weights(2)
                sample_weigh(1)
                weigh(2)
                turn_weights(3)
                sample_back()
                weigh(3)

            turns(pe, turn)

        @block.scalar
        def _(act):
            act.sem_inc(S.exps_done, FIRST)
            act.sem_inc(S.head_out, FIRST)
            act.wait_ge(S.vnew_turned, 1)
            act.activation(vn[:].rearrange("p (a h) x -> p a (h x)", a=2), c.LN[0][0:NS, :, :], ACT.Copy
                           ).then_inc(S.vnew_kept, 1)
            act.wait_ge(S.lam_summed, 1)
            act.activation(le[:], A[:, 0, 0:2], ACT.Exp).then_inc(S.lam_exps, 1)

            def turn(j, par_):
                def exps(i):
                    w = (i + 1) * P
                    act.wait_ge(S.negmax_ready, j * NB + i + 1)
                    if i >= 2:
                        act.wait_ge(S.weights_turned, j * NB + i - 1)
                    for cc in range(2):
                        ins = act.activation(pr[i % 2][:, cc, 0:w], A[:, cc, 0:w], ACT.Exp, bias=nm[:, i, cc:cc + 1],
                                             scale=SCALE, accum_out=sm[:, i, cc:cc + 1])
                    ins.then_inc(S.exps_done, 1)

                def keep_weights(i):
                    act.wait_ge(S.weights_turned, j * NB + i + 1)
                    act.wait_ge(S.block_weighed, j * NB + i + FIRST)
                    act.activation(aT[:, 0:(i + 1) * P], turned[:, 0:(i + 1) * P], ACT.Copy).then_inc(S.weights_kept, 1)

                act.wait_ge(S.v_turned, j + 1 + FIRST)
                act.activation(vtok[:].rearrange("p k x -> p (k x)"), turned, ACT.Copy).then_inc(S.v_kept, 1)
                exps(0)
                keep_weights(0)
                act.wait_ge(S.snegmax_ready, j + 1)
                act.activation(spr[:], Bp[:].rearrange("p a x -> p (a x)"), ACT.Exp, bias=snm[:], scale=SCALE,
                               accum_out=ssm[:, 0:1])
                act.activation(sn[:], sn[:], ACT.Exp, bias=snm[:], scale=SCALE, accum_out=ssm[:, 1:2]
                               ).then_inc(S.sexps_done, 1)
                exps(1)
                act.wait_ge(S.sweights_turned, j + 1)
                act.activation(aTs[:, 0:PAGES * 32], keyed[:, 0:PAGES * 32], ACT.Copy)
                act.activation(aTs[0:NS, PAGES * 32:], keyed[0:NS, PAGES * 32:(PAGES + 1) * 32], ACT.Copy
                               ).then_inc(S.sweights_kept, 1)
                keep_weights(1)
                exps(2)
                keep_weights(2)
                exps(3)
                keep_weights(3)
                act.wait_ge(S.block_weighed, j * NB + NB + FIRST)
                act.activation(c.hT[:, bass.ds(j, 1), 0:SEQ].rearrange("p a x -> p (a x)"), heads_out, ACT.Copy
                               ).then_inc(S.head_out, 1)

            turns(act, turn)

        @block.vector
        def _(dve):
            dve.sem_inc(S.sample_out, FIRST)
            lp = par[0:64, G_LAM:G_LAM + 4].rearrange("p (m two) -> p m two", two=2)
            dve.tensor_tensor(lam2[:], lp[:, :, 0], lp[:, :, 1], ALU.mult).then_inc(S.lam_products, 1)
            dve.tensor_scalar(c.gsub[:], par[:, G_SUB:G_SUB + 1], 1.0 - LAM_INIT, None, ALU.mult)
            dve.wait_ge(S.lam_exps, 1)
            dve.tensor_tensor(nlam[:], le[:, 1:2], le[:, 0:1], ALU.subtract).then_inc(S.lam_step, 1)
            dve.wait_ge(S.lam_step, 1)
            dve.tensor_scalar(nlam[:], nlam[:], -LAM_INIT, None, ALU.add).then_inc(S.lam_ready, 1)
            dve.wait_ge(S.lam_ready, 1)
            dve.scalar_tensor_tensor(out=cf[:], in0=cst[:, C_COMP + 1:C_COMP + 2], scalar=nlam[:, 0:1],
                                     in1=cst[:, C_COMP:C_COMP + 1], op0=ALU.mult, op1=ALU.add).then_inc(S.cf_ready, 1)
            dve.wait_ge(S.cf_ready, 1)

            def turn(j, par_):
                def maxima(i):
                    dve.wait_ge(S[f"scores_ready{par_}"], (j - par_) * (NB // 2) + i + 1 + FIRST)
                    dve.tensor_reduce(mx[:, i, :], A[:, :, 0:(i + 1) * P], AX.X, ALU.max).then_inc(S.max_ready, 1)
                    dve.wait_ge(S.max_ready, j * NB + i + 1)
                    dve.tensor_scalar(nm[:, i, :], mx[:, i, :], -SCALE, None, ALU.mult).then_inc(S.negmax_ready, 1)

                def combine(i):
                    w = (i + 1) * P
                    n = j * (3 * NB) + 3 * i
                    p_ = pr[i % 2]
                    dve.wait_ge(S.exps_done, j * NB + i + 1 + FIRST)
                    dve.reciprocal(sm[:, i, :], sm[:, i, :]).then_inc(S.combine_step, 1)
                    dve.wait_ge(S.combine_step, n + 1)
                    dve.tensor_scalar(sm[:, i, 1:2], sm[:, i, 1:2], nlam[:, 0:1], None, ALU.mult
                                      ).then_inc(S.combine_step, 1)
                    dve.tensor_scalar(p_[:, 0, 0:w], p_[:, 0, 0:w], sm[:, i, 0:1], None, ALU.mult
                                      ).then_inc(S.combine_step, 1)
                    dve.wait_ge(S.combine_step, n + 3)
                    dve.scalar_tensor_tensor(out=p_[:, 0, 0:w], in0=p_[:, 1, 0:w], scalar=sm[:, i, 1:2],
                                             in1=p_[:, 0, 0:w], op0=ALU.mult, op1=ALU.add).then_inc(S.weights_ready, 1)

                maxima(0)
                combine(0)
                dve.wait_ge(S.samples_scored, j + 1 + FIRST)
                dve.tensor_reduce(smx[:, 0:1], Bp[:].rearrange("p a x -> p (a x)"), AX.X, ALU.max)
                dve.tensor_tensor(sn[:], keyed[:, 0:NS],
                                  cst[:, C_NEWM:C_NEWM + DB * NS].rearrange("p (b x) -> p b x", b=DB)
                                  [:, bass.ds(j, 1), :].rearrange("p a x -> p (a x)"), ALU.add
                                  ).then_inc(S.new_masked, 1)
                dve.wait_ge(S.new_masked, j + 1)
                dve.tensor_reduce(smx[:, 1:2], sn[:], AX.X, ALU.max).then_inc(S.smax_ready, 1)
                dve.wait_ge(S.smax_ready, j + 1)
                dve.tensor_scalar(snm[:], smx[:, 0:1], smx[:, 1:2], -SCALE, ALU.max, ALU.mult
                                  ).then_inc(S.snegmax_ready, 1)
                maxima(1)
                dve.wait_ge(S.sexps_done, j + 1)
                dve.tensor_tensor(sden[:], ssm[:, 0:1], ssm[:, 1:2], ALU.add).then_inc(S.sample_step, 1)
                dve.wait_ge(S.sample_step, j * 2 + 1)
                dve.reciprocal(sden[:], sden[:]).then_inc(S.sample_step, 1)
                dve.wait_ge(S.sample_step, j * 2 + 2)
                dve.tensor_scalar(cmb[:], cst[:, C_PAT:C_PAT + 32], sden[:, 0:1], cf[:, 0:1], ALU.mult, ALU.mult
                                  ).then_inc(S.cmb_ready, 1)
                combine(1)
                maxima(2)
                combine(2)
                maxima(3)
                combine(3)
                dve.wait_ge(S.sample_weighed, j + 1)
                dve.tensor_copy(osb[:], weighed[:, 0:2 * P]).then_inc(S.sample_kept_out, 1)
                dve.wait_ge(S.sample_back, j + 1)
                for hh in range(2):
                    v = weighed[:, (2 + hh) * P:(3 + hh) * P].rearrange("p (t x) -> p t x", t=4)
                    ins = dve.tensor_copy(c.hT[:, 4 * hh:4 * hh + 4, bass.ds(j * DS + SEQ, DS)],
                                          v[:, :, 4 * hh:4 * hh + DS])
                ins.then_inc(S.sample_out, 1)

            turns(dve, turn)

        @block.gpsimd
        def _(pool):
            pool.sem_inc(S.head_copied, FIRST)
            for n in range(2):
                pool.memset(qz[n][:], 0.0)
                ins = pool.memset(qst[n][:], 0.0)
            ins.then_inc(S.zeroed, 1)
            pool.wait_ge(S.zeroed, 1)

            def turn(j, par_):
                pool.wait_ge(S[f"scores_ready{par_}"], (j - par_) * (NB // 2) + FIRST)
                pool.wait_ge(S.head_copied, j + FIRST)
                for cc in range(2):
                    lo = 64 * cc
                    for hh in range(2):
                        pool.tensor_copy(qst[par_][lo:lo + 64, 4 * hh:4 * hh + 4, 8 * hh + 4 * cc:8 * hh + 4 * cc + DS],
                                         c.qk[lo:lo + 64, 4 * hh:4 * hh + 4, bass.ds(j * DS + SEQ, DS)])
                    ins = pool.tensor_copy(qz[par_][lo:lo + 64, cc, 0:SEQ],
                                           c.qk[lo:lo + 64, bass.ds(j, 1), 0:SEQ].rearrange("p a x -> p (a x)"))
                ins.then_inc(S.q_copied, 1)
                pool.wait_ge(S.q_copied, j + 1)
                pool.wait_ge(S.v_turned, j + FIRST)
                pool.tensor_copy(vs[:], c.vT[:, bass.ds(j, 1), 0:SEQ].rearrange("p a x -> p (a x)")
                                 ).then_inc(S.head_copied, 1)

            turns(pool, turn)


def last_phase(c, blocks):
    nc, S = c.nc, c.S
    with ExitStack() as ctx:
        c.Wh, c.Wl = split_buffers(nc, ctx, "W5", 2, D)
        c.Hh, c.Hl = split_buffers(nc, ctx, "H5", KT, T)
        c.Yh, c.Yl = split_buffers(nc, ctx, "Y5", 2 * KT, T)
        c.full = ctx.enter_context(nc.sbuf_tensor("full5", [P, 2, T], F32))
        rq = ctx.enter_context(nc.sbuf_tensor("rq5", [P, NH, T], F32))
        squares = [c.tmp[:, 0, :], c.tmp[:, 1, :], c.full[:, 0, :], c.full[:, 1, :]]
        pairs = [c.LN[0], c.LN[1], c.A, c.Bp]
        block = ctx.enter_context(nc.Block())
        b0 = c.stage["o"][1]
        first = 3 * KT

        @block.sync
        def _(sp):
            sp_stream_split(c, sp, b0 + SLOTS, blocks - b0 - SLOTS)
            for u in range(2):
                sp.wait_ge(S[f"pair_free{u}"], (c.stage["dn11"][0] + KT) // 2)
            sp.dma_start(c.y_o, c.xT).then_inc(S.stored, 16)
            sp.wait_ge(S.stored, 64)
            sp.wait_ge(S.state_stored, 16 * GROUPS)
            sp.wait_ge(S.samples_stored, 16 * GROUPS)

        @block.tensor
        def _(pe):
            for k in range(NH):
                pe.wait_ge(S.head_squared, k + 1)
                if k >= 4:
                    pe.wait_ge(S.head_logged, k - 3)
                for h in range(2):
                    mm = pe.matmul(pairs[k % 4][:, h, 0:HT], c.ones, squares[k % 4][:, h * HT:(h + 1) * HT],
                                   start=True, stop=True)
                mm.then_inc(S.head_summed, 1)
            pe_layer(c, pe, "o", (c.Hh, c.Hl), lambda k: (S.tile_split, first + k + 1))
            pe_norm(c, pe, 3)
            pe_mlp(c, pe, 1, first + KT)

        @block.scalar
        def _(act):
            act_split(c, act, 0, b0)
            for k in range(NH):
                act.wait_ge(S.head_summed, k + 1)
                act.activation(halves(rq[:, k, :]), pairs[k % 4][:, :, 0:HT], ACT.Ln, bias=c.eps, scale=1.0 / P
                               ).then_inc(S.head_logged, 1)
            for k in range(NH + 1):
                if k < NH:
                    act.wait_ge(S.head_logged, k + 1)
                    act.activation(rq[:, k, :], rq[:, k, :], ACT.Exp, scale=-0.5).then_inc(S.head_inverted, 1)
                if k:
                    act.wait_ge(S.tile_scaled, first + k)
                    act.activation(c.Hh[:, k - 1, :], c.hT[:, k - 1, :], ACT.Copy).then_inc(S.tile_high, 1)
            act_idle_layer(c, act, "o")
            act_wait_added(c, act, "o")
            act_norm(c, act, 3)
            act_scale(c, act, first + KT)
            act_mlp(c, act, 1)

        @block.vector
        def _(dve):
            dve_split(c, dve, 0, b0)
            for k in range(NH):
                if k >= 4:
                    dve.wait_ge(S.head_summed, k - 3)
                dve.tensor_tensor(squares[k % 4], c.hT[:, k, :], c.hT[:, k, :], ALU.mult).then_inc(S.head_squared, 1)
            for k in range(NH):
                dve.wait_ge(S.head_inverted, k + 1)
                dve.scalar_tensor_tensor(out=c.hT[:, k, :], in0=c.hT[:, k, :], scalar=c.gsub[:, 0:1],
                                         in1=rq[:, k, :], op0=ALU.mult, op1=ALU.mult).then_inc(S.tile_scaled, 1)
                dve.wait_ge(S.tile_high, first + k + 1)
                dve.tensor_tensor(c.Hl[:, k, :], c.hT[:, k, :], c.Hh[:, k, :].bitcast(F32), ALU.subtract
                                  ).then_inc(S.tile_split, 1)
            dve_add_layer(c, dve, "o")
            dve.wait_ge(S.inverted, 4)
            dve_scale(c, dve, first + KT, G_MB)
            dve_mlp(c, dve, 1)


OUTS = {
    "y_o": (P, KT, T), "nst_p": (GROUPS, P, R * HP), "nconv_o": (P, 32, 27), "k_o": (P, KT, T), "v_o": (P, KT, T),
    "nst_s": (GROUPS, P, DB * R * HP),
}


def build_program(nc, wblocks, wdt, xin, cst_d, par_d, hist_d, h0_d, ck_d, cv_d, pt_d,
                  y_o, nst_p, nconv_o, k_o, v_o, nst_s):
    with ExitStack() as ctx:
        c = Chip()
        c.nc, c.wblocks, c.wdt, c.xin, c.cst_d, c.par_d, c.hist_d, c.h0_d = nc, wblocks, wdt, xin, cst_d, par_d, hist_d, h0_d
        c.ck_d, c.cv_d, c.y_o, c.nst_p, c.nconv_o, c.k_o, c.v_o, c.nst_s = ck_d, cv_d, y_o, nst_p, nconv_o, k_o, v_o, nst_s
        c.n_pool = ck_d.shape[0]
        c.scr = nc.dram_tensor("decay_scratch", (32, T), F32, kind="Internal").ap()
        c.S = Sems(nc, ctx)
        c.stage, blocks = plan()

        def sb(name, shape, dt=F32):
            return ctx.enter_context(nc.sbuf_tensor(name, shape, dt))

        c.ring = sb("ring", [P, SLOTS, D])
        c.cst = sb("cst", [P, C_W])
        c.par = sb("par", [P, G_W])
        c.tmp = sb("tmp", [P, 2, T])
        c.rn = sb("rn", [P, T])
        c.gsub = sb("gsub", [P, 1])
        c.pt = sb("pt", [1, DB * PAGES], I32)
        c.LN = [ctx.enter_context(nc.psum_tensor(f"LN{n}", [P, 2, 512], F32)) for n in range(2)]
        c.A = ctx.enter_context(nc.psum_tensor("A", [P, 2, 512], F32))
        c.Bp = ctx.enter_context(nc.psum_tensor("Bp", [P, 2, 512], F32))
        c.AB = [c.A, c.Bp]
        c.ident, c.ones = c.cst[:, C_ID:C_ID + P], c.cst[:, C_ONE:C_ONE + P]
        c.blk64, c.eps = c.cst[:, C_B64:C_B64 + P], c.cst[:, C_EPS:C_EPS + 1]
        c.pt_d = pt_d
        c.yT = sb("yT", [P, 2 * KT, T])
        c.xT = c.yT[:, KT:2 * KT, :]
        mixer_phase(c)
        c.xT = c.yT[:, 0:KT, :]
        c.hT = c.yT[:, KT:2 * KT, :]
        out_phase(c)
        mlp_phase(c)
        with ExitStack() as heads:
            c.qk = heads.enter_context(nc.sbuf_tensor("qk", [P, 2 * KT, T], F32))
            c.vT = heads.enter_context(nc.sbuf_tensor("vT", [P, KT, T], F32))
            qkv_phase(c)
            attention_phase(c)
        last_phase(c, blocks)


def feature_tiles(a):
    return a.reshape(-1, P).T


def weight_blocks(w):
    k, n = w.shape
    w = w.reshape(k // D, KT, P, n // P, P).transpose(3, 0, 2, 1, 4)
    return w.reshape(-1, P, KT * P)


def kernel(**inputs):
    import concourse.bacc as bacc
    from concourse.bass_utils import run_bass_kernel_spmd

    a = {k: np.asarray(v) for k, v in inputs.items()}
    DI = 2 * D
    w_in = a["w_in_a"][0]
    zc, xcols, bcols, ccols = 0, DI, 2 * DI, 2 * DI + D
    order, conv_order = [], []
    for g in range(GROUPS):
        conv = [xcols + 256 * g, xcols + 256 * g + P, bcols + P * g, ccols + P * g]
        order += conv + [zc + 256 * g, zc + 256 * g + P]
        conv_order += [o - DI for o in conv]
    cols = np.concatenate([np.arange(o, o + P) for o in order])
    ccol = np.concatenate([np.arange(o, o + P) for o in conv_order])
    up, dn = a["w_up"], a["w_down"]
    half = DF // 2
    parts = [weight_blocks(w_in[:, cols]), weight_blocks(a["w_out_a"][0])]
    mlps = []
    for layer in range(2):
        mlps.append([b for h in range(2) for b in (weight_blocks(up[layer][:, h * half:(h + 1) * half]),
                                                   weight_blocks(dn[layer][h * half:(h + 1) * half]))])
    w_k, w_v = np.split(a["w_kv"], 2, axis=-1)
    parts += mlps[0] + [weight_blocks(w_k), weight_blocks(a["w_q"][0]), weight_blocks(w_v), weight_blocks(a["w_o"][0])] + mlps[1]
    wblocks = np.concatenate(parts)
    wdt = w_in[:, DI + 2 * DI:].reshape(KT, P, 32).transpose(1, 0, 2).reshape(P, KT * 32)

    x = np.concatenate([a["x_prompt"][0], a["x_sample"].reshape(NS, D)])
    xin = x.T.reshape(KT, P, T).transpose(1, 0, 2)

    par = np.zeros((P, G_W), np.float32)
    for at, v in ((G_A, a["norm_a"][0]), (G_MA, a["norm_m"][0]), (G_KV, a["kv_norm"]), (G_B, a["norm_b"][0]),
                  (G_MB, a["norm_m"][1])):
        par[:, at:at + KT] = feature_tiles(v)
    par[:, G_GN:G_GN + 16] = feature_tiles(a["gnorm_w"][0])
    par[:, G_DSK:G_DSK + 16] = feature_tiles(np.repeat(a["d_skip"][0], HP))
    par[:, G_CW:G_CW + P] = a["conv_w"][0][:, ccol].reshape(4, 32, P).transpose(2, 1, 0).reshape(P, P)
    par[:, G_CBI:G_CBI + 32] = a["conv_b"][0][ccol].reshape(32, P).T
    par[:, G_KN] = np.tile(a["k_norm"], 2)
    par[:, G_QN] = np.tile(a["q_norm"][0], 2)
    par[:, G_SUB] = a["subln"][0]
    par[:32, G_DTB] = a["dt_bias"][0]
    par[:32, G_ALOG] = a["a_log"][0]
    for n, k in enumerate(("lam_q1", "lam_k1", "lam_q2", "lam_k2")):
        par[:64, G_LAM + n] = a[k][0]

    hist = a["state_conv"][0][:, :, ccol].reshape(DB, 3, 32, P).transpose(3, 2, 0, 1).reshape(P, 32, 24)
    h0 = a["state_ssm"][0].reshape(DB, GROUPS, R * HP, P).transpose(1, 3, 0, 2).reshape(GROUPS, P, DB * R * HP)
    n_pool = a["cache_k"].shape[0]
    ck = a["cache_k"].reshape(n_pool, P, NH, P).transpose(0, 3, 2, 1).reshape(n_pool, P, NH * P)
    cv = a["cache_v"].reshape(n_pool, P, NH * P)

    arrays = {
        "wblocks": wblocks, "wdt": wdt, "xin": xin, "cst_d": constants(), "par_d": par, "hist_d": hist, "h0_d": h0,
        "ck_d": ck, "cv_d": cv, "pt_d": a["page_table"].reshape(1, DB * PAGES),
    }
    arrays = {k: np.ascontiguousarray(v) for k, v in arrays.items()}
    nc = bacc.Bacc("TRN2", target_bir_lowering=False, num_devices=1)
    aps = {k: nc.dram_tensor(k, v.shape, mybir.dt.from_np(v.dtype), kind="ExternalInput").ap()
           for k, v in arrays.items()}
    aps |= {k: nc.dram_tensor(k, s, F32, kind="ExternalOutput").ap() for k, s in OUTS.items()}
    build_program(nc, **aps)
    r = run_bass_kernel_spmd(nc, [arrays], core_ids=[0]).results[0]

    def tokens(o):
        t = o.transpose(2, 1, 0).reshape(T, D)
        return t[:SEQ], t[SEQ:].reshape(DB, DS, D)

    y_p, y_s = tokens(r["y_o"])
    k_p, k_s = tokens(r["k_o"])
    v_p, v_s = tokens(r["v_o"])
    ssm_p = r["nst_p"].transpose(0, 2, 1).reshape(1, 1, 32, HP, P)
    ssm_s = r["nst_s"].reshape(GROUPS, P, DB, R * HP).transpose(2, 0, 3, 1).reshape(1, DB, 32, HP, P)
    back = np.argsort(ccol)
    conv = r["nconv_o"].transpose(2, 1, 0).reshape(27, 32 * P)[:, back]
    return (
        y_p.reshape(1, SEQ, D), y_s, ssm_p, conv[:3].reshape(1, 1, 3, -1), k_p.reshape(1, SEQ, NH, 2, 64),
        v_p.reshape(1, SEQ, NH, P), ssm_s, conv[3:].reshape(DB, 3, -1)[None], k_s.reshape(DB, DS, NH, 2, 64),
        v_s.reshape(DB, DS, NH, P),
    )
```
